# Optimizing a Trainium2 kernel written in Bass

```python
import math
import jax
import jax.numpy as jnp
from jax import lax
import numpy as np

D_MODEL = 1024
BATCH = 1
SEQ = 256
DEPTH = 2

F32 = jnp.float32
MIX_WIDTH = D_MODEL
HALF_MIX = MIX_WIDTH // 2
DA_HEADS = 4
DA_HEAD = HALF_MIX // (2 * DA_HEADS)
DA_ROPE = DA_HEAD // 4
ROPE_THETA = 500000.0
Q_BLOCK = 128
LRU_WIDTH = HALF_MIX
LRU_BLOCKS = 8
LRU_BLOCK = LRU_WIDTH // LRU_BLOCKS
CONV_W = 4
LRU_C = 8.0
S5_WIDTH = HALF_MIX
S5_GROUP = 16
S5_GROUPS = S5_WIDTH // S5_GROUP
S5_STATE = 64
RET_HEADS = 4
RET_QK = HALF_MIX // (2 * RET_HEADS)
RET_V = HALF_MIX // RET_HEADS
RET_THETA = 10000.0
RET_CHUNK = 128
MEM_LEN = 256
XA_HEADS = 4
XA_HEAD = D_MODEL // XA_HEADS
D_FF = ((8 * D_MODEL // 3 + 127) // 128) * 128
DN_ALPHA = (2 * DEPTH) ** 0.25
DN_BETA = (8 * DEPTH) ** -0.25
LN_EPS = 1e-5
N_EVEN = (DEPTH + 1) // 2
N_ODD = DEPTH // 2
EVEN_IN = 3 * HALF_MIX + 2 * LRU_WIDTH
ODD_IN = S5_WIDTH + 2 * RET_HEADS * RET_QK + 2 * RET_HEADS * RET_V

kernel_name = 'hybrid_diffattn_rglru_s5_retention_trunk'

def layer_norm(x, g, b):
    xf = x.astype(F32)
    mu = jnp.mean(xf, -1, keepdims=True)
    var = jnp.mean(jnp.square(xf - mu), -1, keepdims=True)
    return ((xf - mu) * lax.rsqrt(var + LN_EPS) * g.astype(F32) + b.astype(F32)).astype(x.dtype)

def rms_norm(x, g):
    xf = x.astype(F32)
    return xf * lax.rsqrt(jnp.mean(jnp.square(xf), -1, keepdims=True) + LN_EPS) * g.astype(F32)

def head_group_norm(x, g):
    xf = x.astype(F32)
    mu = jnp.mean(xf, -1, keepdims=True)
    var = jnp.mean(jnp.square(xf - mu), -1, keepdims=True)
    return (xf - mu) * lax.rsqrt(var + LN_EPS) * g.astype(F32)

def rotary(x, pos, rot_dim, theta):
    half = rot_dim // 2
    inv = theta ** (-jnp.arange(half, dtype=F32) * 2.0 / rot_dim)
    ang = pos.astype(F32)[:, None] * inv[None, :]
    shape = (1, x.shape[1]) + (1,) * (x.ndim - 3) + (half,)
    cos = jnp.cos(ang).reshape(shape)
    sin = jnp.sin(ang).reshape(shape)
    xf = x.astype(F32)
    x1, x2, xp = xf[..., :half], xf[..., half:rot_dim], xf[..., rot_dim:]
    return jnp.concatenate([x1 * cos - x2 * sin, x1 * sin + x2 * cos, xp], -1).astype(x.dtype)

def swiglu(x, w_gate, w_up, w_down):
    return (jax.nn.silu(x @ w_gate) * (x @ w_up)) @ w_down

def diff_lambda_init(layer):
    return 0.8 - 0.6 * math.exp(-0.3 * layer)

def diff_attention(q, k, v, lam, norm_g, lambda_init):
    B, S, H, _, d = q.shape
    scale = d ** -0.5
    lf = lam.astype(F32)
    lmbda = jnp.exp(jnp.sum(lf[0] * lf[1])) - jnp.exp(jnp.sum(lf[2] * lf[3])) + lambda_init
    nb = S // Q_BLOCK
    qb = q.reshape(B, nb, Q_BLOCK, H, 2, d).transpose(1, 0, 2, 3, 4, 5)
    kpos = jnp.arange(S)

    def block(args):
        qi, i = args
        s = jnp.einsum('bqhmd,bkhmd->bhmqk', qi, k).astype(F32) * scale
        qpos = i * Q_BLOCK + jnp.arange(Q_BLOCK)
        causal = kpos[None, :] <= qpos[:, None]
        p = jax.nn.softmax(jnp.where(causal, s, -jnp.inf), axis=-1)
        w = p[:, :, 0] - lmbda * p[:, :, 1]
        return jnp.einsum('bhqk,bkhe->bqhe', w.astype(v.dtype), v)

    o = lax.map(block, (qb, jnp.arange(nb)))
    o = o.transpose(1, 0, 2, 3, 4).reshape(B, S, H, 2 * d)
    o = rms_norm(o, norm_g) * (1.0 - lambda_init)
    return o.reshape(B, S, H * 2 * d).astype(q.dtype)

def causal_depthwise_conv(x, w, b):
    K, C = w.shape
    y = lax.conv_general_dilated(x, w[:, None, :].astype(x.dtype), window_strides=(1,),
                                 padding=[(K - 1, 0)], dimension_numbers=('NWC', 'WIO', 'NWC'),
                                 feature_group_count=C)
    return y + b.astype(x.dtype)

def linear_combine(left, right):
    a_l, b_l = left
    a_r, b_r = right
    return a_l * a_r, a_r * b_l + b_r

def rg_lru(x, gate_w, gate_b, lam):
    B, S, W = x.shape
    xb = x.reshape(B, S, LRU_BLOCKS, LRU_BLOCK)
    gates = jnp.einsum('bsnc,gncd->gbsnd', xb, gate_w).reshape(2, B, S, W).astype(F32)
    gates = gates + gate_b.astype(F32)[:, None, None, :]
    r = jax.nn.sigmoid(gates[0])
    i = jax.nn.sigmoid(gates[1])
    log_a = -LRU_C * r * jax.nn.softplus(-lam.astype(F32))
    a = jnp.exp(log_a)
    b = jnp.sqrt(-jnp.expm1(2.0 * log_a)) * (i * x.astype(F32))
    _, h = lax.associative_scan(linear_combine, (a, b), axis=1)
    return h.astype(x.dtype)

def complex_combine(left, right):
    ar_l, ai_l, br_l, bi_l = left
    ar_r, ai_r, br_r, bi_r = right
    return (ar_r * ar_l - ai_r * ai_l, ar_r * ai_l + ai_r * ar_l,
            ar_r * br_l - ai_r * bi_l + br_r, ar_r * bi_l + ai_r * br_l + bi_r)

def s5_ssm(u, lam_re, lam_im, log_step, b_re, b_im, c_re, c_im, d_skip, glu_w, glu_b):
    B, S, W = u.shape
    uf = u.astype(F32)
    ug = uf.reshape(B, S, S5_GROUPS, S5_GROUP)
    step = jnp.exp(log_step.astype(F32))[:, None]
    lr = jnp.minimum(lam_re.astype(F32), -1e-4)
    li = lam_im.astype(F32)
    mag = jnp.exp(lr * step)
    ang = li * step
    ab_re, ab_im = mag * jnp.cos(ang), mag * jnp.sin(ang)
    den = lr * lr + li * li
    nr, ni = ab_re - 1.0, ab_im
    f_re = (nr * lr + ni * li) / den
    f_im = (ni * lr - nr * li) / den
    bu_re = jnp.einsum('bsgc,gnc->bsgn', ug, b_re.astype(F32))
    bu_im = jnp.einsum('bsgc,gnc->bsgn', ug, b_im.astype(F32))
    x_re = f_re * bu_re - f_im * bu_im
    x_im = f_re * bu_im + f_im * bu_re
    a_re = jnp.broadcast_to(ab_re[None, None], (1, S, S5_GROUPS, S5_STATE))
    a_im = jnp.broadcast_to(ab_im[None, None], (1, S, S5_GROUPS, S5_STATE))
    _, _, h_re, h_im = lax.associative_scan(complex_combine, (a_re, a_im, x_re, x_im), axis=1)
    y = (jnp.einsum('bsgn,gcn->bsgc', h_re, c_re.astype(F32))
         - jnp.einsum('bsgn,gcn->bsgc', h_im, c_im.astype(F32)))
    y = y.reshape(B, S, W) + d_skip.astype(F32) * uf
    z = jax.nn.gelu(y)
    out = z * jax.nn.sigmoid(z @ glu_w.astype(F32) + glu_b.astype(F32))
    return out.astype(u.dtype)

def retention(q, k, v, g, norm_g, pos):
    B, S, H, dk = q.shape
    dv = v.shape[-1]
    q = rotary(q, pos, dk, RET_THETA).astype(F32)
    k = rotary(k, pos, dk, RET_THETA).astype(F32) * dk ** -0.5
    v = v.astype(F32)
    log_g = jnp.log(1.0 - jnp.exp2(-5.0 - jnp.arange(H, dtype=F32)))
    C = RET_CHUNK
    nc = S // C
    idx = jnp.arange(C, dtype=F32)
    diff = idx[:, None] - idx[None, :]
    causal = diff >= 0
    decay_in = jnp.where(causal[None], jnp.exp(log_g[:, None, None] * jnp.where(causal, diff, 0.0)[None]), 0.0)
    xi = jnp.exp(log_g[:, None] * (idx + 1.0))[None, :, :, None]
    zeta = jnp.exp(log_g[:, None] * (C - 1.0 - idx))[None, :, :, None]
    chunk_decay = jnp.exp(log_g * C)[None, :, None, None]
    qc = q.reshape(B, nc, C, H, dk).transpose(1, 0, 3, 2, 4)
    kc = k.reshape(B, nc, C, H, dk).transpose(1, 0, 3, 2, 4)
    vc = v.reshape(B, nc, C, H, dv).transpose(1, 0, 3, 2, 4)

    def step(R, inp):
        qi, ki, vi = inp
        inner = jnp.einsum('bhqd,bhkd->bhqk', qi, ki) * decay_in[None]
        o = (jnp.einsum('bhqk,bhke->bhqe', inner, vi)
             + jnp.einsum('bhqd,bhde->bhqe', qi, R) * xi)
        R = chunk_decay * R + jnp.einsum('bhkd,bhke->bhde', ki * zeta, vi)
        return R, o

    R0 = jnp.zeros((B, H, dk, dv), F32)
    _, o = lax.scan(step, R0, (qc, kc, vc))
    o = o.transpose(1, 0, 3, 2, 4).reshape(B, S, H, dv)
    o = head_group_norm(o, norm_g).reshape(B, S, H * dv)
    return (jax.nn.silu(g.astype(F32)) * o).astype(g.dtype)

def even_mixer(x, pos, w_in, w_out, lam, norm_g, conv_w, conv_b, gate_w, gate_b, lru_lam, lambda_init):
    B, S, _ = x.shape
    z = x @ w_in
    q, k, v, gate, xr = jnp.split(z, [HALF_MIX, 2 * HALF_MIX, 3 * HALF_MIX, 3 * HALF_MIX + LRU_WIDTH], axis=-1)
    q = rotary(q.reshape(B, S, DA_HEADS, 2, DA_HEAD), pos, DA_ROPE, ROPE_THETA)
    k = rotary(k.reshape(B, S, DA_HEADS, 2, DA_HEAD), pos, DA_ROPE, ROPE_THETA)
    v = v.reshape(B, S, DA_HEADS, 2 * DA_HEAD)
    a_out = diff_attention(q, k, v, lam, norm_g, lambda_init)
    h = rg_lru(causal_depthwise_conv(xr, conv_w, conv_b), gate_w, gate_b, lru_lam)
    b_out = jax.nn.gelu(gate) * h
    return jnp.concatenate([a_out, b_out], axis=-1) @ w_out

def odd_mixer(x, pos, w_in, w_out, lam_re, lam_im, log_step, b_re, b_im, c_re, c_im, d_skip, glu_w, glu_b, ret_g):
    B, S, _ = x.shape
    z = x @ w_in
    o1 = S5_WIDTH
    o2 = o1 + RET_HEADS * RET_QK
    o3 = o2 + RET_HEADS * RET_QK
    o4 = o3 + RET_HEADS * RET_V
    u, q, k, v, g = jnp.split(z, [o1, o2, o3, o4], axis=-1)
    c_out = s5_ssm(u, lam_re, lam_im, log_step, b_re, b_im, c_re, c_im, d_skip, glu_w, glu_b)
    d_out = retention(q.reshape(B, S, RET_HEADS, RET_QK), k.reshape(B, S, RET_HEADS, RET_QK),
                      v.reshape(B, S, RET_HEADS, RET_V), g, ret_g, pos)
    return jnp.concatenate([c_out, d_out], axis=-1) @ w_out

def memory_cross_attention(x, mem, w_q, w_kv, w_o):
    B, S, _ = x.shape
    M = mem.shape[1]
    q = (x @ w_q).reshape(B, S, XA_HEADS, XA_HEAD)
    kv = (mem @ w_kv).reshape(B, M, 2, XA_HEADS, XA_HEAD)
    s = jnp.einsum('bshd,bmhd->bhsm', q, kv[:, :, 0]).astype(F32) * XA_HEAD ** -0.5
    p = jax.nn.softmax(s, axis=-1)
    o = jnp.einsum('bhsm,bmhd->bshd', p.astype(x.dtype), kv[:, :, 1]).reshape(B, S, D_MODEL)
    return o @ w_o

def setup_inputs(seed: int = 0) -> dict:
    key = jax.random.key(seed)
    ks = iter(jax.random.split(key, 40))

    def nrm(shape, scale):
        return jax.random.normal(next(ks), shape, F32) * scale

    x = nrm((BATCH, SEQ, D_MODEL), 1.0)
    mem = nrm((BATCH, MEM_LEN, D_MODEL), 1.0)
    ln_g = 1.0 + nrm((DEPTH, 4, D_MODEL), 0.02)
    ln_b = nrm((DEPTH, 4, D_MODEL), 0.02)
    ffn_w_gate = nrm((DEPTH, 2, D_MODEL, D_FF), D_MODEL ** -0.5)
    ffn_w_up = nrm((DEPTH, 2, D_MODEL, D_FF), D_MODEL ** -0.5)
    ffn_w_down = nrm((DEPTH, 2, D_FF, D_MODEL), D_FF ** -0.5 * DN_BETA)
    xa_w_q = nrm((DEPTH, D_MODEL, D_MODEL), D_MODEL ** -0.5)
    xa_w_kv = nrm((DEPTH, D_MODEL, 2 * D_MODEL), D_MODEL ** -0.5)
    xa_w_o = nrm((DEPTH, D_MODEL, D_MODEL), D_MODEL ** -0.5 * DN_BETA)
    ev_w_in = nrm((N_EVEN, D_MODEL, EVEN_IN), D_MODEL ** -0.5)
    ev_w_out = nrm((N_EVEN, MIX_WIDTH, D_MODEL), MIX_WIDTH ** -0.5 * DN_BETA)
    da_lambda = nrm((N_EVEN, 4, DA_HEAD), 0.1)
    da_norm_g = 1.0 + nrm((N_EVEN, 2 * DA_HEAD), 0.02)
    lru_conv_w = nrm((N_EVEN, CONV_W, LRU_WIDTH), CONV_W ** -0.5)
    lru_conv_b = nrm((N_EVEN, LRU_WIDTH), 0.02)
    lru_gate_w = nrm((N_EVEN, 2, LRU_BLOCKS, LRU_BLOCK, LRU_BLOCK), LRU_BLOCK ** -0.5)
    lru_gate_b = nrm((N_EVEN, 2, LRU_WIDTH), 0.02)
    a_c = jax.random.uniform(next(ks), (N_EVEN, LRU_WIDTH), F32, 0.9, 0.999)
    a0 = a_c ** (1.0 / LRU_C)
    lru_lambda = jnp.log(a0) - jnp.log1p(-a0)
    od_w_in = nrm((N_ODD, D_MODEL, ODD_IN), D_MODEL ** -0.5)
    od_w_out = nrm((N_ODD, MIX_WIDTH, D_MODEL), MIX_WIDTH ** -0.5 * DN_BETA)
    s5_lam_re = -0.5 + nrm((N_ODD, S5_GROUPS, S5_STATE), 0.01)
    s5_lam_im = jnp.pi * jnp.arange(S5_STATE, dtype=F32) + nrm((N_ODD, S5_GROUPS, S5_STATE), 0.01)
    s5_log_step = jax.random.uniform(next(ks), (N_ODD, S5_GROUPS), F32, math.log(1e-3), math.log(1e-1))
    s5_b_re = nrm((N_ODD, S5_GROUPS, S5_STATE, S5_GROUP), (2 * S5_GROUP) ** -0.5)
    s5_b_im = nrm((N_ODD, S5_GROUPS, S5_STATE, S5_GROUP), (2 * S5_GROUP) ** -0.5)
    s5_c_re = nrm((N_ODD, S5_GROUPS, S5_GROUP, S5_STATE), S5_STATE ** -0.5)
    s5_c_im = nrm((N_ODD, S5_GROUPS, S5_GROUP, S5_STATE), S5_STATE ** -0.5)
    s5_d = nrm((N_ODD, S5_WIDTH), 1.0)
    s5_glu_w = nrm((N_ODD, S5_WIDTH, S5_WIDTH), S5_WIDTH ** -0.5)
    s5_glu_b = nrm((N_ODD, S5_WIDTH), 0.02)
    ret_norm_g = 1.0 + nrm((N_ODD, RET_V), 0.02)
    return {'x': x, 'mem': mem, 'ln_g': ln_g, 'ln_b': ln_b,
            'ffn_w_gate': ffn_w_gate, 'ffn_w_up': ffn_w_up, 'ffn_w_down': ffn_w_down,
            'xa_w_q': xa_w_q, 'xa_w_kv': xa_w_kv, 'xa_w_o': xa_w_o,
            'ev_w_in': ev_w_in, 'ev_w_out': ev_w_out, 'da_lambda': da_lambda, 'da_norm_g': da_norm_g,
            'lru_conv_w': lru_conv_w, 'lru_conv_b': lru_conv_b, 'lru_gate_w': lru_gate_w,
            'lru_gate_b': lru_gate_b, 'lru_lambda': lru_lambda,
            'od_w_in': od_w_in, 'od_w_out': od_w_out, 's5_lam_re': s5_lam_re, 's5_lam_im': s5_lam_im,
            's5_log_step': s5_log_step, 's5_b_re': s5_b_re, 's5_b_im': s5_b_im,
            's5_c_re': s5_c_re, 's5_c_im': s5_c_im, 's5_d': s5_d, 's5_glu_w': s5_glu_w,
            's5_glu_b': s5_glu_b, 'ret_norm_g': ret_norm_g}

def reference(x, mem, ln_g, ln_b, ffn_w_gate, ffn_w_up, ffn_w_down, xa_w_q, xa_w_kv, xa_w_o,
              ev_w_in, ev_w_out, da_lambda, da_norm_g, lru_conv_w, lru_conv_b, lru_gate_w,
              lru_gate_b, lru_lambda, od_w_in, od_w_out, s5_lam_re, s5_lam_im, s5_log_step,
              s5_b_re, s5_b_im, s5_c_re, s5_c_im, s5_d, s5_glu_w, s5_glu_b, ret_norm_g):
    S = x.shape[1]
    pos = jnp.arange(S, dtype=jnp.int32)
    for l in range(DEPTH):
        h = swiglu(x, ffn_w_gate[l, 0], ffn_w_up[l, 0], ffn_w_down[l, 0])
        x = layer_norm(DN_ALPHA * x + 0.5 * h, ln_g[l, 0], ln_b[l, 0])
        if l % 2 == 0:
            e = l // 2
            m = even_mixer(x, pos, ev_w_in[e], ev_w_out[e], da_lambda[e], da_norm_g[e],
                           lru_conv_w[e], lru_conv_b[e], lru_gate_w[e], lru_gate_b[e],
                           lru_lambda[e], diff_lambda_init(l))
        else:
            o = l // 2
            m = odd_mixer(x, pos, od_w_in[o], od_w_out[o], s5_lam_re[o], s5_lam_im[o],
                          s5_log_step[o], s5_b_re[o], s5_b_im[o], s5_c_re[o], s5_c_im[o],
                          s5_d[o], s5_glu_w[o], s5_glu_b[o], ret_norm_g[o])
        x = layer_norm(DN_ALPHA * x + m, ln_g[l, 1], ln_b[l, 1])
        c = memory_cross_attention(x, mem, xa_w_q[l], xa_w_kv[l], xa_w_o[l])
        x = layer_norm(DN_ALPHA * x + c, ln_g[l, 2], ln_b[l, 2])
        h = swiglu(x, ffn_w_gate[l, 1], ffn_w_up[l, 1], ffn_w_down[l, 1])
        x = layer_norm(DN_ALPHA * x + 0.5 * h, ln_g[l, 3], ln_b[l, 3])
    return x


_drawn_inputs = setup_inputs


def setup_inputs(seed=0):
    import zlib

    import numpy as np

    out = dict(_drawn_inputs(seed))
    spreads = {}
    factors = {'da_lambda': 2.805,
     'da_norm_g': 8.0,
     'lru_conv_b': 4.388,
     'lru_gate_b': 64.0,
     's5_lam_re': 64.0,
     's5_lam_im': 56.76,
     's5_log_step': 61.376,
     's5_b_re': 64.0,
     's5_b_im': 64.0,
     's5_c_re': 64.0,
     's5_c_im': 64.0,
     's5_glu_b': 64.0,
     'ret_norm_g': 30.815,
     's5_glu_w': 3.053}
    for name, (base, spread) in spreads.items():
        noise = np.random.default_rng([zlib.crc32(name.encode()), seed]).standard_normal(out[name].shape)
        drawn = base * np.exp(spread * noise) if base else spread * noise
        out[name] = jnp.asarray(drawn.astype(out[name].dtype))
    for name, factor in factors.items():
        out[name] = (out[name] * factor).astype(out[name].dtype)
    return out
```

```python
import math
from contextlib import ExitStack

import numpy as np
import concourse.bass as bass
from concourse import mybir

F32 = mybir.dt.float32
F32R = mybir.dt.float32r
ALU = mybir.AluOpType
ACT = mybir.ActivationFunctionType
AX_X = mybir.AxisListType.X

P = 128
SEQ = 256
TT = SEQ // P
D = 1024
KT = D // P
DEPTH = 2
D_FF = 2816
FB = 256
NB = D_FF // FB
HALF = D // 2
UW = 2048
NSLOT = 3
FFN_UNITS = 3 * NB
ALPHA = (2 * DEPTH) ** 0.25
LN_EPS = 1e-5
LRU_C = 8.0
DA_H, DA_D, DA_ROPE, DA_THETA = 4, 64, 16, 500000.0
RET_H, RET_D, RET_THETA = 4, 64, 10000.0
XA_H, XA_D = 4, 256
S5_TILES = 16
S5_CH = 128
LAMBDA_INIT = 0.8 - 0.6 * math.exp(-0.3 * 0)
NORMS = 4 * DEPTH


class Steps:

    def __init__(self, name, sem, marks, final):
        self.name, self.sem, self.marks, self.final, self.n = name, sem, marks, final, 0

    def up(self, *step):
        self.n += 1
        if step:
            self.marks[(self.name, *step)] = self.n
        return self.sem, 1

    def now(self):
        return self.sem, self.n

    def at(self, *step):
        if self.final:
            return self.sem, self.marks[(self.name, *step)]
        return self.sem, 1


def constant_table():
    p = np.arange(P)
    parts = {"ident": np.eye(P)}
    tri = np.where(p[None, :] <= p[:, None], 0.0, -1e30)
    parts["mask"] = np.concatenate([tri, np.zeros((P, P)), tri], 1)

    def rope(rot, theta, heads):
        half = rot // 2
        inv = np.float32(theta) ** (-np.arange(half, dtype=np.float32) * np.float32(2.0 / rot))
        ang = np.arange(SEQ, dtype=np.float32)[:, None] * inv[None, :].astype(np.float32)
        c, s = np.cos(ang), np.sin(ang)
        c = np.tile(np.concatenate([c, c], 1), (1, heads)).reshape(TT, P, -1).transpose(1, 0, 2)
        s = np.tile(np.concatenate([-s, s], 1), (1, heads)).reshape(TT, P, -1).transpose(1, 0, 2)
        return c.reshape(P, -1), s.reshape(P, -1)

    parts["da_cos"], parts["da_sin"] = rope(DA_ROPE, DA_THETA, 2 * DA_H)
    parts["ret_cos"], parts["ret_sin"] = rope(RET_D, RET_THETA, RET_H)
    gamma = 1.0 - np.exp2(-5.0 - np.arange(RET_H))
    lag = np.arange(SEQ)[None, :] - p[:, None]
    decay = np.where(lag >= 0, np.exp(np.log(gamma)[:, None, None] * np.maximum(lag, 0)), 0.0)
    parts["decay"] = (decay * RET_D ** -0.5).transpose(1, 0, 2).reshape(P, -1)
    parity = (p // 16) % 2
    parts["parity"] = np.stack([parity == 0, parity == 1], 1)
    at, where, cols = 0, {}, []
    for name, a in parts.items():
        where[name] = (at, a.shape[1])
        at += a.shape[1]
        cols.append(np.asarray(a, np.float32))
    return where, np.ascontiguousarray(np.concatenate(cols, 1))


def unit_table():
    first, u = {}, 0

    def phase(key, n):
        nonlocal u
        first[key] = u
        u += n

    def blocks(kind, cols):
        for c in cols:
            phase((kind, c), 2)

    phase(("ffn", 0), FFN_UNITS)
    blocks(("kv", 0), [0])
    blocks("ev_in", [4, 3, 0, 1, 2])
    blocks(("kv", 0), [1, 2])
    blocks("ev_out", [0, 1])
    blocks(("kv", 0), [3])
    blocks(("xq", 0), [0, 1])
    blocks(("xo", 0), [0, 1])
    blocks(("kv", 1), [0])
    phase(("ffn", 1), FFN_UNITS)
    blocks(("kv", 1), [1])
    phase(("ffn", 2), FFN_UNITS)
    blocks(("kv", 1), [2])
    blocks("od_in", [0, 1, 2, 3])
    blocks(("kv", 1), [3])
    phase("glu", 1)
    blocks("od_out", [0, 1])
    blocks(("xq", 1), [0, 1])
    blocks(("xo", 1), [0, 1])
    phase(("ffn", 3), FFN_UNITS)
    return first, u


def build(nc, A, marks, final):
    ctx = ExitStack()
    with ctx:
        write_program(nc, ctx, A, marks, final)


def write_program(nc, ctx, A, marks, final):
    def sb(name, shape, dt=F32, to=ctx):
        return to.enter_context(nc.sbuf_tensor(name, shape, dt))

    def sem(name):
        return ctx.enter_context(nc.semaphore(name))

    def steps(name):
        return Steps(name, sem(name), marks, final)

    first, n_units = unit_table()
    where, _ = constant_table()
    n_const = sum(n for _, n in where.values())

    raw = sb("raw", [P, NSLOT, UW])
    w_hi = sb("w_hi", [P, NSLOT, UW], F32R)
    w_lo = sb("w_lo", [P, NSLOT, UW], F32R)
    x = sb("x", [P, TT, D])
    ax = sb("ax", [P, TT, D])
    xT_hi = sb("xT_hi", [P, KT, SEQ], F32R)
    xT_lo = sb("xT_lo", [P, KT, SEQ], F32R)
    zero_r = sb("zero_r", [P, P], F32R)
    k_mem = sb("k_mem", [P, KT, SEQ])
    v_mem = sb("v_mem", [P, TT, D])
    gb = sb("gb", [P, 2, D])
    const = sb("const", [P, n_const])
    act_h = sb("act_h", [P, TT, FB])
    hid = sb("hid", [P, TT, FB])
    hT_hi = sb("hT_hi", [P, 2, SEQ], F32R)
    hT_lo = sb("hT_lo", [P, 2, SEQ], F32R)
    tk = sb("tk", [P, 2, TT, HALF])
    pv = sb("pv", [P, 4, 10])
    da_g = sb("da_g", [P, 2 * DA_D])
    ret_g = sb("ret_g", [P, P])
    sm = sb("sm", [P, 96])
    bn = sb("bn", [P, TT, 12])
    mv = sb("mv", [P, TT, 4])
    nat = tk[0:16, 1, :, :].rearrange("p a b -> p (a b)")[:, 0:896]

    s5_small = sb("s5_small", [P, 12, S5_TILES])
    rot_tmp = v_mem[:, 0, 0:2 * P].rearrange("p (a b) -> p a b", a=2)

    zero = rot_tmp[:, 0, :]

    def s5_par(n):
        return s5_small[:, n, :]

    memory = ExitStack()
    memT_hi = sb("memT_hi", [P, KT, SEQ], F32R, memory)
    memT_lo = sb("memT_lo", [P, KT, SEQ], F32R, memory)
    with ExitStack() as own:
        xrT = sb("xrT", [P, 4, SEQ + 3], F32, own)
        conv = sb("conv", [P, 4, SEQ], F32, own)
        lru_a = sb("lru_a", [P, 4, SEQ], F32, own)
        lru_b = sb("lru_b", [P, 4, SEQ], F32, own)
        gateT = sb("gateT", [P, 4, SEQ], F32, own)
        kT_da = sb("kT_da", [P, DA_H, SEQ], F32, own)
    qT_da = k_mem[:, 4:8, :]
    v_da = v_mem[:, :, HALF:D]
    with ExitStack() as own:
        q_x = sb("q_x", [P, KT, SEQ], F32, own)
        p_x = sb("p_x", [P, 2, TT, SEQ], F32, own)
        pT_x = sb("pT_x", [P, 2, TT, SEQ], F32, own)
    with ExitStack() as own:
        e_cos = sb("e_cos", [P, S5_TILES, S5_CH], F32, own)
        e_sin = sb("e_sin", [P, S5_TILES, S5_CH], F32, own)
        s5_bT = sb("s5_bT", [P, 2, 4, P], F32, own)
        s5_cT = sb("s5_cT", [P, 2, 4, P], F32, own)
        uT = sb("uT", [P, 4, SEQ], F32, own)
        qkT = sb("qkT", [P, 2, 2, SEQ], F32, own)
    memory.close()
    with ExitStack() as own:
        s5_g = sb("s5_g", [P, 2, 2, SEQ], F32, own)
        s5_t = sb("s5_t", [P, 2, 2, SEQ], F32, own)
        s5_h = sb("s5_h", [P, 2, 2, SEQ], F32, own)
        osb = sb("osb", [P, TT, HALF], F32, own)

    gw = act_h[:, :, :].rearrange("p a b -> p (a b)"), hid[:, :, :].rearrange("p a b -> p (a b)")
    gw = [g.rearrange("p (t c) -> p t c", t=4) for g in gw]

    def k_(name):
        a, n = where[name]
        return const[:, a:a + n]

    ident = k_("ident")
    banks = [ctx.enter_context(nc.psum_tensor(f"bank{i}", [P, 512], F32)) for i in range(8)]
    ACC, GU, TR = (0, 2), (4, 5), (6, 7)

    raw_in = [sem(f"raw_in{s}") for s in range(NSLOT)]
    hi_done, lo_done, unit_done = sem("hi_done"), sem("lo_done"), sem("unit_done")
    gu_full, silu_done, h_done = sem("gu_full"), sem("silu_done"), sem("h_done")
    h_turned, h_hi, h_lo = sem("h_turned"), sem("h_hi"), sem("h_lo")
    loaded = {n: sem(f"in_{n}") for n in ("const", "x", "mem", "nat", "rows", "gates", "gb", "s5", "s5b")}
    zeroed = steps("zeroed")
    gate_zero = steps("gate_zero")
    pe_half = steps("pe_half")
    pe_turn = steps("pe_turn")
    pe_core = steps("pe_core")
    act_ln = steps("act_ln")
    act_out = steps("act_out")
    act_hi = steps("act_hi")
    act_core = steps("act_core")
    dve_ln = steps("dve_ln")
    dve_out = steps("dve_out")
    dve_lo = steps("dve_lo")
    dve_core = steps("dve_core")
    pool_core = steps("pool_core")
    out_done = sem("out_done")

    def w3(ring, u, k):
        return ring[:, u % NSLOT, :].rearrange("p (k c) -> p k c", k=k)

    kv_of_norm = {0: (0, 0), 1: (0, 3), 2: (1, 0), 3: (1, 1), 4: (1, 2)}
    norm_units = {
        0: first[("ffn", 0)] + FFN_UNITS - 1, 1: first[("ev_out", 1)] + 1,
        2: first[(("xo", 0), 1)] + 1, 3: first[("ffn", 1)] + FFN_UNITS - 1,
        4: first[("ffn", 2)] + FFN_UNITS - 1, 5: first[("od_out", 1)] + 1,
        6: first[(("xo", 1), 1)] + 1, 7: first[("ffn", 3)] + FFN_UNITS - 1}


    def xrT_w(h):
        return xrT[:, :, :].rearrange("p a b -> p (a b)")[:, (h % 2) * 384:(h % 2) * 384 + 384]

    def wT(h):
        return lru_b[:, :, :].rearrange("p a b -> p (a b)")[:, (h % 2) * 384:(h % 2) * 384 + 384]

    def kT_da_flat(t):
        return kT_da[:, 2 * t:2 * t + 2, :].rearrange("p a b -> p (a b)")

    def scores_sb(h, m):
        return x[:, 0, :].rearrange("p d -> p d")[:, 0:768][:, m * 384:(m + 1) * 384] if h % 2 == 0 else \
            x[:, 1, 0:768][:, m * 384:(m + 1) * 384]

    def ret_w(h):
        return s5_g[:, h % 2, :, :].rearrange("p r k -> p (r k)")[:, 0:384]

    lru_gate = [x[:, g, :].rearrange("p (t k) -> p t k", t=4) for g in range(2)]
    ret_v = x[:, 0, :].rearrange("p (t d) -> p t d", t=TT)
    ret_gate = x[:, 1, :].rearrange("p (t d) -> p t d", t=TT)
    s5_y = [act_h[:, :, :], hid[:, :, :]]

    def end_of(key, t):
        name, u = key
        return pe_half.at(*name) if t == 0 else (unit_done, u + 2)

    block = ctx.enter_context(nc.Block())

    @block.sync
    def _(sp):
        sp.dma_start(const[:, :], A["constants"]).then_inc(loaded["const"], 16)
        sp.dma_start(x[:, :, :], A["x"][0].rearrange("(t p) d -> p t d", p=P)).then_inc(loaded["x"], 16)

        def room(u):
            if u >= NSLOT:
                sp.wait_ge(lo_done, u - NSLOT + 1)

        def columns(w, u):
            for half in range(2):
                room(u + half)
                for j in range(2):
                    r0 = half * HALF + j * 256
                    sp.dma_start(w3(raw, u + half, 4)[:, 2 * j:2 * j + 2, :],
                                 w[r0:r0 + 256, :].rearrange("(k p) c -> p k c", p=P)
                                 ).then_inc(raw_in[(u + half) % NSLOT], 16)

        def gate_up(wg, wu, u, b, wait):
            for half in range(2):
                if wait is not None:
                    sp.wait_ge(lo_done, wait + half)
                for j, w in enumerate((wg, wu)):
                    sp.dma_start(w3(raw, u + half, 4)[:, :, j * FB:(j + 1) * FB], w[b, half]
                                 ).then_inc(raw_in[(u + half) % NSLOT], 16)

        def down(wd, u, b, wait):
            sp.wait_ge(lo_done, wait)
            for j in range(2):
                sp.dma_start(w3(raw, u, 2)[:, j, :], wd[b, j]).then_inc(raw_in[u % NSLOT], 16)

        def ffn(f):
            l, j = f // 2, f % 2
            wg, wu = (A[n][l, j].rearrange("(h k p) (b c) -> b h p k c", p=P, k=4, c=FB)
                      for n in ("ffn_w_gate", "ffn_w_up"))
            wd = A["ffn_w_down"][l, j].rearrange("(b k p) c -> b k p c", p=P, k=2)
            u = first[("ffn", f)]
            gate_up(wg, wu, u, 0, u - NSLOT + 1 if u else None)
            with sp.Fori(0, NB - 1) as i:
                for half in range(2):
                    if u or half:
                        sp.wait_ge(lo_done, i * 3 + (u + 2 + half - NSLOT + 1))
                    else:
                        sp.wait_ge(lo_done, i * 3 + 1)
                    for q, w in enumerate((wg, wu)):
                        sp.dma_start(w3(raw, u + 2 + half, 4)[:, :, q * FB:(q + 1) * FB], w[i + 1, half]
                                     ).then_inc(raw_in[(u + 2 + half) % NSLOT], 16)
                down(wd, u + 4, i, i * 3 + (u + 4 - NSLOT + 1))
            down(wd, u + FFN_UNITS - 1, NB - 1, u + FFN_UNITS - NSLOT)

        def cols_of(name, l, c):
            return A[name][l][:, c * 512:(c + 1) * 512]

        def kv(l, c):
            columns(cols_of("xa_w_kv", l, c), first[(("kv", l), c)])

        def cross(l):
            for kind, name in (("xq", "xa_w_q"), ("xo", "xa_w_o")):
                for c in range(2):
                    columns(cols_of(name, l, c), first[((kind, l), c)])

        ffn(0)
        kv(0, 0)
        for c in (4, 3, 0, 1, 2):
            columns(cols_of("ev_w_in", 0, c), first[("ev_in", c)])
        kv(0, 1)
        kv(0, 2)
        for c in range(2):
            columns(cols_of("ev_w_out", 0, c), first[("ev_out", c)])
        kv(0, 3)
        cross(0)
        kv(1, 0)
        ffn(1)
        kv(1, 1)
        ffn(2)
        kv(1, 2)
        for c in range(4):
            columns(cols_of("od_w_in", 0, c), first[("od_in", c)])
        kv(1, 3)
        u = first["glu"]
        room(u)
        for j in range(2):
            sp.dma_start(w3(raw, u, 4)[:, 2 * j:2 * j + 2, :],
                         A["s5_glu_w"][0][j * 256:(j + 1) * 256, :].rearrange("(k p) c -> p k c", p=P)
                         ).then_inc(raw_in[u % NSLOT], 16)
        for c in range(2):
            columns(cols_of("od_w_out", 0, c), first[("od_out", c)])
        cross(1)
        ffn(3)
        for t in range(TT):
            sp.wait_ge(*dve_ln.at("x", NORMS - 1, t))
            sp.dma_start(A["out"][0, t * P:(t + 1) * P, :], x[:, t, :]).then_inc(out_done, 16)
        sp.wait_ge(out_done, 16 * TT)

    @block.gpsimd
    def _(pool):
        pool.dma_start(ax[:, :, :], A["mem"][0].rearrange("(t p) d -> p t d", p=P)).then_inc(loaded["mem"], 16)
        with nc.allow_non_contiguous_dma(reason="rows of parameters"):
            rows = [A["lru_conv_w"][0], A["lru_conv_b"], A["lru_gate_b"][0], A["lru_lambda"], A["s5_d"],
                    A["s5_glu_b"]]
            r = 0
            for a in rows:
                n = a.shape[0]
                pool.dma_start(nat[r:r + n, 0:512], a).then_inc(loaded["nat"], 16)
                r += n
            pool.dma_start(nat[0:16, 512:640], A["s5_lam_re"][0].rearrange("(j g) n -> j (g n)", g=2)
                           ).then_inc(loaded["nat"], 16)
            pool.dma_start(nat[0:16, 640:768], A["s5_lam_im"][0].rearrange("(j g) n -> j (g n)", g=2)
                           ).then_inc(loaded["nat"], 16)
            pool.dma_start(sm[0:16, 90:92], A["s5_log_step"][0].rearrange("(j g) -> j g", g=2)
                           ).then_inc(loaded["nat"], 16)
            pool.dma_start(da_g[:, :], A["da_norm_g"].partition_broadcast(P).rearrange("p a d -> p (a d)")
                           ).then_inc(loaded["rows"], 16)
            pool.dma_start(ret_g[:, :], A["ret_norm_g"].partition_broadcast(P).rearrange("p a d -> p (a d)")
                           ).then_inc(loaded["rows"], 16)
            pool.dma_start(tk[:, 0, 0, 0:256], A["da_lambda"].partition_broadcast(P)
                           .rearrange("p a b d -> p (a b d)")).then_inc(loaded["rows"], 16)

        def norm_rows(i):
            l, j = i // 4, i % 4
            pool.dma_start(gb[:, 0, :], A["ln_g"][l, j].partition_broadcast(P)).then_inc(loaded["gb"], 16)
            pool.dma_start(gb[:, 1, :], A["ln_b"][l, j].partition_broadcast(P)).then_inc(loaded["gb"], 16)

        norm_rows(0)
        for i in range(NORMS - 1):
            for t in range(TT):
                pool.wait_ge(*dve_ln.at("x", i, t))
            norm_rows(i + 1)
            if i == 0:
                for g in range(2):
                    pool.memset(gw[g], 0.0).then_inc(*gate_zero.up())
                pool.wait_ge(*gate_zero.now())
                with nc.allow_non_contiguous_dma(reason="64-float rows"):
                    for g in range(2):
                        for b in range(2):
                            src = A["lru_gate_w"][0, g].rearrange("(t b) c d -> b c t d", b=2)[b]
                            pool.dma_start(gw[g][64 * b:64 * b + 64, :, 64 * b:64 * b + 64], src
                                           ).then_inc(loaded["gates"], 16)
            if i == 2:
                with nc.allow_non_contiguous_dma(reason="16-float rows"):
                    for ri, n in enumerate(("s5_b_re", "s5_b_im")):
                        pool.dma_start(qkT[:, ri, 0, :].rearrange("p (j c) -> p j c", c=16),
                                       A[n][0].rearrange("(j g) n c -> (g n) j c", g=2)).then_inc(loaded["s5"], 16)
                    for ri, n in enumerate(("s5_c_re", "s5_c_im")):
                        pool.dma_start(qkT[:, ri, 1, :].rearrange("p (q n) -> p q n", n=64),
                                       A[n][0].rearrange("(q g) c n -> (g c) q n", g=8)).then_inc(loaded["s5"], 16)
                pool.wait_ge(*dve_core.at("theta"))
                pool.wait_ge(*pe_turn.at("s5_c", 1))
                n = 1
                while n < S5_CH:
                    sc = uT[:, :, :].rearrange("p a b -> p (a b)")[:, 0:16 * n].rearrange("p (j k) -> p j k", k=n)
                    ss = qkT[:, :, :, :].rearrange("p a b c -> p (a b c)")[:, 0:16 * n].rearrange(
                        "p (j k) -> p j k", k=n)
                    cl = e_cos[:, :, n - 1:n].to_broadcast([P, 16, n])
                    sl = e_sin[:, :, n - 1:n].to_broadcast([P, 16, n])
                    c0, s0 = e_cos[:, :, 0:n], e_sin[:, :, 0:n]
                    c1, s1 = e_cos[:, :, n:2 * n], e_sin[:, :, n:2 * n]
                    for a, b, c, d, out, op in ((c0, cl, s0, sl, c1, ALU.subtract), (s0, cl, c0, sl, s1, ALU.add)):
                        pool.tensor_tensor(sc, a, b, ALU.mult).then_inc(*pool_core.up())
                        pool.tensor_tensor(ss, c, d, ALU.mult).then_inc(*pool_core.up())
                        pool.wait_ge(*pool_core.now())
                        pool.tensor_tensor(out, sc, ss, op).then_inc(*pool_core.up("powers"))
                        pool.wait_ge(*pool_core.now())
                    n *= 2
            if i == 4:
                for j in range(S5_TILES):
                    pool.wait_ge(*dve_core.at("s5_g", j))
                    if j >= 2:
                        pool.wait_ge(*pe_core.at("s5_y", j - 2))
                    g = s5_g[:, j % 2].rearrange("p r (c k) -> p r c k", k=S5_CH)
                    h = s5_h[:, j % 2].rearrange("p r (c k) -> p r c k", k=S5_CH)
                    tc, ts = (s5_t[:, q].rearrange("p r (c k) -> p r c k", k=S5_CH) for q in range(2))
                    ec = e_cos[:, j, :].unsqueeze(1).unsqueeze(1).to_broadcast([P, 2, 2, S5_CH])
                    es = e_sin[:, j, :].unsqueeze(1).unsqueeze(1).to_broadcast([P, 2, 2, S5_CH])
                    pool.tensor_tensor(tc, g, ec, ALU.mult).then_inc(*pool_core.up())
                    pool.tensor_tensor(ts, g, es, ALU.mult).then_inc(*pool_core.up())
                    pool.wait_ge(*pool_core.now())
                    pool.tensor_tensor(h[:, 0], tc[:, 0], ts[:, 1], ALU.subtract).then_inc(*pool_core.up())
                    pool.tensor_tensor(h[:, 1], tc[:, 1], ts[:, 0], ALU.add).then_inc(*pool_core.up("s5_h", j))
                    pool.wait_ge(*pool_core.now())

    @block.tensor
    def _(pe):
        emptied = {}

        def take(b):
            for who, step in emptied.pop(b, ()):
                pe.wait_ge(*who.at(*step))

        def three(out, lh, ll, rh, rl, start, stop):
            pe.matmul(out, lh, rh, start=start, stop=False)
            pe.matmul(out, lh, rl, start=False, stop=False)
            return pe.matmul(out, ll, rh, start=False, stop=stop)

        def column_unit(u, half, sh, sl, dst, key):
            pe.wait_ge(lo_done, u + 1)
            wh, wl = w3(w_hi, u, 4), w3(w_lo, u, 4)
            for t in range(TT):
                for k in range(4):
                    kk = 4 * half + k
                    mm = three(banks[dst[t]][:, :], sh[:, kk, t * P:(t + 1) * P], sl[:, kk, t * P:(t + 1) * P],
                               wh[:, k, :], wl[:, k, :], kk == 0, kk == KT - 1)
                if t == 0 and half == 1:
                    mm.then_inc(*pe_half.up(*key))
            mm.then_inc(unit_done, 1)

        def column_block(key, u, sh, sl, dst, readers=None):
            for t in range(TT):
                take(dst[t])
            for half in range(2):
                column_unit(u + half, half, sh, sl, dst, key)
            if readers:
                for t in range(TT):
                    emptied[dst[t]] = [(who, (*step, t)) for who, step in readers]

        def gate_up_unit(u, half, free):
            wh, wl = w3(w_hi, u, 4), w3(w_lo, u, 4)
            for t in range(TT):
                if half == 0 and free is not None:
                    pe.wait_ge(h_done, free + t)
                for k in range(4):
                    kk = 4 * half + k
                    mm = three(banks[GU[t]][:, :], xT_hi[:, kk, t * P:(t + 1) * P],
                               xT_lo[:, kk, t * P:(t + 1) * P], wh[:, k, :], wl[:, k, :], kk == 0, kk == KT - 1)
                if t == 0 and half == 1:
                    mm.then_inc(gu_full, 1)
            mm.then_inc(unit_done, 1)

        def down_unit(u, last, key=None):
            wh, wl = w3(w_hi, u, 2), w3(w_lo, u, 2)
            for t in range(TT):
                for c in range(2):
                    for k in range(2):
                        mm = three(banks[ACC[t] + c][:, :], hT_hi[:, k, t * P:(t + 1) * P],
                                   hT_lo[:, k, t * P:(t + 1) * P], wh[:, k, c * 512:(c + 1) * 512],
                                   wl[:, k, c * 512:(c + 1) * 512], False, last and k == 1)
                if t == 0 and last:
                    mm.then_inc(*pe_half.up(*key))
            mm.then_inc(unit_done, 1)

        def turn_hidden(ready):
            for t in range(TT):
                pe.wait_ge(h_done, ready + t)
                if not_first_turn:
                    pe.wait_ge(h_lo, ready - 2 + t)
                for k in range(2):
                    mm = pe.transpose(banks[TR[t]][:, k * P:(k + 1) * P], hid[:, t, k * P:(k + 1) * P], ident)
                mm.then_inc(h_turned, 1)

        def ffn(f):
            nonlocal not_first_turn
            u, n = first[("ffn", f)], 2 * NB * f
            for b in range(4):
                take(b)
            for b in (*GU, *TR):
                take(b)
            for c in range(2):
                for t in range(TT):
                    pe.matmul(banks[ACC[t] + c][:, :], zero_r[:, :], xT_hi[:, 0:2, :], start=True, stop=False)
            for half in range(2):
                pe.wait_ge(lo_done, u + half + 1)
                gate_up_unit(u + half, half, n - 1 if f else None)
            not_first_turn = f > 0
            turn_hidden(n + 1)
            not_first_turn = True
            with pe.Fori(0, NB - 1) as i:
                for half in range(2):
                    pe.wait_ge(lo_done, i * 3 + (u + 3 + half))
                    gate_up_unit(u + 2 + half, half, i * 2 + (n + 1))
                pe.wait_ge(lo_done, i * 3 + (u + 5))
                pe.wait_ge(h_lo, i * 2 + (n + 2))
                down_unit(u + 4, False)
                turn_hidden(i * 2 + (n + 3))
            last = u + FFN_UNITS - 1
            pe.wait_ge(lo_done, last + 1)
            pe.wait_ge(h_lo, n + 2 * NB)
            down_unit(last, True, ("acc", f))

        not_first_turn = False

        def turn(name, src, ready, bank, reader, n=4):
            for who, step in ready:
                pe.wait_ge(*who.at(*step))
            take(bank)
            for j in range(n):
                mm = pe.transpose(banks[bank][:, j * P:(j + 1) * P], src[:, j * P:(j + 1) * P], ident)
            mm.then_inc(*pe_turn.up(*name))
            emptied[bank] = reader

        def turn_split(name, t, half, src, ready):
            turn((name, t, half), src, ready, TR[half], [(dve_lo, (name, t, half))])

        def turn_out(name, src, who=act_out):
            for t in range(TT):
                turn((name, t), src[:, t, :], [(who, (name, t))], TR[t], [(dve_out, (name, t))])

        def kv_block(l, c):
            name = ("kv", l, c)
            column_block(name, first[(("kv", l), c)], memT_hi, memT_lo, GU, [(act_out, (name,))])

        def norm(i, turn_it=True):
            for t in range(TT):
                for c in range(2):
                    emptied[ACC[t] + c] = [(dve_ln, ("sum", i, t))]
            kv = kv_of_norm.get(i)
            if kv:
                kv_block(*kv)
            if turn_it:
                for t in range(TT):
                    for half in range(2):
                        turn_split(("x", i), t, half, x[:, t, half * HALF:(half + 1) * HALF],
                                   [(dve_ln, ("x", i, t))])
            if kv and kv[1] < 2:
                turn_out(("kv", *kv), tk[:, kv[1] % 2])

        def operand_ready(name, halves=(0, 1)):
            for t in range(TT):
                for half in halves:
                    pe.wait_ge(*dve_lo.at(name, t, half))

        def out_blocks(kind):
            for c in range(2):
                dst = (ACC[0] + c, ACC[1] + c)
                for t in range(TT):
                    take(dst[t])
                for half in range(2):
                    column_unit(first[(kind, c)] + half, half, xT_hi, xT_lo, dst, (kind, c))

        def even_mixer():
            nm = {4: "xr", 3: "gate", 0: "q", 1: "k", 2: "v"}

            def project(c, dst):
                column_block(("ev", c), first[("ev_in", c)], xT_hi, xT_lo, dst, [(act_out, (nm[c],))])

            project(4, (4, 5))
            project(3, (0, 1))
            turn_out("xr", tk[:, 0])
            project(0, (2, 3))
            pe.wait_ge(loaded["gates"], 64)
            pe.wait_ge(*dve_core.at("conv"))
            for g in range(2):
                for t2 in range(2):
                    take(TR[t2])
                    for j in range(2):
                        tile = 2 * t2 + j
                        mm = pe.matmul(banks[TR[t2]][:, j * SEQ:(j + 1) * SEQ], gw[g][:, tile, :],
                                       conv[:, tile, :], start=True, stop=True)
                    mm.then_inc(*pe_core.up("gates", g, t2))
                    emptied[TR[t2]] = [(act_core, ("gates", g, t2))]
            turn_out("gate", tk[:, 1])
            project(1, (4, 5))
            turn_out("q", tk[:, 0], dve_core)
            project(2, (0, 1))
            turn_out("k", tk[:, 1], dve_core)
            kv_block(0, 1)

            def scores(h):
                for m in range(2):
                    b = 2 * (h % 2) + m
                    take(b)
                    r = slice(64 * m, 64 * m + 64)
                    pe.matmul(banks[b][:, 0:P], qT_da[r, h, 0:P], kT_da[r, h, 0:P], start=True, stop=True)
                    pe.matmul(banks[b][:, P:3 * P], qT_da[r, h, P:SEQ], kT_da[r, h, :], start=True, stop=True
                              ).then_inc(*pe_core.up("scores", h, m))
                    emptied[b] = [(dve_core, ("masked", h, m))]

            def weights(h):
                b = TR[h % 2]
                pe.wait_ge(*dve_core.at("weights", h))
                take(b)
                for j in range(3):
                    mm = pe.transpose(banks[b][:, j * P:(j + 1) * P], xrT_w(h)[:, j * P:(j + 1) * P], ident)
                mm.then_inc(*pe_turn.up("weights", h))
                emptied[b] = [(act_core, ("wT", h))]

            def values(h):
                pe.wait_ge(*act_core.at("wT", h))
                w = wT(h)
                c = slice(h * P, (h + 1) * P)
                if h == 0:
                    take(4)
                    take(5)
                pe.matmul(banks[4][:, c], w[:, 0:P], v_da[:, 0, c], start=True, stop=True)
                pe.matmul(banks[5][:, c], w[:, P:2 * P], v_da[:, 0, c], start=True, stop=False)
                pe.matmul(banks[5][:, c], w[:, 2 * P:3 * P], v_da[:, 1, c], start=False, stop=True
                          ).then_inc(*pe_core.up("o", h))

            for n in ("q", "k"):
                for t in range(TT):
                    pe.wait_ge(*dve_out.at(n, t))
            for t in range(TT):
                pe.wait_ge(*act_out.at("v", t))
            scores(0)
            scores(1)
            for h in range(DA_H):
                weights(h)
                if h + 2 < DA_H:
                    scores(h + 2)
                values(h)
            turn_out(("kv", 0, 1), tk[:, 1])
            for t in range(TT):
                emptied[4 + t] = [(dve_core, ("o_copy", t))]
            column_block(("kv", 0, 2), first[(("kv", 0), 2)], memT_hi, memT_lo, (0, 1), [(act_out, (("kv", 0, 2),))])
            for t in range(TT):
                turn_split("a_out", t, 0, kT_da_flat(t), [(dve_core, ("a_out", t))])
            operand_ready("a_out", (0,))
            pe.wait_ge(*dve_lo.at("b_out"))
            out_blocks("ev_out")

        def cross(l):
            for c in range(2):
                column_block(("xq", l, c), first[(("xq", l), c)], xT_hi, xT_lo, GU if c == 0 else (0, 1),
                             [(act_out, (("xq", l, c),))])
                if c == 1:
                    turn_out(("xq", l, 0), tk[:, 0])
            turn_out(("xq", l, 1), tk[:, 1])
            for c in range(2):
                for t in range(TT):
                    pe.wait_ge(*dve_out.at(("xq", l, c), t))
                    pe.wait_ge(*act_out.at(("kv", l, 2 + c), t))

            def scores(h):
                b = h % 4
                take(b)
                for t in range(TT):
                    for j in range(2):
                        mm = pe.matmul(banks[b][:, t * SEQ:(t + 1) * SEQ], q_x[:, 2 * h + j, t * P:(t + 1) * P],
                                       k_mem[:, 2 * h + j, :], start=(j == 0), stop=(j == 1))
                mm.then_inc(*pe_core.up("xs", l, h))
                emptied[b] = [(act_core, ("xp", l, h))]

            def weights(h):
                b = TR[h % 2]
                pe.wait_ge(*dve_core.at("xw", l, h))
                take(b)
                for mt in range(2):
                    for t in range(TT):
                        mm = pe.transpose(banks[b][:, mt * SEQ + t * P:mt * SEQ + (t + 1) * P],
                                          p_x[:, h % 2, t, mt * P:(mt + 1) * P], ident)
                mm.then_inc(*pe_turn.up("xw", l, h))
                emptied[b] = [(act_core, ("xpT", l, h))]

            def values(h):
                pe.wait_ge(*act_core.at("xpT", l, h))
                b = GU[h % 2]
                take(b)
                for j in range(2):
                    for mt in range(2):
                        c0 = h * XA_D + j * P
                        mm = pe.matmul(banks[b][:, j * SEQ:(j + 1) * SEQ], v_mem[:, mt, c0:c0 + P],
                                       pT_x[:, h % 2, mt, :], start=(mt == 0), stop=(mt == 1))
                mm.then_inc(*pe_core.up("xo", l, h))
                emptied[b] = [(dve_lo, ("xo", l, h))]

            scores(0)
            scores(1)
            for h in range(XA_H):
                weights(h)
                if h + 2 < XA_H:
                    scores(h + 2)
                values(h)
            for h in range(XA_H):
                pe.wait_ge(*dve_lo.at("xo", l, h))
            out_blocks(("xo", l))

        def s5_prepare():
            for kind, n in (("s5_b", 0), ("s5_c", 1)):
                for ri in range(2):
                    src = uT[:, 2 * ri:2 * ri + 2, :].rearrange("p a b -> p (a b)")
                    turn((kind, ri), src, [(dve_core, (kind, ri))], TR[ri], [(dve_core, (kind + "T", ri))])

        def odd_mixer():
            nm = {0: "u", 1: "qk", 2: "rv", 3: "rg"}

            def project(c, dst):
                column_block(("od", c), first[("od_in", c)], xT_hi, xT_lo, dst, [(act_out, (nm[c],))])

            project(0, (4, 5))
            project(1, (0, 1))
            turn_out("u", tk[:, 0])
            project(2, (2, 3))
            turn_out("qk", tk[:, 1], dve_core)
            project(3, (4, 5))
            kv_block(1, 3)
            for t in range(TT):
                pe.wait_ge(*dve_out.at("u", t))
                pe.wait_ge(*dve_out.at("qk", t))
            for b in range(4):
                take(b)

            def inputs(j):
                take(j % 4)
                r = slice(32 * (j % 4), 32 * (j % 4) + 32)
                for ri in range(2):
                    mm = pe.matmul(banks[j % 4][:, ri * SEQ:(ri + 1) * SEQ], s5_bT[r, ri, j // 4, :],
                                   uT[r, j // 4, :], start=True, stop=True)
                mm.then_inc(*pe_core.up("s5_x", j))
                emptied[j % 4] = [(dve_core, ("s5_in", j))]

            def outputs(j):
                pe.wait_ge(*pool_core.at("s5_h", j))
                if j == 0:
                    take(4)
                    take(5)
                q, r = j // 4, 32 * (j % 4)
                for ri in range(2):
                    mm = pe.matmul(banks[4 + q // 2][r:r + 32, (q % 2) * SEQ:(q % 2 + 1) * SEQ],
                                   s5_cT[:, ri, q, r:r + 32], s5_h[:, j % 2, ri, :],
                                   start=(ri == 0), stop=(ri == 1))
                mm.then_inc(*pe_core.up("s5_y", j))

            inputs(0)
            inputs(1)
            for j in range(S5_TILES):
                if j + 2 < S5_TILES:
                    inputs(j + 2)
                outputs(j)
            u = first["glu"]
            pe.wait_ge(lo_done, u + 1)
            pe.wait_ge(*dve_lo.at("z"))
            wh, wl = w3(w_hi, u, 4), w3(w_lo, u, 4)
            for o in range(4):
                if o % 2 == 0:
                    take(TR[o // 2])
                for k in range(4):
                    c = slice(o * P, (o + 1) * P)
                    mm = three(banks[TR[o // 2]][:, (o % 2) * SEQ:(o % 2 + 1) * SEQ], wh[:, k, c], wl[:, k, c],
                               xT_hi[:, k, :], xT_lo[:, k, :], k == 0, k == 3)
            mm.then_inc(unit_done, 1)
            for q in range(2):
                emptied[TR[q]] = [(act_core, ("glu", 3))]

            for h in range(RET_H):
                take(h)
                r = slice(64 * (h % 2), 64 * (h % 2) + 64)
                q, k = qkT[r, 0, h // 2, :], qkT[r, 1, h // 2, :]
                pe.matmul(banks[h][:, 0:SEQ], k[:, 0:P], q, start=True, stop=True)
                pe.matmul(banks[h][:, SEQ:SEQ + P], k[:, P:SEQ], q[:, P:SEQ], start=True, stop=True
                          ).then_inc(*pe_core.up("ret_s", h))
                emptied[h] = [(dve_core, ("ret_w", h))]
            pe.wait_ge(*dve_core.at("s5_out", 3))
            for h in range(RET_H):
                pe.wait_ge(*dve_core.at("ret_w", h))
                w, v = ret_w(h), ret_v
                c = slice(h * P, (h + 1) * P)
                pe.matmul(banks[4][:, c], w[:, 0:P], v[:, 0, c], start=True, stop=True)
                pe.matmul(banks[5][:, c], w[:, P:SEQ], v[:, 0, c], start=True, stop=False)
                pe.matmul(banks[5][:, c], w[:, SEQ:SEQ + P], v[:, 1, c], start=False, stop=True
                          ).then_inc(*pe_core.up("ret_o", h))
            for t in range(TT):
                emptied[4 + t] = [(dve_core, ("ret_n", t))]
            for t in range(TT):
                turn_split("d_out", t, 1, osb[:, t, :], [(dve_core, ("d_out", t))])
            operand_ready("d_out", (1,))
            pe.wait_ge(*dve_lo.at("c_out"))
            out_blocks("od_out")

        pe.wait_ge(loaded["const"], 16)
        pe.wait_ge(*zeroed.at("zero"))
        pe.wait_ge(loaded["nat"], 16 * 9)
        for j in range(4):
            mm = pe.transpose(banks[0][:, 16 * j:16 * j + 10], nat[0:10, j * P:(j + 1) * P], ident[0:10, 0:10])
        pe.wait_ge(*dve_core.at("log_step"))
        for j in range(3):
            mm = pe.transpose(banks[0][:, 64 + 16 * j:80 + 16 * j], nat[0:16, 512 + j * P:512 + (j + 1) * P],
                              ident[0:16, 0:16])
        mm.then_inc(*pe_turn.up("params"))
        emptied[0] = [(dve_core, ("params",))]
        pe.wait_ge(loaded["x"], 16)
        for t in range(TT):
            for half in range(2):
                turn_split("x_in", t, half, x[:, t, half * HALF:(half + 1) * HALF], [])
        pe.wait_ge(loaded["mem"], 16)
        for t in range(TT):
            for half in range(2):
                turn_split("mem", t, half, ax[:, t, half * HALF:(half + 1) * HALF], [])
        operand_ready("x_in")
        ffn(0)
        operand_ready("mem")
        norm(0)
        operand_ready(("x", 0))
        even_mixer()
        norm(1)
        operand_ready(("x", 1))
        cross(0)
        norm(2)
        operand_ready(("x", 2))
        s5_prepare()
        ffn(1)
        norm(3)
        operand_ready(("x", 3))
        ffn(2)
        norm(4)
        operand_ready(("x", 4))
        odd_mixer()
        norm(5)
        operand_ready(("x", 5))
        cross(1)
        norm(6)
        operand_ready(("x", 6))
        ffn(3)

    @block.scalar
    def _(act):
        split = [0]

        def split_to(u):
            while split[0] <= u:
                v = split[0]
                if v < n_units:
                    act.wait_ge(raw_in[v % NSLOT], 32 * (v // NSLOT + 1))
                    if v >= NSLOT:
                        act.wait_ge(unit_done, v - NSLOT + 1)
                    act.activation(w_hi[:, v % NSLOT, :], raw[:, v % NSLOT, :], ACT.Copy).then_inc(hi_done, 1)
                split[0] += 1

        def ffn(f):
            u, n = first[("ffn", f)], 2 * NB * f

            def hi(c, i):
                v = u + 2 + c
                act.wait_ge(raw_in[v % NSLOT], i * 32 + 32 * (v // NSLOT + 1))
                act.wait_ge(unit_done, i * 3 + (v - NSLOT + 1))
                act.activation(w_hi[:, v % NSLOT, :], raw[:, v % NSLOT, :], ACT.Copy).then_inc(hi_done, 1)

            def silu(t, full0, full1, free):
                if t == 0:
                    act.wait_ge(gu_full, full0)
                else:
                    act.wait_ge(unit_done, full1)
                if free is not None:
                    act.wait_ge(h_done, free + t)
                act.activation(act_h[:, t, :], banks[GU[t]][:, 0:FB], ACT.Silu).then_inc(silu_done, 1)

            def hidden_hi(t, ready):
                act.wait_ge(h_turned, ready + t)
                act.activation(hT_hi[:, :, t * P:(t + 1) * P],
                               banks[TR[t]][:, 0:2 * P].rearrange("p (k c) -> p k c", k=2), ACT.Copy
                               ).then_inc(h_hi, 1)

            split_to(u + 2)
            for t in range(TT):
                silu(t, NB * f + 1, u + 2, n - 1 if f else None)
            with act.Fori(0, NB - 1) as i:
                for t in range(TT):
                    hidden_hi(t, i * 2 + (n + 1))
                hi(1, i)
                hi(2, i)
                for t in range(TT):
                    silu(t, i + (NB * f + 2), i * 3 + (u + 4), i * 2 + (n + 1))
                hi(3, i)
            split[0] = u + 3 + 3 * (NB - 1)
            for t in range(TT):
                hidden_hi(t, n + 2 * NB - 1)

        def split_operand(name, t, half, dst=None):
            act.wait_ge(*pe_turn.at(name, t, half))
            dst = xT_hi if dst is None else dst
            act.activation(dst[:, 4 * half:4 * half + 4, t * P:(t + 1) * P],
                           banks[TR[half]][:, :].rearrange("p (k c) -> p k c", k=4), ACT.Copy
                           ).then_inc(*act_hi.up(name, t, half))

        def copy_out(name, key, u, dst, bank, fn=ACT.Copy, free=None):
            split_to(u + 3)
            if free is not None:
                for t in range(TT):
                    act.wait_ge(*pe_turn.at(free, t))
            for t in range(TT):
                act.wait_ge(*end_of((key, u), t))
                act.activation(dst[:, t, :], banks[bank[t]][:, :], fn).then_inc(*act_out.up(name, t))

        def kv_out(l, c, bank=GU, free=None):
            name = ("kv", l, c)
            u = first[(("kv", l), c)]
            if c < 2:
                copy_out(name, name, u, tk[:, c % 2], bank, free=free)
            else:
                copy_out(name, name, u, v_mem[:, :, (c - 2) * HALF:(c - 1) * HALF], bank)

        def norm(i, last=False, free=None):
            e = norm_units[i]
            split_to(e + 2)
            for t in range(TT):
                act.wait_ge(*dve_ln.at("var", i, t))
                act.activation(mv[:, t, 2:3], mv[:, t, 1:2], ACT.Sqrt, bias=eps_col).then_inc(*act_ln.up("sd", i, t))
                if not last:
                    act.wait_ge(*dve_ln.at("x", i, t))
                    act.activation(ax[:, t, :], x[:, t, :], ACT.Copy, scale=ALPHA).then_inc(*act_ln.up("ax", i, t))
            if last:
                return
            kv = kv_of_norm.get(i)
            if kv:
                kv_out(*kv, free=free)
            for t in range(TT):
                for half in range(2):
                    split_operand(("x", i), t, half)

        def even_mixer():
            copy_out("xr", ("ev", 4), first[("ev_in", 4)], tk[:, 0], (4, 5), free=("kv", 0, 0))
            copy_out("gate", ("ev", 3), first[("ev_in", 3)], tk[:, 1], (0, 1), ACT.Gelu_apprx_tanh)
            copy_out("q", ("ev", 0), first[("ev_in", 0)], tk[:, 0], (2, 3), free="xr")
            for g in range(2):
                for t2 in range(2):
                    act.wait_ge(*pe_core.at("gates", g, t2))
                    for j in range(2):
                        tile = 2 * t2 + j
                        ins = act.activation(lru_gate[g][:, tile, :], banks[TR[t2]][:, j * SEQ:(j + 1) * SEQ],
                                             ACT.Sigmoid, bias=pv[:, tile, 5 + g:6 + g]
                                             ).then_inc(*act_core.up("gates", g, t2))
            act.wait_ge(*act_core.now())
            act.wait_ge(*dve_core.at("softplus"))
            for tile in range(4):
                act.activation(lru_a[:, tile, :], lru_gate[0][:, tile, :], ACT.Exp, scale=sm[:, 4 + tile:5 + tile]
                               ).then_inc(*act_core.up())
                act.activation(lru_b[:, tile, :], lru_gate[0][:, tile, :], ACT.Tanh, scale=sm[:, tile:tile + 1]
                               ).then_inc(*act_core.up("decay"))
            copy_out("k", ("ev", 1), first[("ev_in", 1)], tk[:, 1], (4, 5), free="gate")
            act.wait_ge(*dve_core.at("one_minus_a2"))
            act.activation(lru_gate[0], lru_gate[0], ACT.Sqrt).then_inc(*act_core.up("root"))
            copy_out("v", ("ev", 2), first[("ev_in", 2)], v_da, (0, 1))
            kv_out(0, 1, free="k")
            act.wait_ge(*dve_core.at("b_out"))
            act.activation(xT_hi[:, 4:8, :], gateT[:, :, :], ACT.Copy).then_inc(*act_hi.up("b_out"))

            def exps(h):
                for m in range(2):
                    act.wait_ge(*dve_core.at("max", h, m))
                    for t in range(TT):
                        c = slice(0, P) if t == 0 else slice(P, 3 * P)
                        s = scores_sb(h, m)[:, c]
                        k = 16 + 4 * (h % 2) + 2 * m + t
                        act.activation(s, s, ACT.Exp, bias=sm[:, k:k + 1], scale=DA_D ** -0.5,
                                       accum_out=sm[:, k + 8:k + 9]).then_inc(*act_core.up("exp", h, m))

            exps(0)
            for h in range(DA_H):
                if h + 1 < DA_H:
                    exps(h + 1)
                act.wait_ge(*pe_turn.at("weights", h))
                act.activation(wT(h), banks[TR[h % 2]][:, 0:384], ACT.Copy).then_inc(*act_core.up("wT", h))
            split_to(first[("ev_out", 0)])
            for t in range(TT):
                act.wait_ge(*dve_core.at("rms", t))
                act.activation(sm[:, 44 + 4 * t:48 + 4 * t], sm[:, 36 + 4 * t:40 + 4 * t], ACT.Sqrt,
                               scale=1.0 / (2 * DA_D), bias=eps_col).then_inc(*act_core.up("rms", t))
            kv_out(0, 2, (0, 1))
            for t in range(TT):
                split_operand("a_out", t, 0)

        def cross(l):
            for c in range(2):
                name = ("xq", l, c)
                copy_out(name, name, first[(("xq", l), c)], tk[:, c], GU if c == 0 else (0, 1))

            def exps(h):
                act.wait_ge(*dve_core.at("xmax", l, h))
                for t in range(TT):
                    k = 52 + 2 * (h % 2) + t
                    act.activation(p_x[:, h % 2, t, :], banks[h % 4][:, t * SEQ:(t + 1) * SEQ], ACT.Exp,
                                   bias=sm[:, k:k + 1], scale=XA_D ** -0.5, accum_out=sm[:, k + 4:k + 5]
                                   ).then_inc(*act_core.up("xp", l, h))

            def out_hi(h):
                act.wait_ge(*pe_core.at("xo", l, h))
                act.activation(xT_hi[:, 2 * h:2 * h + 2, :],
                               banks[GU[h % 2]][:, :].rearrange("p (k c) -> p k c", k=2), ACT.Copy
                               ).then_inc(*act_hi.up("xo", l, h))

            exps(0)
            exps(1)
            for h in range(XA_H):
                act.wait_ge(*pe_turn.at("xw", l, h))
                act.activation(pT_x[:, h % 2, :, :], banks[TR[h % 2]][:, :].rearrange("p (k c) -> p k c", k=2),
                               ACT.Copy).then_inc(*act_core.up("xpT", l, h))
                if h + 2 < XA_H:
                    exps(h + 2)
                out_hi(h)

        def odd_mixer():
            copy_out("u", ("od", 0), first[("od_in", 0)], tk[:, 0], (4, 5))
            copy_out("qk", ("od", 1), first[("od_in", 1)], tk[:, 1], (0, 1))
            copy_out("rv", ("od", 2), first[("od_in", 2)], ret_v, (2, 3))
            copy_out("rg", ("od", 3), first[("od_in", 3)], ret_gate, (4, 5), ACT.Silu)
            kv_out(1, 3)
            for q in range(4):
                act.wait_ge(*dve_core.at("s5_out", q))
            for a in range(2):
                act.activation(s5_y[a], s5_y[a], ACT.Gelu_apprx_tanh).then_inc(*act_core.up("gelu"))
            act.wait_ge(*act_core.now())
            for a in range(2):
                act.activation(xT_hi[:, 2 * a:2 * a + 2, :], s5_y[a], ACT.Copy).then_inc(*act_hi.up("z"))
            act.wait_ge(unit_done, first["glu"] + 1)
            for o in range(4):
                act.activation(s5_t[:, o // 2, o % 2, :], banks[TR[o // 2]][:, (o % 2) * SEQ:(o % 2 + 1) * SEQ],
                               ACT.Sigmoid, bias=pv[:, o, 9:10]).then_inc(*act_core.up("glu", o))
            act.wait_ge(*dve_core.at("c_out"))
            for a in range(2):
                act.activation(xT_hi[:, 2 * a:2 * a + 2, :], s5_y[a], ACT.Copy).then_inc(*act_hi.up("c_out"))
            split_to(first[("od_out", 0)] + 1)
            act.wait_ge(*dve_core.at("ret_var"))
            act.activation(sm[:, 78:86], s5_h[:, 0, 0, 64:80].rearrange("p (a b) -> p a b", b=2)[:, :, 1], ACT.Sqrt,
                           bias=eps_col).then_inc(*act_core.up("ret_sd"))
            for t in range(TT):
                split_operand("d_out", t, 1)

        eps_col = sm[:, 92:93]
        act.wait_ge(*dve_core.at("neg_abs"))
        act.activation(sm[:, 8:12], sm[:, 12:16], ACT.Exp).then_inc(*act_core.up("exp_lambda"))
        act.wait_ge(*dve_core.at("lambda_sum"))
        act.activation(sm[:, 32:34], sm[:, 34:36], ACT.Exp).then_inc(*act_core.up("da_exp"))
        for t in range(TT):
            for half in range(2):
                split_operand("x_in", t, half)
        split_to(1)
        for t in range(TT):
            for half in range(2):
                split_operand("mem", t, half, memT_hi)
        for t in range(TT):
            for half in range(2):
                act.wait_ge(*pe_turn.at("mem", t, half))
            act.activation(ax[:, t, :], x[:, t, :], ACT.Copy, scale=ALPHA).then_inc(*act_ln.up("ax", -1, t))
        ffn(0)
        norm(0)
        even_mixer()
        norm(1)
        cross(0)
        norm(2, free=("xq", 0, 0))
        s = s5_par
        act.wait_ge(*dve_core.at("s5_args"))
        act.activation(s(3), s(3), ACT.Exp).then_inc(*act_core.up("s5_step"))
        act.wait_ge(*dve_core.at("s5_angle"))
        act.activation(s(4), s(4), ACT.Exp).then_inc(*act_core.up())
        act.activation(s(5), s(6), ACT.Sin).then_inc(*act_core.up())
        act.activation(s(7), s(6), ACT.Sin, scale=0.5).then_inc(*act_core.up("s5_sin"))
        ffn(1)
        norm(3, free=("kv", 1, 0))
        ffn(2)
        norm(4)
        odd_mixer()
        norm(5)
        cross(1)
        norm(6)
        ffn(3)
        norm(7, last=True)

    @block.vector
    def _(v):
        split = [0]
        V = nc.vector

        def split_to(u):
            while split[0] <= u:
                w = split[0]
                if w < n_units:
                    v.wait_ge(hi_done, w + 1)
                    s = w % NSLOT
                    V.tensor_tensor(w_lo[:, s, :], raw[:, s, :], w_hi[:, s, :].bitcast(F32), ALU.subtract
                                    ).then_inc(lo_done, 1)
                split[0] += 1

        def ffn(f):
            u, n = first[("ffn", f)], 2 * NB * f

            def lo(c, i):
                s = (u + 2 + c) % NSLOT
                v.wait_ge(hi_done, i * 3 + (u + 3 + c))
                V.tensor_tensor(w_lo[:, s, :], raw[:, s, :], w_hi[:, s, :].bitcast(F32), ALU.subtract
                                ).then_inc(lo_done, 1)

            def hidden(t, ready, turned):
                v.wait_ge(silu_done, ready + t)
                if turned is not None:
                    v.wait_ge(h_turned, turned + t)
                V.tensor_tensor(hid[:, t, :], act_h[:, t, :], banks[GU[t]][:, FB:2 * FB], ALU.mult
                                ).then_inc(h_done, 1)

            def hidden_lo(t, ready):
                v.wait_ge(h_hi, ready + t)
                V.tensor_tensor(hT_lo[:, :, t * P:(t + 1) * P],
                                banks[TR[t]][:, 0:2 * P].rearrange("p (k c) -> p k c", k=2),
                                hT_hi[:, :, t * P:(t + 1) * P].bitcast(F32), ALU.subtract).then_inc(h_lo, 1)

            split_to(u + 2)
            for t in range(TT):
                hidden(t, n + 1, n - 1 if f else None)
            with v.Fori(0, NB - 1) as i:
                for t in range(TT):
                    hidden_lo(t, i * 2 + (n + 1))
                lo(1, i)
                lo(2, i)
                for t in range(TT):
                    hidden(t, i * 2 + (n + 3), i * 2 + (n + 1))
                lo(3, i)
            split[0] = u + 3 + 3 * (NB - 1)
            for t in range(TT):
                hidden_lo(t, n + 2 * NB - 1)

        def split_operand(name, t, half, hi=None, lo=None):
            hi = xT_hi if hi is None else hi
            lo = xT_lo if lo is None else lo
            v.wait_ge(*act_hi.at(name, t, half))
            at = (slice(None), slice(4 * half, 4 * half + 4), slice(t * P, (t + 1) * P))
            V.tensor_tensor(lo[at], banks[TR[half]][:, :].rearrange("p (k c) -> p k c", k=4), hi[at].bitcast(F32),
                            ALU.subtract).then_inc(*dve_lo.up(name, t, half))

        def feature_out(name, dst):
            for t in range(TT):
                v.wait_ge(*pe_turn.at(name, t))
                V.tensor_copy(dst(t), banks[TR[t]][:, :].rearrange("p (k c) -> p k c", k=4)
                              ).then_inc(*dve_out.up(name, t))

        def kv_turned(l, c):
            if c < 2:
                feature_out(("kv", l, c), lambda t: k_mem[:, 4 * c:4 * c + 4, t * P:(t + 1) * P])

        def norm(i, scale, key, last=False):
            e = norm_units[i]
            split_to(e + 2)
            v.wait_ge(loaded["gb"], 32 * (i + 1))
            for t in range(TT):
                v.wait_ge(*act_ln.at("ax", i - 1, t))
                if t == 0:
                    v.wait_ge(*pe_half.at(*key))
                else:
                    v.wait_ge(unit_done, e + 1)
                for c in range(2):
                    s = slice(c * 512, (c + 1) * 512)
                    V.scalar_tensor_tensor(out=x[:, t, s], in0=banks[ACC[t] + c][:, :], scalar=scale,
                                           in1=ax[:, t, s], op0=ALU.mult, op1=ALU.add
                                           ).then_inc(*dve_ln.up("sum", i, t))
                for c in range(2):
                    v.wait_ge(dve_ln.sem, dve_ln.n - (1 if c == 0 else 1))
                    V.bn_stats(bn[:, t, 6 * c:6 * c + 6], x[:, t, c * 512:(c + 1) * 512]).then_inc(*dve_ln.up())
                v.wait_ge(*dve_ln.now())
                V.bn_aggr(mv[:, t, 0:2], bn[:, t, :]).then_inc(*dve_ln.up("var", i, t))
                v.wait_ge(*dve_ln.now())
                V.scalar_tensor_tensor(out=x[:, t, :], in0=x[:, t, :], scalar=mv[:, t, 0:1], in1=gb[:, 0, :],
                                       op0=ALU.subtract, op1=ALU.mult).then_inc(*dve_ln.up())
                v.wait_ge(*act_ln.at("sd", i, t))
                V.reciprocal(mv[:, t, 3:4], mv[:, t, 2:3]).then_inc(*dve_ln.up())
                v.wait_ge(*dve_ln.now())
                V.scalar_tensor_tensor(out=x[:, t, :], in0=x[:, t, :], scalar=mv[:, t, 3:4], in1=gb[:, 1, :],
                                       op0=ALU.mult, op1=ALU.add).then_inc(*dve_ln.up("x", i, t))
            if last:
                return
            kv = kv_of_norm.get(i)
            if kv:
                split_to(e + 4)
            for t in range(TT):
                for half in range(2):
                    split_operand(("x", i), t, half)
            if kv:
                kv_turned(*kv)

        def op(ins, *name):
            return ins.then_inc(*dve_core.up(*name))

        def done():
            v.wait_ge(*dve_core.now())

        def rotate(name, t, data, halfw, cos, sin, ta, tb):
            lo, hi = slice(0, halfw), slice(halfw, 2 * halfw)
            V.tensor_tensor(ta, data, cos, ALU.mult).then_inc(*dve_core.up())
            V.tensor_tensor(tb[..., lo], data[..., hi], sin[..., lo], ALU.mult).then_inc(*dve_core.up())
            V.tensor_tensor(tb[..., hi], data[..., lo], sin[..., hi], ALU.mult).then_inc(*dve_core.up())
            v.wait_ge(*dve_core.now())
            V.tensor_tensor(data, ta, tb, ALU.add).then_inc(*dve_core.up(name, t))

        def even_mixer():
            split_to(first[("ev_in", 3)] + 3)
            V.memset(xrT[:, :, 0:3], 0.0).then_inc(*dve_core.up())
            feature_out("xr", lambda t: xrT[:, :, 3 + t * P:3 + (t + 1) * P])
            v.wait_ge(*dve_out.now())
            v.wait_ge(*dve_core.now())
            for k in range(4):
                for tile in range(4):
                    src = xrT[:, tile, k:k + SEQ]
                    if k == 0:
                        V.tensor_scalar(conv[:, tile, :], src, pv[:, tile, 0:1], pv[:, tile, 4:5], ALU.mult, ALU.add
                                        ).then_inc(*dve_core.up())
                    else:
                        v.wait_ge(dve_core.sem, dve_core.n - 3)
                        V.scalar_tensor_tensor(out=conv[:, tile, :], in0=src, scalar=pv[:, tile, k:k + 1],
                                               in1=conv[:, tile, :], op0=ALU.mult, op1=ALU.add
                                               ).then_inc(*dve_core.up("conv"))
            split_to(first[("ev_in", 0)] + 3)
            feature_out("gate", lambda t: gateT[:, :, t * P:(t + 1) * P])
            ta, tb = rot_tmp[:, 0, :], rot_tmp[:, 1, :]

            def rotate_da(name, buf):
                for t in range(TT):
                    v.wait_ge(*act_out.at(name, t))
                    d3 = tk[:, buf, t, :].rearrange("p (g d) -> p g d", d=DA_D)[:, :, 0:DA_ROPE]
                    cs, sn = (k_(n).rearrange("p (t g d) -> p t g d", t=TT, d=DA_ROPE)[:, t]
                              for n in ("da_cos", "da_sin"))
                    done()
                    rotate(name, t, d3, DA_ROPE // 2, cs, sn, ta.rearrange("p (g d) -> p g d", d=DA_ROPE),
                           tb.rearrange("p (g d) -> p g d", d=DA_ROPE))

            rotate_da("q", 0)
            split_to(first[("ev_in", 1)] + 3)
            v.wait_ge(*act_core.at("decay"))
            g0, g1 = lru_gate
            V.tensor_tensor(g0, lru_a[:, :, :], lru_a[:, :, :], ALU.mult).then_inc(*dve_core.up())
            v.wait_ge(*act_core.at("gates", 1, 1))
            V.tensor_tensor(g1, g1, conv[:, :, :], ALU.mult).then_inc(*dve_core.up())
            done()
            V.scalar_tensor_tensor(out=g0, in0=g0, scalar=1.0, in1=lru_b[:, :, :], op0=ALU.add, op1=ALU.mult
                                   ).then_inc(*dve_core.up("one_minus_a2"))
            rotate_da("k", 1)
            feature_out("q", lambda t: qT_da[:, :, t * P:(t + 1) * P])
            split_to(first[("ev_in", 2)] + 3)
            v.wait_ge(*act_core.at("root"))
            V.tensor_tensor(lru_b[:, :, :], g0, g1, ALU.mult).then_inc(*dve_core.up())
            done()
            for tile in range(4):
                V.tensor_tensor_scan(conv[:, tile, :], lru_a[:, tile, :], lru_b[:, tile, :], 0.0, ALU.mult, ALU.add
                                     ).then_inc(*dve_core.up())
            feature_out("k", lambda t: kT_da[:, :, t * P:(t + 1) * P])
            done()
            v.wait_ge(*dve_out.now())
            V.tensor_tensor(gateT[:, :, :], gateT[:, :, :], conv[:, :, :], ALU.mult
                            ).then_inc(*dve_core.up("b_out"))
            split_to(first[(("kv", 0), 1)] + 3)
            v.wait_ge(*act_hi.at("b_out"))
            V.tensor_tensor(xT_lo[:, 4:8, :], gateT[:, :, :], xT_hi[:, 4:8, :].bitcast(F32), ALU.subtract
                            ).then_inc(*dve_lo.up("b_out"))

            def masked(h):
                for m in range(2):
                    s = scores_sb(h, m)
                    k = 16 + 4 * (h % 2) + 2 * m
                    v.wait_ge(*pe_core.at("scores", h, m))
                    V.tensor_tensor(s, banks[2 * (h % 2) + m][:, 0:384], k_("mask"), ALU.add
                                    ).then_inc(*dve_core.up("masked", h, m))
                    done()
                    V.reduce_max(sm[:, 86:87], s[:, 0:P], AX_X).then_inc(*dve_core.up())
                    V.reduce_max(sm[:, 87:88], s[:, P:3 * P], AX_X).then_inc(*dve_core.up())
                    done()
                    V.tensor_scalar(sm[:, k:k + 2], sm[:, 86:88], -(DA_D ** -0.5), None, ALU.mult
                                    ).then_inc(*dve_core.up("max", h, m))
                    done()

            def combine(h):
                k = 24 + 4 * (h % 2)
                v.wait_ge(*act_core.at("exp", h, 1))
                if h >= 2:
                    v.wait_ge(*pe_turn.at("weights", h - 2))
                V.reciprocal(sm[:, k:k + 4], sm[:, k:k + 4]).then_inc(*dve_core.up())
                done()
                V.tensor_scalar(sm[:, k + 2:k + 4], sm[:, k + 2:k + 4], sm[:, 93:94], None, ALU.mult
                                ).then_inc(*dve_core.up())
                done()
                for t in range(TT):
                    c = slice(0, P) if t == 0 else slice(P, 3 * P)
                    s0, s1 = scores_sb(h, 0)[:, c], scores_sb(h, 1)[:, c]
                    V.tensor_scalar(s1, s1, sm[:, k + 2 + t:k + 3 + t], None, ALU.mult).then_inc(*dve_core.up())
                    done()
                    V.scalar_tensor_tensor(out=xrT_w(h)[:, c], in0=s0, scalar=sm[:, k + t:k + t + 1], in1=s1,
                                           op0=ALU.mult, op1=ALU.add).then_inc(*dve_core.up("weights", h))

            masked(0)
            masked(1)
            for h in range(DA_H):
                combine(h)
                done()
                if h + 2 < DA_H:
                    masked(h + 2)
            kv_turned(0, 1)
            split_to(first[("ev_out", 0)])
            v.wait_ge(*pe_core.at("o", DA_H - 1))
            o2 = lru_a[:, :, :].rearrange("p a b -> p (a b)").rearrange("p (t d) -> p t d", t=TT)
            sq = conv[:, :, :].rearrange("p a b -> p (a b)").rearrange("p (t d) -> p t d", t=TT)
            for t in range(TT):
                V.tensor_copy(o2[:, t, :], banks[4 + t][:, :]).then_inc(*dve_core.up("o_copy", t))
                done()
                V.tensor_tensor(sq[:, t, :], o2[:, t, :], o2[:, t, :], ALU.mult).then_inc(*dve_core.up())
                done()
                V.reduce_sum(sm[:, 36 + 4 * t:40 + 4 * t], sq[:, t, :].rearrange("p (h d) -> p h d", h=DA_H), AX_X
                             ).then_inc(*dve_core.up("rms", t))
            for t in range(TT):
                c = slice(44 + 4 * t, 48 + 4 * t)
                v.wait_ge(*act_core.at("rms", t))
                V.reciprocal(sm[:, c], sm[:, c]).then_inc(*dve_core.up())
                done()
                V.tensor_scalar(sm[:, c], sm[:, c], 1.0 - LAMBDA_INIT, None, ALU.mult).then_inc(*dve_core.up())
                done()
                for h in range(DA_H):
                    V.scalar_tensor_tensor(out=kT_da_flat(t)[:, h * P:(h + 1) * P], in0=o2[:, t, h * P:(h + 1) * P],
                                           scalar=sm[:, 44 + 4 * t + h:45 + 4 * t + h], in1=da_g[:, :],
                                           op0=ALU.mult, op1=ALU.mult).then_inc(*dve_core.up("a_out", t))
            for t in range(TT):
                split_operand("a_out", t, 0)

        def cross(l):
            split_to(first[(("xq", l), 1)] + 3)
            for c in range(2):
                feature_out(("xq", l, c), lambda t: q_x[:, 4 * c:4 * c + 4, t * P:(t + 1) * P])

            def maxima(h):
                v.wait_ge(*pe_core.at("xs", l, h))
                V.tensor_reduce(sm[:, 86:88], banks[h % 4][:, :].rearrange("p (t k) -> p t k", t=TT), AX_X, ALU.max
                                ).then_inc(*dve_core.up())
                done()
                k = 52 + 2 * (h % 2)
                V.tensor_scalar(sm[:, k:k + 2], sm[:, 86:88], -(XA_D ** -0.5), None, ALU.mult
                                ).then_inc(*dve_core.up("xmax", l, h))
                done()

            def normalise(h):
                k = 56 + 2 * (h % 2)
                v.wait_ge(*act_core.at("xp", l, h))
                V.reciprocal(sm[:, k:k + 2], sm[:, k:k + 2]).then_inc(*dve_core.up())
                done()
                for t in range(TT):
                    V.tensor_scalar(p_x[:, h % 2, t, :], p_x[:, h % 2, t, :], sm[:, k + t:k + t + 1], None, ALU.mult
                                    ).then_inc(*dve_core.up("xw", l, h))

            def out_lo(h):
                v.wait_ge(*act_hi.at("xo", l, h))
                V.tensor_tensor(xT_lo[:, 2 * h:2 * h + 2, :],
                                banks[GU[h % 2]][:, :].rearrange("p (k c) -> p k c", k=2),
                                xT_hi[:, 2 * h:2 * h + 2, :].bitcast(F32), ALU.subtract
                                ).then_inc(*dve_lo.up("xo", l, h))

            maxima(0)
            maxima(1)
            normalise(0)
            for h in range(XA_H):
                if h + 2 < XA_H:
                    maxima(h + 2)
                if h + 1 < XA_H:
                    normalise(h + 1)
                out_lo(h)
            split_to(first[(("xo", l), 0)] + 1)

        def s5_prepare():
            s = s5_par
            V.tensor_scalar(s(0), s(0), -1e-4, None, ALU.min).then_inc(*dve_core.up("s5_args"))
            v.wait_ge(*act_core.at("s5_step"))
            done()
            V.tensor_tensor(s(4), s(0), s(3), ALU.mult).then_inc(*dve_core.up())
            V.tensor_tensor(s(6), s(1), s(3), ALU.mult).then_inc(*dve_core.up())
            done()
            V.tensor_scalar(s(8), s(6), 1.0 / (2 * math.pi), 12582912.0, ALU.mult, ALU.add).then_inc(*dve_core.up())
            done()
            V.tensor_scalar(s(8), s(8), 12582912.0, None, ALU.subtract).then_inc(*dve_core.up())
            done()
            for part in (6.28125, 0.0019350051879882812, 3.0199159819500178e-07):
                V.scalar_tensor_tensor(out=s(6), in0=s(8), scalar=-part, in1=s(6), op0=ALU.mult, op1=ALU.add
                                       ).then_inc(*dve_core.up())
                done()
            V.tensor_scalar(s(6), s(6), 3.1415925, -3.1415925, ALU.min, ALU.max).then_inc(*dve_core.up("s5_angle"))
            v.wait_ge(*act_core.at("s5_sin"))
            V.tensor_tensor(s(7), s(7), s(7), ALU.mult).then_inc(*dve_core.up())
            done()
            cos, sin, mag = s(8), s(5), s(4)
            V.tensor_scalar(cos, s(7), -2.0, 1.0, ALU.mult, ALU.add).then_inc(*dve_core.up())
            done()
            V.tensor_copy(e_cos[:, :, 0], cos).then_inc(*dve_core.up())
            V.tensor_copy(e_sin[:, :, 0], sin).then_inc(*dve_core.up("theta"))
            nr, ni, lr, li = s(6), s(3), s(0), s(1)
            V.tensor_tensor(nr, mag, cos, ALU.mult).then_inc(*dve_core.up())
            V.tensor_tensor(ni, mag, sin, ALU.mult).then_inc(*dve_core.up())
            done()
            V.tensor_scalar(nr, nr, 1.0, None, ALU.subtract).then_inc(*dve_core.up())
            V.tensor_tensor(s(7), lr, lr, ALU.mult).then_inc(*dve_core.up())
            V.tensor_tensor(s(9), li, li, ALU.mult).then_inc(*dve_core.up())
            done()
            V.tensor_tensor(s(7), s(7), s(9), ALU.add).then_inc(*dve_core.up())
            done()
            V.reciprocal(s(7), s(7)).then_inc(*dve_core.up())
            V.tensor_tensor(s(9), nr, lr, ALU.mult).then_inc(*dve_core.up())
            V.tensor_tensor(s(10), ni, li, ALU.mult).then_inc(*dve_core.up())
            done()
            V.tensor_tensor(s(9), s(9), s(10), ALU.add).then_inc(*dve_core.up())
            done()
            V.tensor_tensor(s(9), s(9), s(7), ALU.mult).then_inc(*dve_core.up())
            V.tensor_tensor(s(10), ni, lr, ALU.mult).then_inc(*dve_core.up())
            V.tensor_tensor(s(11), nr, li, ALU.mult).then_inc(*dve_core.up())
            done()
            V.tensor_tensor(s(10), s(10), s(11), ALU.subtract).then_inc(*dve_core.up())
            done()
            V.tensor_tensor(s(10), s(10), s(7), ALU.mult).then_inc(*dve_core.up())
            done()
            v.wait_ge(loaded["s5"], 64)
            b = [qkT[:, ri, 0, :].rearrange("p (j c) -> p j c", c=16) for ri in range(2)]
            fr, fi = (s(n).unsqueeze(2).to_broadcast([P, 16, 16]) for n in (9, 10))
            flat = uT[:, :, :].rearrange("p a b -> p (a b)")
            bd = [flat[:, ri * 512:(ri + 1) * 512].rearrange("p (j c) -> p j c", c=32) for ri in range(2)]
            t1, t2 = (s5_cT[:, 0, 2 * a:2 * a + 2, :].rearrange("p a b -> p (a b)").rearrange(
                "p (j c) -> p j c", c=16) for a in range(2))
            V.memset(flat, 0.0).then_inc(*dve_core.up())
            for ri in range(2):
                V.tensor_tensor(t1, b[ri], fr, ALU.mult).then_inc(*dve_core.up())
                V.tensor_tensor(t2, b[1 - ri], fi, ALU.mult).then_inc(*dve_core.up())
                done()
                for g in range(2):
                    r = slice(64 * g, 64 * g + 64)
                    V.tensor_tensor(bd[ri][r, :, 16 * g:16 * g + 16], t1[r], t2[r],
                                    ALU.subtract if ri == 0 else ALU.add).then_inc(*dve_core.up("s5_b", ri))
                done()
            for ri in range(2):
                v.wait_ge(*pe_turn.at("s5_b", ri))
                V.tensor_copy(s5_bT[:, ri].rearrange("p a b -> p (a b)"), banks[TR[ri]][:, :]
                              ).then_inc(*dve_core.up("s5_bT", ri))
            for ri in range(2):
                c = qkT[:, ri, 1, :].rearrange("p (q n) -> p q n", n=64)
                cd = flat[:, ri * 512:(ri + 1) * 512].rearrange("p (q n) -> p q n", n=P)
                for g in range(2):
                    V.tensor_scalar(cd[:, :, 64 * g:64 * g + 64], c, k_("parity")[:, g:g + 1],
                                    1.0 if ri == 0 else -1.0, ALU.mult, ALU.mult
                                    ).then_inc(*dve_core.up("s5_c", ri))
            for ri in range(2):
                v.wait_ge(*pe_turn.at("s5_c", ri))
                V.tensor_copy(s5_cT[:, ri].rearrange("p a b -> p (a b)"), banks[TR[ri]][:, :]
                              ).then_inc(*dve_core.up("s5_cT", ri))

        def odd_mixer():
            split_to(first[("od_in", 1)] + 2)
            v.wait_ge(*pool_core.at("powers"))
            feature_out("u", lambda t: uT[:, :, t * P:(t + 1) * P])
            split_to(first[("od_in", 1)] + 3)
            rt = [w[:, :, :].rearrange("p a b -> p (a b)") for w in (act_h, hid)]
            for t in range(TT):
                v.wait_ge(*act_out.at("qk", t))
                done()
                data, ta, tb = (w.rearrange("p (a h d) -> p a h d", a=2, d=RET_D)
                                for w in (tk[:, 1, t, :], rt[0], rt[1]))
                cs, sn = (k_(n).rearrange("p (t h d) -> p t h d", t=TT, d=RET_D)[:, t] for n in ("ret_cos", "ret_sin"))
                lo, hi = slice(0, RET_D // 2), slice(RET_D // 2, RET_D)
                for a in range(2):
                    V.tensor_tensor(ta[:, a], data[:, a], cs, ALU.mult).then_inc(*dve_core.up())
                    V.tensor_tensor(tb[:, a, :, lo], data[:, a, :, hi], sn[:, :, lo], ALU.mult
                                    ).then_inc(*dve_core.up())
                    V.tensor_tensor(tb[:, a, :, hi], data[:, a, :, lo], sn[:, :, hi], ALU.mult
                                    ).then_inc(*dve_core.up())
                done()
                V.tensor_tensor(tk[:, 1, t, :], rt[0], rt[1], ALU.add).then_inc(*dve_core.up("qk", t))
            split_to(first[("od_in", 2)] + 3)
            feature_out("qk", lambda t: qkT[:, :, :, t * P:(t + 1) * P].rearrange("p a b c -> p (a b) c"))
            split_to(first[(("kv", 1), 3)] + 3)
            xp = tk[:, 0, 0, :].rearrange("p (r k) -> p r k", r=2)
            xc, xs = (tk[:, 1, t, :].rearrange("p (r k) -> p r k", r=2) for t in range(2))
            for j in range(S5_TILES):
                g = s5_g[:, j % 2]
                mag = s5_par(4)[:, j:j + 1]
                ec, es = e_cos[:, j, :], e_sin[:, j, :]
                ecb, esb = (e.unsqueeze(1).unsqueeze(1).to_broadcast([P, 2, 2, S5_CH]) for e in (ec, es))
                src = banks[j % 4][:, :].rearrange("p (r c k) -> p r c k", r=2, k=S5_CH)
                v.wait_ge(*pe_core.at("s5_x", j))
                V.tensor_tensor(xc.rearrange("p r (c k) -> p r c k", k=S5_CH), src, ecb, ALU.mult
                                ).then_inc(*dve_core.up())
                V.tensor_tensor(xs.rearrange("p r (c k) -> p r c k", k=S5_CH), src, esb, ALU.mult
                                ).then_inc(*dve_core.up("s5_in", j))
                done()
                V.tensor_tensor(xp[:, 0], xc[:, 0], xs[:, 1], ALU.add).then_inc(*dve_core.up())
                V.tensor_tensor(xp[:, 1], xc[:, 1], xs[:, 0], ALU.subtract).then_inc(*dve_core.up())
                done()
                if j == 0:
                    v.wait_ge(unit_done, first[(("kv", 1), 3)] + 2)
                if j >= 2:
                    v.wait_ge(*pool_core.at("s5_h", j - 2))
                decay = mag.to_broadcast([P, S5_CH])
                for r in range(2):
                    V.tensor_tensor_scan(g[:, r, 0:S5_CH], decay, xp[:, r, 0:S5_CH], 0.0, ALU.mult, ALU.add
                                         ).then_inc(*dve_core.up())
                done()
                last = slice(S5_CH - 1, S5_CH)
                V.tensor_tensor(sm[:, 86:87], g[:, 1, last], es[:, last], ALU.mult).then_inc(*dve_core.up())
                V.tensor_tensor(sm[:, 87:88], g[:, 1, last], ec[:, last], ALU.mult).then_inc(*dve_core.up())
                done()
                V.scalar_tensor_tensor(out=sm[:, 88:89], in0=g[:, 0, last], scalar=ec[:, last], in1=sm[:, 86:87],
                                       op0=ALU.mult, op1=ALU.subtract).then_inc(*dve_core.up())
                V.scalar_tensor_tensor(out=sm[:, 89:90], in0=g[:, 0, last], scalar=es[:, last], in1=sm[:, 87:88],
                                       op0=ALU.mult, op1=ALU.add).then_inc(*dve_core.up())
                done()
                for r in range(2):
                    V.tensor_tensor_scan(g[:, r, S5_CH:SEQ], decay, xp[:, r, S5_CH:SEQ], sm[:, 88 + r:89 + r],
                                         ALU.mult, ALU.add).then_inc(*dve_core.up("s5_g", j))
                done()
            v.wait_ge(*pe_core.at("s5_y", S5_TILES - 1))
            for q in range(4):
                V.scalar_tensor_tensor(out=s5_y[q // 2][:, q % 2, :], in0=uT[:, q, :], scalar=pv[:, q, 8:9],
                                       in1=banks[4 + q // 2][:, (q % 2) * SEQ:(q % 2 + 1) * SEQ],
                                       op0=ALU.mult, op1=ALU.add).then_inc(*dve_core.up("s5_out", q))
            v.wait_ge(*act_hi.at("z"))
            for a in range(2):
                V.tensor_tensor(xT_lo[:, 2 * a:2 * a + 2, :], s5_y[a], xT_hi[:, 2 * a:2 * a + 2, :].bitcast(F32),
                                ALU.subtract).then_inc(*dve_lo.up("z"))
            for h in range(RET_H):
                v.wait_ge(*pe_core.at("ret_s", h))
                if h >= 2:
                    v.wait_ge(*pe_core.at("ret_o", h - 2))
                dec = k_("decay").rearrange("p (h k) -> p h k", h=RET_H)[:, h]
                V.tensor_tensor(ret_w(h)[:, 0:SEQ], banks[h][:, 0:SEQ], dec, ALU.mult).then_inc(*dve_core.up())
                V.tensor_tensor(ret_w(h)[:, SEQ:SEQ + P], banks[h][:, SEQ:SEQ + P], dec[:, 0:P], ALU.mult
                                ).then_inc(*dve_core.up("ret_w", h))
            v.wait_ge(*act_core.at("glu", 3))
            for a in range(2):
                V.tensor_tensor(s5_y[a], s5_y[a], s5_t[:, a], ALU.mult).then_inc(*dve_core.up("c_out"))
            v.wait_ge(*act_hi.at("c_out"))
            for a in range(2):
                V.tensor_tensor(xT_lo[:, 2 * a:2 * a + 2, :], s5_y[a], xT_hi[:, 2 * a:2 * a + 2, :].bitcast(F32),
                                ALU.subtract).then_inc(*dve_lo.up("c_out"))
            split_to(first[("od_out", 0)] + 1)
            stat = s5_h[:, 0, 0, 0:64].rearrange("p (a b) -> p a b", b=8)
            agg = s5_h[:, 0, 0, 64:80].rearrange("p (a b) -> p a b", b=2)
            v.wait_ge(*pe_core.at("ret_o", RET_H - 1))
            for t in range(TT):
                for h in range(RET_H):
                    V.bn_stats(stat[:, 4 * t + h, 0:6], banks[4 + t][:, h * P:(h + 1) * P]).then_inc(*dve_core.up())
            done()
            for n in range(8):
                V.bn_aggr(agg[:, n, :], stat[:, n, 0:6]).then_inc(*dve_core.up("ret_var"))
            v.wait_ge(*act_core.at("ret_sd"))
            V.reciprocal(sm[:, 78:86], sm[:, 78:86]).then_inc(*dve_core.up())
            done()
            for t in range(TT):
                for h in range(RET_H):
                    n = 4 * t + h
                    V.tensor_scalar(osb[:, t, h * P:(h + 1) * P], banks[4 + t][:, h * P:(h + 1) * P], agg[:, n, 0:1],
                                    sm[:, 78 + n:79 + n], ALU.subtract, ALU.mult).then_inc(*dve_core.up("ret_n", t))
                V.tensor_tensor(ret_gate[:, t, :].rearrange("p (h d) -> p h d", h=RET_H),
                                ret_gate[:, t, :].rearrange("p (h d) -> p h d", h=RET_H),
                                ret_g[:, :].unsqueeze(1).to_broadcast([P, RET_H, P]), ALU.mult
                                ).then_inc(*dve_core.up())
                done()
                V.tensor_tensor(osb[:, t, :], osb[:, t, :], ret_gate[:, t, :], ALU.mult
                                ).then_inc(*dve_core.up("d_out", t))
            for t in range(TT):
                split_operand("d_out", t, 1)

        V.memset(zero[:, :], 0.0).then_inc(*zeroed.up())
        v.wait_ge(*zeroed.now())
        V.tensor_copy(zero_r[:, :], zero[:, :]).then_inc(*zeroed.up("zero"))
        V.memset(sm[:, 92:93], LN_EPS).then_inc(*dve_core.up())
        v.wait_ge(loaded["nat"], 16 * 9)
        for g in range(2):
            V.tensor_copy(nat[0:16, 768 + 64 * g:832 + 64 * g], sm[0:16, 90 + g:91 + g].to_broadcast([16, 64])
                          ).then_inc(*dve_core.up("log_step"))
        v.wait_ge(*pe_turn.at("params"))
        V.tensor_copy(pv[:, :, :], banks[0][:, 0:64].rearrange("p (a b) -> p a b", b=16)[:, :, 0:10]
                      ).then_inc(*dve_core.up())
        for n, at in ((0, 64), (1, 80), (3, 96)):
            V.tensor_copy(s5_par(n), banks[0][:, at:at + 16]).then_inc(*dve_core.up("params"))
        done()
        lam = pv[:, :, 7]
        nl, na, e4, z4, z2, pl = (sm[:, c:c + 4] for c in (60, 12, 8, 64, 68, 72))
        V.tensor_scalar(nl, lam, -1.0, None, ALU.mult).then_inc(*dve_core.up())
        done()
        V.tensor_tensor(na, nl, lam, ALU.min).then_inc(*dve_core.up("neg_abs"))
        v.wait_ge(*act_core.at("exp_lambda"))
        V.tensor_scalar(z4, e4, 2.0, None, ALU.add).then_inc(*dve_core.up())
        done()
        V.reciprocal(z4, z4).then_inc(*dve_core.up())
        done()
        V.tensor_tensor(z4, z4, e4, ALU.mult).then_inc(*dve_core.up())
        done()
        V.tensor_tensor(z2, z4, z4, ALU.mult).then_inc(*dve_core.up())
        V.memset(pl, 1.0 / 17).then_inc(*dve_core.up())
        for n in range(15, 0, -2):
            done()
            V.tensor_tensor(pl, pl, z2, ALU.mult).then_inc(*dve_core.up())
            done()
            V.tensor_scalar(pl, pl, 1.0 / n, None, ALU.add).then_inc(*dve_core.up())
        done()
        V.tensor_tensor(pl, pl, z4, ALU.mult).then_inc(*dve_core.up())
        V.tensor_scalar(nl, nl, 0.0, None, ALU.max).then_inc(*dve_core.up())
        done()
        V.scalar_tensor_tensor(out=nl, in0=pl, scalar=2.0, in1=nl, op0=ALU.mult, op1=ALU.add
                               ).then_inc(*dve_core.up())
        done()
        V.tensor_scalar(sm[:, 0:4], nl, LRU_C, None, ALU.mult).then_inc(*dve_core.up())
        V.tensor_scalar(sm[:, 4:8], nl, -LRU_C, None, ALU.mult).then_inc(*dve_core.up("softplus"))
        v.wait_ge(loaded["rows"], 48)
        dl = tk[:, 0, 0, 0:256].rearrange("p (a b d) -> p a b d", a=2, b=2)
        pr = tk[:, 0, 0, 256:384].rearrange("p (a d) -> p a d", a=2)
        V.tensor_tensor(pr, dl[:, :, 0, :], dl[:, :, 1, :], ALU.mult).then_inc(*dve_core.up())
        done()
        V.reduce_sum(sm[:, 34:36], pr, AX_X).then_inc(*dve_core.up("lambda_sum"))
        v.wait_ge(*act_core.at("da_exp"))
        V.tensor_scalar(sm[:, 93:94], sm[:, 33:34], LAMBDA_INIT, sm[:, 32:33], ALU.subtract, ALU.subtract
                        ).then_inc(*dve_core.up())

        def in_operand():
            for t in range(TT):
                for half in range(2):
                    split_operand("x_in", t, half)
            split_to(1)
            for t in range(TT):
                for half in range(2):
                    split_operand("mem", t, half, memT_hi, memT_lo)

        in_operand()
        ffn(0)
        norm(0, 0.5, ("acc", 0))
        even_mixer()
        norm(1, 1.0, ("ev_out", 1))
        cross(0)
        norm(2, 1.0, (("xo", 0), 1))
        s5_prepare()
        ffn(1)
        norm(3, 0.5, ("acc", 1))
        ffn(2)
        norm(4, 0.5, ("acc", 2))
        odd_mixer()
        norm(5, 1.0, ("od_out", 1))
        cross(1)
        norm(6, 1.0, (("xo", 1), 1))
        ffn(3)
        norm(7, 0.5, ("acc", 3), last=True)


INPUTS = ("x", "mem", "ln_g", "ln_b", "ffn_w_gate", "ffn_w_up", "ffn_w_down", "xa_w_q", "xa_w_kv", "xa_w_o",
          "ev_w_in", "ev_w_out", "da_lambda", "da_norm_g", "lru_conv_w", "lru_conv_b", "lru_gate_w", "lru_gate_b",
          "lru_lambda", "od_w_in", "od_w_out", "s5_lam_re", "s5_lam_im", "s5_log_step", "s5_b_re", "s5_b_im",
          "s5_c_re", "s5_c_im", "s5_d", "s5_glu_w", "s5_glu_b", "ret_norm_g")


def kernel(**inputs):
    import concourse.bacc as bacc
    from concourse.bass_utils import run_bass_kernel_spmd

    arrays = {f"in_{n}": np.ascontiguousarray(inputs[n]) for n in INPUTS}
    arrays["in_constants"] = constant_table()[1]

    def program(marks, final):
        nc = bacc.Bacc("TRN2", target_bir_lowering=False, num_devices=1)
        A = {n[3:]: nc.dram_tensor(n, a.shape, mybir.dt.from_np(a.dtype), kind="ExternalInput").ap()
             for n, a in arrays.items()}
        A["out"] = nc.dram_tensor("out", (1, SEQ, D), F32, kind="ExternalOutput").ap()
        build(nc, A, marks, final)
        return nc

    marks = {}
    program(marks, False)
    nc = program(marks, True)
    got = run_bass_kernel_spmd(nc, [arrays], core_ids=[0])
    return got.results[0]["out"]
```

```python
import math
from contextlib import ExitStack

import numpy as np
import concourse.bass as bass
from concourse import mybir

F32 = mybir.dt.float32
F32R = mybir.dt.float32r
ALU = mybir.AluOpType
ACT = mybir.ActivationFunctionType
AX_X = mybir.AxisListType.X

P = 128
SEQ = 256
TT = SEQ // P
D = 1024
KT = D // P
DEPTH = 2
D_FF = 2816
FB = 256
NB = D_FF // FB
HALF = D // 2
UW = 2048
NSLOT = 3
FFN_UNITS = 3 * NB
ALPHA = (2 * DEPTH) ** 0.25
LN_EPS = 1e-5
LRU_C = 8.0
DA_H, DA_D, DA_ROPE, DA_THETA = 4, 64, 16, 500000.0
RET_H, RET_D, RET_THETA = 4, 64, 10000.0
XA_H, XA_D = 4, 256
S5_TILES = 16
S5_CH = 128
LAMBDA_INIT = 0.8 - 0.6 * math.exp(-0.3 * 0)
NORMS = 4 * DEPTH


class Steps:

    def __init__(self, name, sem, marks, final):
        self.name, self.sem, self.marks, self.final, self.n = name, sem, marks, final, 0

    def up(self, *step):
        self.n += 1
        if step:
            self.marks[(self.name, *step)] = self.n
        return self.sem, 1

    def now(self):
        return self.sem, self.n

    def at(self, *step):
        if self.final:
            return self.sem, self.marks[(self.name, *step)]
        return self.sem, 1


def constant_table():
    p = np.arange(P)
    parts = {"ident": np.eye(P)}
    tri = np.where(p[None, :] <= p[:, None], 0.0, -1e30)
    parts["mask"] = np.concatenate([tri, np.zeros((P, P)), tri], 1)

    def rope(rot, theta, heads):
        half = rot // 2
        inv = np.float32(theta) ** (-np.arange(half, dtype=np.float32) * np.float32(2.0 / rot))
        ang = np.arange(SEQ, dtype=np.float32)[:, None] * inv[None, :].astype(np.float32)
        c, s = np.cos(ang), np.sin(ang)
        c = np.tile(np.concatenate([c, c], 1), (1, heads)).reshape(TT, P, -1).transpose(1, 0, 2)
        s = np.tile(np.concatenate([-s, s], 1), (1, heads)).reshape(TT, P, -1).transpose(1, 0, 2)
        return c.reshape(P, -1), s.reshape(P, -1)

    parts["da_cos"], parts["da_sin"] = rope(DA_ROPE, DA_THETA, 2 * DA_H)
    parts["ret_cos"], parts["ret_sin"] = rope(RET_D, RET_THETA, RET_H)
    gamma = 1.0 - np.exp2(-5.0 - np.arange(RET_H))
    lag = np.arange(SEQ)[None, :] - p[:, None]
    decay = np.where(lag >= 0, np.exp(np.log(gamma)[:, None, None] * np.maximum(lag, 0)), 0.0)
    parts["decay"] = (decay * RET_D ** -0.5).transpose(1, 0, 2).reshape(P, -1)
    parity = (p // 16) % 2
    parts["parity"] = np.stack([parity == 0, parity == 1], 1)
    at, where, cols = 0, {}, []
    for name, a in parts.items():
        where[name] = (at, a.shape[1])
        at += a.shape[1]
        cols.append(np.asarray(a, np.float32))
    return where, np.ascontiguousarray(np.concatenate(cols, 1))


def unit_table():
    first, u = {}, 0

    def phase(key, n):
        nonlocal u
        first[key] = u
        u += n

    def blocks(kind, cols):
        for c in cols:
            phase((kind, c), 2)

    phase(("ffn", 0), FFN_UNITS)
    blocks(("kv", 0), [0])
    blocks("ev_in", [4, 3, 0, 1, 2])
    blocks(("kv", 0), [1, 2])
    blocks("ev_out", [0, 1])
    blocks(("kv", 0), [3])
    blocks(("xq", 0), [0, 1])
    blocks(("xo", 0), [0, 1])
    blocks(("kv", 1), [0])
    phase(("ffn", 1), FFN_UNITS)
    blocks(("kv", 1), [1])
    phase(("ffn", 2), FFN_UNITS)
    blocks(("kv", 1), [2])
    blocks("od_in", [0, 1])
    blocks(("kv", 1), [3])
    blocks("od_in", [2, 3])
    phase("glu", 1)
    blocks("od_out", [0, 1])
    blocks(("xq", 1), [0, 1])
    blocks(("xo", 1), [0, 1])
    phase(("ffn", 3), FFN_UNITS)
    return first, u


def build(nc, A, marks, final):
    ctx = ExitStack()
    with ctx:
        write_program(nc, ctx, A, marks, final)


def write_program(nc, ctx, A, marks, final):
    def sb(name, shape, dt=F32, to=ctx):
        return to.enter_context(nc.sbuf_tensor(name, shape, dt))

    def sem(name):
        return ctx.enter_context(nc.semaphore(name))

    def steps(name):
        return Steps(name, sem(name), marks, final)

    first, n_units = unit_table()
    where, _ = constant_table()
    n_const = sum(n for _, n in where.values())

    raw = sb("raw", [P, NSLOT, UW])
    w_hi = sb("w_hi", [P, NSLOT, UW], F32R)
    w_lo = sb("w_lo", [P, NSLOT, UW], F32R)
    x = sb("x", [P, TT, D])
    ax = sb("ax", [P, TT, D])
    xT_hi = sb("xT_hi", [P, KT, SEQ], F32R)
    xT_lo = sb("xT_lo", [P, KT, SEQ], F32R)
    zero_r = sb("zero_r", [P, P], F32R)
    k_mem = sb("k_mem", [P, KT, SEQ])
    v_mem = sb("v_mem", [P, TT, D])
    gb = sb("gb", [P, 2, D])
    const = sb("const", [P, n_const])
    act_h = sb("act_h", [P, TT, FB])
    hid = sb("hid", [P, TT, FB])
    hT_hi = sb("hT_hi", [P, 2, SEQ], F32R)
    hT_lo = sb("hT_lo", [P, 2, SEQ], F32R)
    tk = sb("tk", [P, 2, TT, HALF])
    pv = sb("pv", [P, 4, 10])
    da_g = sb("da_g", [P, 2 * DA_D])
    ret_g = sb("ret_g", [P, P])
    sm = sb("sm", [P, 96])
    bn = sb("bn", [P, TT, 12])
    mv = sb("mv", [P, TT, 4])
    nat = tk[0:16, 1, :, :].rearrange("p a b -> p (a b)")[:, 0:896]

    s5_small = sb("s5_small", [P, 12, S5_TILES])
    rot_tmp = v_mem[:, 0, 0:2 * P].rearrange("p (a b) -> p a b", a=2)

    zero = rot_tmp[:, 0, :]

    def s5_par(n):
        return s5_small[:, n, :]

    memory = ExitStack()
    memT_hi = sb("memT_hi", [P, KT, SEQ], F32R, memory)
    memT_lo = sb("memT_lo", [P, KT, SEQ], F32R, memory)
    with ExitStack() as own:
        xrT = sb("xrT", [P, 4, SEQ + 3], F32, own)
        conv = sb("conv", [P, 4, SEQ], F32, own)
        lru_a = sb("lru_a", [P, 4, SEQ], F32, own)
        lru_b = sb("lru_b", [P, 4, SEQ], F32, own)
        gateT = sb("gateT", [P, 4, SEQ], F32, own)
        kT_da = sb("kT_da", [P, DA_H, SEQ], F32, own)
    qT_da = k_mem[:, 4:8, :]
    v_da = v_mem[:, :, HALF:D]
    with ExitStack() as own:
        q_x = sb("q_x", [P, KT, SEQ], F32, own)
        p_x = sb("p_x", [P, 2, TT, SEQ], F32, own)
        pT_x = sb("pT_x", [P, 2, TT, SEQ], F32, own)
    with ExitStack() as own:
        e_cos = sb("e_cos", [P, S5_TILES, S5_CH], F32, own)
        e_sin = sb("e_sin", [P, S5_TILES, S5_CH], F32, own)
        s5_bT = sb("s5_bT", [P, 2, 4, P], F32, own)
        s5_cT = sb("s5_cT", [P, 2, 4, P], F32, own)
        uT = sb("uT", [P, 4, SEQ], F32, own)
        qkT = sb("qkT", [P, 2, 2, SEQ], F32, own)
    memory.close()
    with ExitStack() as own:
        s5_g = sb("s5_g", [P, 2, 2, SEQ], F32, own)
        s5_t = sb("s5_t", [P, 2, 2, SEQ], F32, own)
        s5_h = sb("s5_h", [P, 2, 2, SEQ], F32, own)
        osb = sb("osb", [P, TT, HALF], F32, own)

    gw = act_h[:, :, :].rearrange("p a b -> p (a b)"), hid[:, :, :].rearrange("p a b -> p (a b)")
    gw = [g.rearrange("p (t c) -> p t c", t=4) for g in gw]

    def k_(name):
        a, n = where[name]
        return const[:, a:a + n]

    ident = k_("ident")
    banks = [ctx.enter_context(nc.psum_tensor(f"bank{i}", [P, 512], F32)) for i in range(8)]
    ACC, GU, TR = (0, 2), (4, 5), (6, 7)
    S5_IN = (2, 3, 6, 7)
    XT = ((6, 7), (0, 1))

    raw_in = [sem(f"raw_in{s}") for s in range(NSLOT)]
    hi_done, lo_done, unit_done = sem("hi_done"), sem("lo_done"), sem("unit_done")
    gu_full, silu_done, h_done = sem("gu_full"), sem("silu_done"), sem("h_done")
    h_turned, h_hi, h_lo = sem("h_turned"), sem("h_hi"), sem("h_lo")
    loaded = {n: sem(f"in_{n}") for n in ("const", "x", "mem", "nat", "rows", "gates", "gb", "x1", "tables", "s5")}
    zeroed = steps("zeroed")
    gate_zero = steps("gate_zero")
    pe_half = steps("pe_half")
    pe_turn = steps("pe_turn")
    pe_core = steps("pe_core")
    act_ln = steps("act_ln")
    act_out = steps("act_out")
    act_hi = steps("act_hi")
    act_core = steps("act_core")
    dve_ln = steps("dve_ln")
    dve_out = steps("dve_out")
    dve_lo = steps("dve_lo")
    dve_core = steps("dve_core")
    pool_core = steps("pool_core")
    out_done = sem("out_done")

    def w3(ring, u, k):
        return ring[:, u % NSLOT, :].rearrange("p (k c) -> p k c", k=k)

    kv_of_norm = {0: (0, 0), 1: (0, 3), 2: (1, 0), 3: (1, 1), 4: (1, 2)}
    norm_units = {
        0: first[("ffn", 0)] + FFN_UNITS - 1, 1: first[("ev_out", 1)] + 1,
        2: first[(("xo", 0), 1)] + 1, 3: first[("ffn", 1)] + FFN_UNITS - 1,
        4: first[("ffn", 2)] + FFN_UNITS - 1, 5: first[("od_out", 1)] + 1,
        6: first[(("xo", 1), 1)] + 1, 7: first[("ffn", 3)] + FFN_UNITS - 1}


    def xrT_w(h):
        return xrT[:, :, :].rearrange("p a b -> p (a b)")[:, (h % 2) * 384:(h % 2) * 384 + 384]

    def wT(h):
        return lru_b[:, :, :].rearrange("p a b -> p (a b)")[:, (h % 2) * 384:(h % 2) * 384 + 384]

    def kT_da_flat(t):
        return kT_da[:, 2 * t:2 * t + 2, :].rearrange("p a b -> p (a b)")

    def scores_sb(h, m):
        return x[:, 0, :].rearrange("p d -> p d")[:, 0:768][:, m * 384:(m + 1) * 384] if h % 2 == 0 else \
            x[:, 1, 0:768][:, m * 384:(m + 1) * 384]

    def ret_w(h):
        return s5_g[:, h % 2, :, :].rearrange("p r k -> p (r k)")[:, 0:384]

    s5_neg_c = osb[:, 0, :].rearrange("p (q c) -> p q c", q=4)
    s5_blocks = (uT[:, :, :].rearrange("p a b -> p (a b)"),
                 e_sin[:, :, :].rearrange("p a b -> p (a b)")[:, 0:1024])
    lru_gate = [x[:, g, :].rearrange("p (t k) -> p t k", t=4) for g in range(2)]
    ret_v = x[:, 0, :].rearrange("p (t d) -> p t d", t=TT)
    ret_gate = x[:, 1, :].rearrange("p (t d) -> p t d", t=TT)
    s5_y = [act_h[:, :, :], hid[:, :, :]]

    def end_of(key, t):
        name, u = key
        return pe_half.at(*name) if t == 0 else (unit_done, u + 2)

    block = ctx.enter_context(nc.Block())

    @block.sync
    def _(sp):
        sp.dma_start(ident, A["constants"][:, 0:P]).then_inc(loaded["const"], 16)
        sp.dma_start(x[:, 0, :], A["x"][0, 0:P, :]).then_inc(loaded["x"], 16)

        def room(u):
            if u >= NSLOT:
                sp.wait_ge(lo_done, u - NSLOT + 1)

        def columns(w, u):
            for half in range(2):
                room(u + half)
                for j in range(2):
                    r0 = half * HALF + j * 256
                    sp.dma_start(w3(raw, u + half, 4)[:, 2 * j:2 * j + 2, :],
                                 w[r0:r0 + 256, :].rearrange("(k p) c -> p k c", p=P)
                                 ).then_inc(raw_in[(u + half) % NSLOT], 16)

        def gate_up(wg, wu, u, b, wait):
            for half in range(2):
                if wait is not None:
                    sp.wait_ge(lo_done, wait + half)
                for j, w in enumerate((wg, wu)):
                    sp.dma_start(w3(raw, u + half, 4)[:, :, j * FB:(j + 1) * FB], w[b, half]
                                 ).then_inc(raw_in[(u + half) % NSLOT], 16)

        def down(wd, u, b, wait):
            sp.wait_ge(lo_done, wait)
            for j in range(2):
                sp.dma_start(w3(raw, u, 2)[:, j, :], wd[b, j]).then_inc(raw_in[u % NSLOT], 16)

        def ffn(f):
            l, j = f // 2, f % 2
            wg, wu = (A[n][l, j].rearrange("(h k p) (b c) -> b h p k c", p=P, k=4, c=FB)
                      for n in ("ffn_w_gate", "ffn_w_up"))
            wd = A["ffn_w_down"][l, j].rearrange("(b k p) c -> b k p c", p=P, k=2)
            u = first[("ffn", f)]
            gate_up(wg, wu, u, 0, u - NSLOT + 1 if u else None)
            with sp.Fori(0, NB - 1) as i:
                for half in range(2):
                    if u or half:
                        sp.wait_ge(lo_done, i * 3 + (u + 2 + half - NSLOT + 1))
                    else:
                        sp.wait_ge(lo_done, i * 3 + 1)
                    for q, w in enumerate((wg, wu)):
                        sp.dma_start(w3(raw, u + 2 + half, 4)[:, :, q * FB:(q + 1) * FB], w[i + 1, half]
                                     ).then_inc(raw_in[(u + 2 + half) % NSLOT], 16)
                down(wd, u + 4, i, i * 3 + (u + 4 - NSLOT + 1))
            down(wd, u + FFN_UNITS - 1, NB - 1, u + FFN_UNITS - NSLOT)

        def cols_of(name, l, c):
            return A[name][l][:, c * 512:(c + 1) * 512]

        def kv(l, c):
            columns(cols_of("xa_w_kv", l, c), first[(("kv", l), c)])

        def cross(l):
            for kind, name in (("xq", "xa_w_q"), ("xo", "xa_w_o")):
                for c in range(2):
                    columns(cols_of(name, l, c), first[((kind, l), c)])

        ffn(0)
        kv(0, 0)
        for c in (4, 3, 0, 1, 2):
            columns(cols_of("ev_w_in", 0, c), first[("ev_in", c)])
        kv(0, 1)
        kv(0, 2)
        for c in range(2):
            columns(cols_of("ev_w_out", 0, c), first[("ev_out", c)])
        kv(0, 3)
        cross(0)
        kv(1, 0)
        ffn(1)
        kv(1, 1)
        ffn(2)
        kv(1, 2)
        for c in range(2):
            columns(cols_of("od_w_in", 0, c), first[("od_in", c)])
        kv(1, 3)
        for c in range(2, 4):
            columns(cols_of("od_w_in", 0, c), first[("od_in", c)])
        u = first["glu"]
        room(u)
        for j in range(2):
            sp.dma_start(w3(raw, u, 4)[:, 2 * j:2 * j + 2, :],
                         A["s5_glu_w"][0][j * 256:(j + 1) * 256, :].rearrange("(k p) c -> p k c", p=P)
                         ).then_inc(raw_in[u % NSLOT], 16)
        for c in range(2):
            columns(cols_of("od_w_out", 0, c), first[("od_out", c)])
        cross(1)
        ffn(3)
        for t in range(TT):
            sp.wait_ge(*dve_ln.at("x", NORMS - 1, t))
            sp.dma_start(A["out"][0, t * P:(t + 1) * P, :], x[:, t, :]).then_inc(out_done, 16)
        sp.wait_ge(out_done, 16 * TT)

    @block.gpsimd
    def _(pool):
        with nc.allow_non_contiguous_dma(reason="rows of parameters"):
            rows = [A["lru_conv_w"][0], A["lru_conv_b"], A["lru_gate_b"][0], A["lru_lambda"], A["s5_d"],
                    A["s5_glu_b"]]
            r = 0
            for a in rows:
                n = a.shape[0]
                pool.dma_start(nat[r:r + n, 0:512], a).then_inc(loaded["nat"], 16)
                r += n
            pool.dma_start(nat[0:16, 512:640], A["s5_lam_re"][0].rearrange("(j g) n -> j (g n)", g=2)
                           ).then_inc(loaded["nat"], 16)
            pool.dma_start(nat[0:16, 640:768], A["s5_lam_im"][0].rearrange("(j g) n -> j (g n)", g=2)
                           ).then_inc(loaded["nat"], 16)
            pool.dma_start(sm[0:16, 90:92], A["s5_log_step"][0].rearrange("(j g) -> j g", g=2)
                           ).then_inc(loaded["nat"], 16)
            pool.dma_start(da_g[:, :], A["da_norm_g"].partition_broadcast(P).rearrange("p a d -> p (a d)")
                           ).then_inc(loaded["rows"], 16)
            pool.dma_start(ret_g[:, :], A["ret_norm_g"].partition_broadcast(P).rearrange("p a d -> p (a d)")
                           ).then_inc(loaded["rows"], 16)
            pool.dma_start(tk[:, 0, 0, 0:256], A["da_lambda"].partition_broadcast(P)
                           .rearrange("p a b d -> p (a b d)")).then_inc(loaded["rows"], 16)

        def norm_rows(i):
            l, j = i // 4, i % 4
            pool.dma_start(gb[:, 0, :], A["ln_g"][l, j].partition_broadcast(P)).then_inc(loaded["gb"], 16)
            pool.dma_start(gb[:, 1, :], A["ln_b"][l, j].partition_broadcast(P)).then_inc(loaded["gb"], 16)

        pool.dma_start(ax[:, :, :], A["mem"][0].rearrange("(t p) d -> p t d", p=P)).then_inc(loaded["mem"], 16)
        norm_rows(0)
        pool.dma_start(const[:, P:n_const], A["constants"][:, P:n_const]).then_inc(loaded["tables"], 16)
        for i in range(NORMS - 1):
            for t in range(TT):
                pool.wait_ge(*dve_ln.at("x", i, t))
            norm_rows(i + 1)
            if i == 0:
                for g in range(2):
                    pool.memset(gw[g], 0.0).then_inc(*gate_zero.up())
                pool.wait_ge(*gate_zero.now())
                with nc.allow_non_contiguous_dma(reason="64-float rows"):
                    for g in range(2):
                        for b in range(2):
                            src = A["lru_gate_w"][0, g].rearrange("(t b) c d -> b c t d", b=2)[b]
                            pool.dma_start(gw[g][64 * b:64 * b + 64, :, 64 * b:64 * b + 64], src
                                           ).then_inc(loaded["gates"], 16)
            if i == 2:
                with nc.allow_non_contiguous_dma(reason="16-float rows"):
                    for ri, n in enumerate(("s5_b_re", "s5_b_im")):
                        pool.dma_start(qkT[:, ri, 0, :].rearrange("p (j c) -> p j c", c=16),
                                       A[n][0].rearrange("(j g) n c -> (g n) j c", g=2)).then_inc(loaded["s5"], 16)
                    for ri, n in enumerate(("s5_c_re", "s5_c_im")):
                        pool.dma_start(qkT[:, ri, 1, :].rearrange("p (q n) -> p q n", n=64),
                                       A[n][0].rearrange("(q g) c n -> (g c) q n", g=8)).then_inc(loaded["s5"], 16)
            if i == 3:
                pool.wait_ge(*dve_core.at("theta"))
                pool.wait_ge(*pe_turn.at("s5_c", 1))
                n = 1
                while n < S5_CH:
                    sc = uT[:, :, :].rearrange("p a b -> p (a b)")[:, 0:16 * n].rearrange("p (j k) -> p j k", k=n)
                    ss = qkT[:, :, :, :].rearrange("p a b c -> p (a b c)")[:, 0:16 * n].rearrange(
                        "p (j k) -> p j k", k=n)
                    cl = e_cos[:, :, n - 1:n].to_broadcast([P, 16, n])
                    sl = e_sin[:, :, n - 1:n].to_broadcast([P, 16, n])
                    c0, s0 = e_cos[:, :, 0:n], e_sin[:, :, 0:n]
                    c1, s1 = e_cos[:, :, n:2 * n], e_sin[:, :, n:2 * n]
                    for a, b, c, d, out, op in ((c0, cl, s0, sl, c1, ALU.subtract), (s0, cl, c0, sl, s1, ALU.add)):
                        pool.tensor_tensor(sc, a, b, ALU.mult).then_inc(*pool_core.up())
                        pool.tensor_tensor(ss, c, d, ALU.mult).then_inc(*pool_core.up())
                        pool.wait_ge(*pool_core.now())
                        pool.tensor_tensor(out, sc, ss, op).then_inc(*pool_core.up("powers"))
                        pool.wait_ge(*pool_core.now())
                    n *= 2
            if i == 4:
                for j in range(S5_TILES):
                    pool.wait_ge(*dve_core.at("s5_g", j))
                    if j >= 2:
                        pool.wait_ge(*pe_core.at("s5_y", j - 2))
                    g = s5_g[:, j % 2]
                    for e, out in ((e_cos, s5_h), (e_sin, s5_t)):
                        pool.tensor_tensor(out[:, j % 2].rearrange("p r (c k) -> p r c k", k=S5_CH),
                                           g.rearrange("p r (c k) -> p r c k", k=S5_CH),
                                           e[:, j, :].unsqueeze(1).unsqueeze(1).to_broadcast([P, 2, 2, S5_CH]),
                                           ALU.mult).then_inc(*pool_core.up("s5_h", j))

    @block.tensor
    def _(pe):
        emptied = {}

        def take(b):
            for who, step in emptied.pop(b, ()):
                pe.wait_ge(*who.at(*step))

        def three(out, lh, ll, rh, rl, start, stop):
            pe.matmul(out, lh, rh, start=start, stop=False)
            pe.matmul(out, lh, rl, start=False, stop=False)
            return pe.matmul(out, ll, rh, start=False, stop=stop)

        def column_part(u, t, half, sh, sl, dst, key, need=None, steps_k=range(4)):
            if t == 0:
                pe.wait_ge(lo_done, u + 1)
            if need:
                for who, step in need(t, half):
                    pe.wait_ge(*who.at(*step))
            wh, wl = w3(w_hi, u, 4), w3(w_lo, u, 4)
            for k in steps_k:
                kk = 4 * half + k
                mm = three(banks[dst[t]][:, :], sh[:, kk, t * P:(t + 1) * P], sl[:, kk, t * P:(t + 1) * P],
                           wh[:, k, :], wl[:, k, :], kk == 0, kk == KT - 1)
            if 3 not in steps_k:
                return
            if t == 1:
                mm.then_inc(unit_done, 1)
            elif half == 1:
                mm.then_inc(*pe_half.up(*key))

        def column_block(key, u, sh, sl, dst, readers=None, need=None, between=None):
            for t in range(TT):
                take(dst[t])
                for half in range(2):
                    column_part(u + half, t, half, sh, sl, dst, key, need)
                if t == 0 and between:
                    between()
            if readers:
                for t in range(TT):
                    emptied[dst[t]] = [(who, (*step, t)) for who, step in readers]

        def gate_up_part(u, t, half):
            wh, wl = w3(w_hi, u + half, 4), w3(w_lo, u + half, 4)
            for k in range(4):
                kk = 4 * half + k
                mm = three(banks[GU[t]][:, :], xT_hi[:, kk, t * P:(t + 1) * P], xT_lo[:, kk, t * P:(t + 1) * P],
                           wh[:, k, :], wl[:, k, :], kk == 0, kk == KT - 1)
            if t == 1:
                mm.then_inc(unit_done, 1)
            elif half == 1:
                mm.then_inc(gu_full, 1)

        def gate_up_first(u, free, need, between):
            for t in range(TT):
                if free is not None:
                    pe.wait_ge(h_done, free + t)
                for half in range(2):
                    if t == 0:
                        pe.wait_ge(lo_done, u + half + 1)
                    for who, step in need(t, half):
                        pe.wait_ge(*who.at(*step))
                    gate_up_part(u, t, half)
                if t == 0 and between:
                    between()

        def gate_up_block(u, split, free):
            for half in range(2):
                pe.wait_ge(lo_done, split + half)
                for t in range(TT):
                    if half == 0:
                        pe.wait_ge(h_done, free + t)
                    gate_up_part(u, t, half)

        def down_part(u, t, hi, lo, last=False):
            wh, wl = w3(w_hi, u, 2), w3(w_lo, u, 2)
            for c in range(2):
                for k in range(2):
                    mm = three(banks[ACC[t] + c][:, :], hi[:, k, t * P:(t + 1) * P], lo[:, k, t * P:(t + 1) * P],
                               wh[:, k, c * 512:(c + 1) * 512], wl[:, k, c * 512:(c + 1) * 512], False,
                               last and k == 1)
            return mm

        def turn_hidden(t, ready, free):
            pe.wait_ge(h_done, ready + t)
            if free is not None:
                pe.wait_ge(h_lo, free + t)
            for k in range(2):
                mm = pe.transpose(banks[TR[t]][:, k * P:(k + 1) * P], hid[:, t, k * P:(k + 1) * P], ident)
            mm.then_inc(h_turned, 1)

        def ffn(f, need, between=None, interlude=None):
            u, n = first[("ffn", f)], 2 * NB * f
            for b in GU:
                take(b)
            gate_up_first(u, n - 1 if f else None, need, between)
            if interlude:
                interlude()
            for t in range(TT):
                take(TR[t])
                turn_hidden(t, n + 1, n - 1 if f else None)
            for c in range(2):
                for t in range(TT):
                    take(ACC[t] + c)
                    pe.matmul(banks[ACC[t] + c][:, :], zero_r[:, :], xT_hi[:, 0:2, :], start=True, stop=False)
            with pe.Fori(0, NB - 2) as i:
                gate_up_block(u + 2, i * 3 + (u + 3), i * 2 + (n + 1))
                pe.wait_ge(lo_done, i * 3 + (u + 5))
                pe.wait_ge(h_lo, i * 2 + (n + 2))
                for t in range(TT):
                    mm = down_part(u + 4, t, hT_hi, hT_lo)
                mm.then_inc(unit_done, 1)
                for t in range(TT):
                    turn_hidden(t, i * 2 + (n + 3), i * 2 + (n + 1))
            b = NB - 1
            d0, d1 = u + 3 * NB - 2, u + 3 * NB - 1
            gate_up_block(u + 3 * b - 1, u + 3 * b, n + 2 * b - 1)
            turn_hidden(0, n + 2 * b + 1, n + 2 * b - 1)
            pe.wait_ge(lo_done, d0 + 1)
            pe.wait_ge(h_lo, n + 2 * b)
            down_part(d0, 0, hT_hi, hT_lo)
            turn_hidden(1, n + 2 * b + 1, n + 2 * b - 1)
            pe.wait_ge(lo_done, d1 + 1)
            pe.wait_ge(h_lo, n + 2 * b + 1)
            down_part(d1, 0, xT_hi, xT_lo, True).then_inc(*pe_half.up("acc", f))
            down_part(d0, 1, hT_hi, hT_lo).then_inc(unit_done, 1)
            pe.wait_ge(h_lo, n + 2 * b + 2)
            down_part(d1, 1, xT_hi, xT_lo, True).then_inc(unit_done, 1)

        def turn(name, src, ready, bank, reader, n=4):
            for who, step in ready:
                pe.wait_ge(*who.at(*step))
            take(bank)
            for j in range(n):
                mm = pe.transpose(banks[bank][:, j * P:(j + 1) * P], src[:, j * P:(j + 1) * P], ident)
            mm.then_inc(*pe_turn.up(*name))
            emptied[bank] = reader

        def turn_split(name, t, half, src, ready):
            turn((name, t, half), src, ready, XT[t][half], [(dve_lo, (name, t, half))])

        def turn_out(name, src, who=act_out):
            for t in range(TT):
                turn((name, t), src[:, t, :], [(who, (name, t))], TR[t], [(dve_out, (name, t))])

        def kv_block(l, c, dst=GU, between=None):
            name = ("kv", l, c)
            column_block(name, first[(("kv", l), c)], memT_hi, memT_lo, dst, [(act_out, (name,))],
                         lambda t, half: [(dve_lo, ("mem", t, half))], between)

        def turn_x(i, t):
            for half in range(2):
                turn_split(("x", i), t, half, x[:, t, half * HALF:(half + 1) * HALF], [(dve_ln, ("x", i, t))])

        def norm(i):
            for t in range(TT):
                for c in range(2):
                    emptied[ACC[t] + c] = [(dve_ln, ("sum", i, t, c))]
            kv = kv_of_norm.get(i)
            if not kv:
                turn_x(i, 0)
                return lambda: turn_x(i, 1)
            kv_block(*kv, between=lambda: turn_x(i, 0))
            turn_x(i, 1)
            return (lambda: turn_out(("kv", *kv), tk[:, kv[1] % 2])) if kv[1] < 2 else None

        def x_ready(i):
            return lambda t, half: [(dve_lo, (("x", i), t, half))]

        def out_blocks(kind, need):
            for c in range(2):
                column_block((kind, c), first[(kind, c)], xT_hi, xT_lo, (ACC[0] + c, ACC[1] + c), need=need)

        def even_mixer(need, between):
            nm = {4: "xr", 3: "gate", 0: "q", 1: "k", 2: "v"}

            def project(c, dst, **first_one):
                column_block(("ev", c), first[("ev_in", c)], xT_hi, xT_lo, dst, [(act_out, (nm[c],))], **first_one)

            project(4, (4, 5), need=need, between=between)
            project(3, (0, 1))
            turn_out("xr", tk[:, 0])
            project(0, (2, 3))
            pe.wait_ge(loaded["gates"], 64)
            pe.wait_ge(*dve_core.at("conv"))
            for g in range(2):
                for t2 in range(2):
                    take(TR[t2])
                    for j in range(2):
                        tile = 2 * t2 + j
                        mm = pe.matmul(banks[TR[t2]][:, j * SEQ:(j + 1) * SEQ], gw[g][:, tile, :],
                                       conv[:, tile, :], start=True, stop=True)
                    mm.then_inc(*pe_core.up("gates", g, t2))
                    emptied[TR[t2]] = [(act_core, ("gates", g, t2))]
            turn_out("gate", tk[:, 1])
            project(1, (4, 5))
            turn_out("q", tk[:, 0], dve_core)
            project(2, (0, 1))
            turn_out("k", tk[:, 1], dve_core)
            kv_block(0, 1)

            def scores(h):
                for m in range(2):
                    b = 2 * (h % 2) + m
                    take(b)
                    r = slice(64 * m, 64 * m + 64)
                    pe.matmul(banks[b][:, 0:P], qT_da[r, h, 0:P], kT_da[r, h, 0:P], start=True, stop=True)
                    pe.matmul(banks[b][:, P:3 * P], qT_da[r, h, P:SEQ], kT_da[r, h, :], start=True, stop=True
                              ).then_inc(*pe_core.up("scores", h, m))
                    emptied[b] = [(dve_core, ("masked", h, m))]

            def weights(h):
                b = TR[h % 2]
                pe.wait_ge(*dve_core.at("weights", h))
                take(b)
                for j in range(3):
                    mm = pe.transpose(banks[b][:, j * P:(j + 1) * P], xrT_w(h)[:, j * P:(j + 1) * P], ident)
                mm.then_inc(*pe_turn.up("weights", h))
                emptied[b] = [(act_core, ("wT", h))]

            def values(h):
                pe.wait_ge(*act_core.at("wT", h))
                w = wT(h)
                c = slice(h * P, (h + 1) * P)
                if h == 0:
                    take(4)
                    take(5)
                pe.matmul(banks[4][:, c], w[:, 0:P], v_da[:, 0, c], start=True, stop=True)
                pe.matmul(banks[5][:, c], w[:, P:2 * P], v_da[:, 0, c], start=True, stop=False)
                pe.matmul(banks[5][:, c], w[:, 2 * P:3 * P], v_da[:, 1, c], start=False, stop=True
                          ).then_inc(*pe_core.up("o", h))

            for n in ("q", "k"):
                for t in range(TT):
                    pe.wait_ge(*dve_out.at(n, t))
            for t in range(TT):
                pe.wait_ge(*act_out.at("v", t))
            scores(0)
            scores(1)
            kv_block(0, 2)
            for h in range(DA_H):
                weights(h)
                if h + 2 < DA_H:
                    scores(h + 2)
                values(h)
            turn_out(("kv", 0, 1), tk[:, 1])
            for t in range(TT):
                emptied[4 + t] = [(dve_core, ("o_copy", t))]
            for t in range(TT):
                turn_split("a_out", t, 0, kT_da_flat(t), [(dve_core, ("a_out", t))])
            out_blocks("ev_out", lambda t, half: [(dve_lo, ("a_out", t, 0))] if half == 0 else [(dve_lo, ("b_out",))])

        def cross(l, need, between):
            for c in range(2):
                column_block(("xq", l, c), first[(("xq", l), c)], xT_hi, xT_lo, GU if c == 0 else (2, 3),
                             [(act_out, (("xq", l, c),))], need, between if c == 0 else None)
                if c == 1:
                    turn_out(("xq", l, 0), tk[:, 0])
            turn_out(("xq", l, 1), tk[:, 1])
            for c in range(2):
                for t in range(TT):
                    pe.wait_ge(*dve_out.at(("xq", l, c), t))
                    pe.wait_ge(*act_out.at(("kv", l, 2 + c), t))

            def scores(h):
                b = h % 4
                take(b)
                for t in range(TT):
                    for j in range(2):
                        mm = pe.matmul(banks[b][:, t * SEQ:(t + 1) * SEQ], q_x[:, 2 * h + j, t * P:(t + 1) * P],
                                       k_mem[:, 2 * h + j, :], start=(j == 0), stop=(j == 1))
                mm.then_inc(*pe_core.up("xs", l, h))
                emptied[b] = [(act_core, ("xp", l, h))]

            def weights(h):
                b = TR[h % 2]
                pe.wait_ge(*dve_core.at("xw", l, h))
                take(b)
                for mt in range(2):
                    for t in range(TT):
                        mm = pe.transpose(banks[b][:, mt * SEQ + t * P:mt * SEQ + (t + 1) * P],
                                          p_x[:, h % 2, t, mt * P:(mt + 1) * P], ident)
                mm.then_inc(*pe_turn.up("xw", l, h))
                emptied[b] = [(act_core, ("xpT", l, h))]

            def values(h):
                pe.wait_ge(*act_core.at("xpT", l, h))
                b = GU[h % 2]
                take(b)
                for j in range(2):
                    for mt in range(2):
                        c0 = h * XA_D + j * P
                        mm = pe.matmul(banks[b][:, j * SEQ:(j + 1) * SEQ], v_mem[:, mt, c0:c0 + P],
                                       pT_x[:, h % 2, mt, :], start=(mt == 0), stop=(mt == 1))
                mm.then_inc(*pe_core.up("xo", l, h))
                emptied[b] = [(dve_lo, ("xo", l, h))]

            scores(0)
            scores(1)
            for h in range(XA_H):
                weights(h)
                if h + 2 < XA_H:
                    scores(h + 2)
                values(h)
            out_blocks(("xo", l), lambda t, half: [(dve_lo, ("xo", l, 2 * half + 1))])

        def s5_prepare():
            for kind, n in (("s5_b", 0), ("s5_c", 1)):
                for ri in range(2):
                    src = s5_blocks[n][:, ri * 512:(ri + 1) * 512]
                    turn((kind, ri), src, [(dve_core, (kind, ri))], XT[n][ri], [(dve_core, (kind + "T", ri))])

        def odd_mixer(need, between):
            nm = {0: "u", 1: "qk", 2: "rv", 3: "rg"}

            def project(c, dst, **first_one):
                column_block(("od", c), first[("od_in", c)], xT_hi, xT_lo, dst, [(act_out, (nm[c],))], **first_one)

            def inputs(j):
                b = S5_IN[j % 4]
                take(b)
                r = slice(32 * (j % 4), 32 * (j % 4) + 32)
                for ri in range(2):
                    mm = pe.matmul(banks[b][:, ri * SEQ:(ri + 1) * SEQ], s5_bT[r, ri, j // 4, :],
                                   uT[r, j // 4, :], start=True, stop=True)
                mm.then_inc(*pe_core.up("s5_x", j))
                emptied[b] = [(dve_core, ("s5_in", j))]

            def outputs(j):
                pe.wait_ge(*pool_core.at("s5_h", j))
                if j == 0:
                    pe.wait_ge(*dve_core.at("s5_neg_c"))
                    take(4)
                    take(5)
                q, r = j // 4, 32 * (j % 4)
                b = j % 2
                terms = ((s5_cT[:, 0], s5_h[:, b, 0]), (s5_neg_c, s5_t[:, b, 1]),
                         (s5_cT[:, 1], s5_t[:, b, 0]), (s5_cT[:, 1], s5_h[:, b, 1]))
                for n, (c, h) in enumerate(terms):
                    mm = pe.matmul(banks[4 + q // 2][r:r + 32, (q % 2) * SEQ:(q % 2 + 1) * SEQ],
                                   c[:, q, r:r + 32], h, start=(n == 0), stop=(n == len(terms) - 1))
                mm.then_inc(*pe_core.up("s5_y", j))

            project(0, (4, 5), need=need, between=between)
            project(1, (0, 1))
            turn_out("u", tk[:, 0])
            kv_block(1, 3, (4, 5))
            turn_out("qk", tk[:, 1], dve_core)
            for t in range(TT):
                pe.wait_ge(*dve_out.at("u", t))
            for j in range(4):
                inputs(j)
            parts = [(c, t, half, k) for c in (2, 3) for t in range(TT) for half in range(2) for k in (0, 2)]
            for j, (c, t, half, k) in enumerate(parts):
                if half == 0 and k == 0:
                    take(t)
                column_part(first[("od_in", c)] + half, t, half, xT_hi, xT_lo, (0, 1), ("od", c),
                            steps_k=(k, k + 1))
                emptied[t] = [(act_out, (nm[c], t))]
                if j >= 1 and j + 3 < S5_TILES:
                    inputs(j + 3)
                outputs(j)
            for t in range(TT):
                pe.wait_ge(*dve_out.at("qk", t))
            for h in range(RET_H):
                take(h)
                r = slice(64 * (h % 2), 64 * (h % 2) + 64)
                q, k = qkT[r, 0, h // 2, :], qkT[r, 1, h // 2, :]
                pe.matmul(banks[h][:, 0:SEQ], k[:, 0:P], q, start=True, stop=True)
                pe.matmul(banks[h][:, SEQ:SEQ + P], k[:, P:SEQ], q[:, P:SEQ], start=True, stop=True
                          ).then_inc(*pe_core.up("ret_s", h))
                emptied[h] = [(dve_core, ("ret_w", h))]
            u = first["glu"]
            pe.wait_ge(lo_done, u + 1)
            pe.wait_ge(*dve_lo.at("z"))
            wh, wl = w3(w_hi, u, 4), w3(w_lo, u, 4)
            for o in range(4):
                if o % 2 == 0:
                    take(TR[o // 2])
                for k in range(4):
                    c = slice(o * P, (o + 1) * P)
                    mm = three(banks[TR[o // 2]][:, (o % 2) * SEQ:(o % 2 + 1) * SEQ], wh[:, k, c], wl[:, k, c],
                               xT_hi[:, k, :], xT_lo[:, k, :], k == 0, k == 3)
            mm.then_inc(unit_done, 1)
            for q in range(2):
                emptied[TR[q]] = [(act_core, ("glu", 3))]

            pe.wait_ge(*dve_core.at("s5_out", 3))
            for h in range(RET_H):
                pe.wait_ge(*dve_core.at("ret_w", h))
                w, v = ret_w(h), ret_v
                c = slice(h * P, (h + 1) * P)
                pe.matmul(banks[4][:, c], w[:, 0:P], v[:, 0, c], start=True, stop=True)
                pe.matmul(banks[5][:, c], w[:, P:SEQ], v[:, 0, c], start=True, stop=False)
                pe.matmul(banks[5][:, c], w[:, SEQ:SEQ + P], v[:, 1, c], start=False, stop=True
                          ).then_inc(*pe_core.up("ret_o", h))
            for t in range(TT):
                emptied[4 + t] = [(dve_core, ("ret_n", t))]
            for t in range(TT):
                turn_split("d_out", t, 1, osb[:, t, :], [(dve_core, ("d_out", t))])
            out_blocks("od_out", lambda t, half: [(dve_lo, ("d_out", t, 1))] if half else [(dve_lo, ("c_out",))])

        def memory_tokens():
            pe.wait_ge(loaded["nat"], 16 * 9)
            pe.wait_ge(*dve_core.at("log_step"))
            for j in range(4):
                pe.transpose(banks[2][:, 16 * j:16 * j + 10], nat[0:10, j * P:(j + 1) * P], ident[0:10, 0:10])
            for j in range(3):
                mm = pe.transpose(banks[2][:, 64 + 16 * j:80 + 16 * j], nat[0:16, 512 + j * P:512 + (j + 1) * P],
                                  ident[0:16, 0:16])
            mm.then_inc(*pe_turn.up("params"))
            emptied[2] = [(dve_core, ("params",))]
            pe.wait_ge(loaded["mem"], 16)
            for t in range(TT):
                for half in range(2):
                    turn_split("mem", t, half, ax[:, t, half * HALF:(half + 1) * HALF], [])

        def turn_x_in(t):
            pe.wait_ge(loaded["x" if t == 0 else "x1"], 16)
            for half in range(2):
                turn_split("x_in", t, half, x[:, t, half * HALF:(half + 1) * HALF], [])

        pe.wait_ge(loaded["const"], 16)
        pe.wait_ge(*zeroed.at("zero"))
        turn_x_in(0)
        turn_x_in(1)
        ffn(0, lambda t, half: [(dve_lo, ("x_in", t, half))], None, memory_tokens)
        between = norm(0)
        even_mixer(x_ready(0), between)
        between = norm(1)
        cross(0, x_ready(1), between)
        between = norm(2)
        ffn(1, x_ready(2), between)
        between = norm(3)
        ffn(2, x_ready(3), between, s5_prepare)
        between = norm(4)
        odd_mixer(x_ready(4), between)
        between = norm(5)
        cross(1, x_ready(5), between)
        between = norm(6)
        ffn(3, x_ready(6), between)

    @block.scalar
    def _(act):
        split = [0]

        def split_to(u):
            while split[0] <= u:
                v = split[0]
                if v < n_units:
                    act.wait_ge(raw_in[v % NSLOT], 32 * (v // NSLOT + 1))
                    if v >= NSLOT:
                        act.wait_ge(unit_done, v - NSLOT + 1)
                    act.activation(w_hi[:, v % NSLOT, :], raw[:, v % NSLOT, :], ACT.Copy).then_inc(hi_done, 1)
                split[0] += 1

        def ffn(f, interlude=None, late=None):
            u, n = first[("ffn", f)], 2 * NB * f

            def hi(c, i):
                v = u + 2 + c
                act.wait_ge(raw_in[v % NSLOT], i * 32 + 32 * (v // NSLOT + 1))
                act.wait_ge(unit_done, i * 3 + (v - NSLOT + 1))
                act.activation(w_hi[:, v % NSLOT, :], raw[:, v % NSLOT, :], ACT.Copy).then_inc(hi_done, 1)

            def silu(t, full0, full1, free):
                if t == 0:
                    act.wait_ge(gu_full, full0)
                else:
                    act.wait_ge(unit_done, full1)
                if free is not None:
                    act.wait_ge(h_done, free + t)
                act.activation(act_h[:, t, :], banks[GU[t]][:, 0:FB], ACT.Silu).then_inc(silu_done, 1)

            def hidden_hi(t, ready, dst):
                act.wait_ge(h_turned, ready + t)
                act.activation(dst[:, 0:2, t * P:(t + 1) * P],
                               banks[TR[t]][:, 0:2 * P].rearrange("p (k c) -> p k c", k=2), ACT.Copy
                               ).then_inc(h_hi, 1)

            split_to(u + 2)
            for t in range(TT):
                silu(t, NB * f + 1, u + 2, n - 1 if f else None)
            if interlude:
                interlude()
            with act.Fori(0, NB - 2) as i:
                for t in range(TT):
                    hidden_hi(t, i * 2 + (n + 1), hT_hi)
                hi(1, i)
                hi(2, i)
                for t in range(TT):
                    silu(t, i + (NB * f + 2), i * 3 + (u + 4), i * 2 + (n + 1))
                hi(3, i)
            b = NB - 1
            for t in range(TT):
                hidden_hi(t, n + 2 * b - 1, hT_hi)
            split[0] = u + 3 * b
            split_to(u + 3 * b)
            if late:
                late()
            split_to(u + 3 * b + 1)
            silu(0, NB * f + NB, None, n + 2 * b - 1)
            silu(1, None, u + 3 * b + 1, n + 2 * b - 1)
            hidden_hi(0, n + 2 * b + 1, xT_hi)
            split_to(u + 3 * b + 2)
            hidden_hi(1, n + 2 * b + 1, xT_hi)

        def split_operand(name, t, half, dst=None):
            act.wait_ge(*pe_turn.at(name, t, half))
            dst = xT_hi if dst is None else dst
            act.activation(dst[:, 4 * half:4 * half + 4, t * P:(t + 1) * P],
                           banks[XT[t][half]][:, :].rearrange("p (k c) -> p k c", k=4), ACT.Copy
                           ).then_inc(*act_hi.up(name, t, half))

        def copy_out(name, key, u, dst, bank, fn=ACT.Copy, free=None):
            split_to(u + 3)
            if free is not None:
                for t in range(TT):
                    act.wait_ge(*pe_turn.at(free, t))
            for t in range(TT):
                act.wait_ge(*end_of((key, u), t))
                act.activation(dst[:, t, :], banks[bank[t]][:, :], fn).then_inc(*act_out.up(name, t))

        def kv_out(l, c, bank=GU, free=None):
            name = ("kv", l, c)
            u = first[(("kv", l), c)]
            if c < 2:
                copy_out(name, name, u, tk[:, c % 2], bank, free=free)
            else:
                copy_out(name, name, u, v_mem[:, :, (c - 2) * HALF:(c - 1) * HALF], bank)

        def norm(i, last=False, free=None):
            e = norm_units[i]

            def deviation(t):
                act.wait_ge(*dve_ln.at("var", i, t))
                act.activation(mv[:, t, 2:3], mv[:, t, 1:2], ACT.Sqrt, bias=eps_col).then_inc(*act_ln.up("sd", i, t))

            def operand(t):
                for half in range(2):
                    split_operand(("x", i), t, half)

            split_to(e + 1)
            deviation(0)
            split_to(e + 2)
            deviation(1)
            if last:
                return
            operand(0)
            kv = kv_of_norm.get(i)
            if kv:
                kv_out(*kv, free=free)
                operand(1)
            for t in range(TT):
                act.wait_ge(*dve_ln.at("x", i, t))
                act.activation(ax[:, t, :], x[:, t, :], ACT.Copy, scale=ALPHA).then_inc(*act_ln.up("ax", i, t))
            split_to(e + 3)
            if not kv:
                operand(1)

        def even_mixer():
            copy_out("xr", ("ev", 4), first[("ev_in", 4)], tk[:, 0], (4, 5), free=("kv", 0, 0))
            copy_out("gate", ("ev", 3), first[("ev_in", 3)], tk[:, 1], (0, 1), ACT.Gelu_apprx_tanh)
            copy_out("q", ("ev", 0), first[("ev_in", 0)], tk[:, 0], (2, 3), free="xr")
            for g in range(2):
                for t2 in range(2):
                    act.wait_ge(*pe_core.at("gates", g, t2))
                    for j in range(2):
                        tile = 2 * t2 + j
                        ins = act.activation(lru_gate[g][:, tile, :], banks[TR[t2]][:, j * SEQ:(j + 1) * SEQ],
                                             ACT.Sigmoid, bias=pv[:, tile, 5 + g:6 + g]
                                             ).then_inc(*act_core.up("gates", g, t2))
            act.wait_ge(*act_core.now())
            act.wait_ge(*dve_core.at("softplus"))
            for tile in range(4):
                act.activation(lru_a[:, tile, :], lru_gate[0][:, tile, :], ACT.Exp, scale=sm[:, 4 + tile:5 + tile]
                               ).then_inc(*act_core.up())
                act.activation(lru_b[:, tile, :], lru_gate[0][:, tile, :], ACT.Tanh, scale=sm[:, tile:tile + 1]
                               ).then_inc(*act_core.up("decay"))
            copy_out("k", ("ev", 1), first[("ev_in", 1)], tk[:, 1], (4, 5), free="gate")
            act.wait_ge(*dve_core.at("one_minus_a2"))
            act.activation(lru_gate[0], lru_gate[0], ACT.Sqrt).then_inc(*act_core.up("root"))
            copy_out("v", ("ev", 2), first[("ev_in", 2)], v_da, (0, 1))
            kv_out(0, 1, free="k")
            act.wait_ge(*dve_core.at("b_out"))
            act.activation(xT_hi[:, 4:8, :], gateT[:, :, :], ACT.Copy).then_inc(*act_hi.up("b_out"))

            def exps(h):
                for m in range(2):
                    act.wait_ge(*dve_core.at("max", h, m))
                    for t in range(TT):
                        c = slice(0, P) if t == 0 else slice(P, 3 * P)
                        s = scores_sb(h, m)[:, c]
                        k = 16 + 4 * (h % 2) + 2 * m + t
                        act.activation(s, s, ACT.Exp, bias=sm[:, k:k + 1], scale=DA_D ** -0.5,
                                       accum_out=sm[:, k + 8:k + 9]).then_inc(*act_core.up("exp", h, m))

            exps(0)
            exps(1)
            kv_out(0, 2)
            for h in range(DA_H):
                if 1 <= h < DA_H - 1:
                    exps(h + 1)
                act.wait_ge(*pe_turn.at("weights", h))
                act.activation(wT(h), banks[TR[h % 2]][:, 0:384], ACT.Copy).then_inc(*act_core.up("wT", h))
            for t in range(TT):
                act.wait_ge(*dve_core.at("rms", t))
                act.activation(sm[:, 44 + 4 * t:48 + 4 * t], sm[:, 36 + 4 * t:40 + 4 * t], ACT.Sqrt,
                               scale=1.0 / (2 * DA_D), bias=eps_col).then_inc(*act_core.up("rms", t))
            for t in range(TT):
                split_operand("a_out", t, 0)

        def cross(l):
            for c in range(2):
                name = ("xq", l, c)
                copy_out(name, name, first[(("xq", l), c)], tk[:, c], GU if c == 0 else (2, 3))

            def exps(h):
                act.wait_ge(*dve_core.at("xmax", l, h))
                for t in range(TT):
                    k = 52 + 2 * (h % 2) + t
                    act.activation(p_x[:, h % 2, t, :], banks[h % 4][:, t * SEQ:(t + 1) * SEQ], ACT.Exp,
                                   bias=sm[:, k:k + 1], scale=XA_D ** -0.5, accum_out=sm[:, k + 4:k + 5]
                                   ).then_inc(*act_core.up("xp", l, h))

            def out_hi(h):
                act.wait_ge(*pe_core.at("xo", l, h))
                act.activation(xT_hi[:, 2 * h:2 * h + 2, :],
                               banks[GU[h % 2]][:, :].rearrange("p (k c) -> p k c", k=2), ACT.Copy
                               ).then_inc(*act_hi.up("xo", l, h))

            exps(0)
            exps(1)
            for h in range(XA_H):
                act.wait_ge(*pe_turn.at("xw", l, h))
                act.activation(pT_x[:, h % 2, :, :], banks[TR[h % 2]][:, :].rearrange("p (k c) -> p k c", k=2),
                               ACT.Copy).then_inc(*act_core.up("xpT", l, h))
                if h + 2 < XA_H:
                    exps(h + 2)
                out_hi(h)

        def odd_mixer():
            copy_out("u", ("od", 0), first[("od_in", 0)], tk[:, 0], (4, 5))
            copy_out("qk", ("od", 1), first[("od_in", 1)], tk[:, 1], (0, 1))
            kv_out(1, 3, (4, 5))
            for c, name, dst, fn in ((2, "rv", ret_v, ACT.Copy), (3, "rg", ret_gate, ACT.Silu)):
                u = first[("od_in", c)]
                for t in range(TT):
                    split_to(u + 2 + t)
                    act.wait_ge(*end_of((("od", c), u), t))
                    act.activation(dst[:, t, :], banks[t][:, :], fn).then_inc(*act_out.up(name, t))
            split_to(first[("od_out", 0)] + 1)
            for q in range(4):
                act.wait_ge(*dve_core.at("s5_out", q))
            for a in range(2):
                act.activation(s5_y[a], s5_y[a], ACT.Gelu_apprx_tanh).then_inc(*act_core.up("gelu"))
            act.wait_ge(*act_core.now())
            for a in range(2):
                act.activation(xT_hi[:, 2 * a:2 * a + 2, :], s5_y[a], ACT.Copy).then_inc(*act_hi.up("z"))
            act.wait_ge(unit_done, first["glu"] + 1)
            for o in range(4):
                act.activation(s5_t[:, o // 2, o % 2, :], banks[TR[o // 2]][:, (o % 2) * SEQ:(o % 2 + 1) * SEQ],
                               ACT.Sigmoid, bias=pv[:, o, 9:10]).then_inc(*act_core.up("glu", o))
            act.wait_ge(*dve_core.at("c_out"))
            for a in range(2):
                act.activation(xT_hi[:, 2 * a:2 * a + 2, :], s5_y[a], ACT.Copy).then_inc(*act_hi.up("c_out"))
            split_to(first[("od_out", 0)] + 1)
            act.wait_ge(*dve_core.at("ret_var"))
            act.activation(sm[:, 78:86], s5_h[:, 0, 0, 64:80].rearrange("p (a b) -> p a b", b=2)[:, :, 1], ACT.Sqrt,
                           bias=eps_col).then_inc(*act_core.up("ret_sd"))
            for t in range(TT):
                split_operand("d_out", t, 1)

        eps_col = sm[:, 92:93]

        def memory_tokens():
            for t in range(TT):
                for half in range(2):
                    split_operand("mem", t, half, memT_hi)
            for t in range(TT):
                act.activation(ax[:, t, :], x[:, t, :], ACT.Copy, scale=ALPHA).then_inc(*act_ln.up("ax", -1, t))

        def lru_parameters():
            act.wait_ge(*dve_core.at("neg_abs"))
            act.activation(sm[:, 8:12], sm[:, 12:16], ACT.Exp).then_inc(*act_core.up("exp_lambda"))
            act.wait_ge(*dve_core.at("lambda_sum"))
            act.activation(sm[:, 32:34], sm[:, 34:36], ACT.Exp).then_inc(*act_core.up("da_exp"))

        def s5_parameters():
            s = s5_par
            act.wait_ge(*dve_core.at("s5_args"))
            act.activation(s(3), s(3), ACT.Exp).then_inc(*act_core.up("s5_step"))
            act.wait_ge(*dve_core.at("s5_angle"))
            act.activation(s(4), s(4), ACT.Exp).then_inc(*act_core.up())
            act.activation(s(5), s(6), ACT.Sin).then_inc(*act_core.up())
            act.activation(s(7), s(6), ACT.Sin, scale=0.5).then_inc(*act_core.up("s5_sin"))

        act.dma_start(x[:, 1, :], A["x"][0, P:SEQ, :]).then_inc(loaded["x1"], 16)
        for t in range(TT):
            for half in range(2):
                split_operand("x_in", t, half)
        ffn(0, memory_tokens, lru_parameters)
        norm(0)
        even_mixer()
        norm(1)
        cross(0)
        norm(2, free=("xq", 0, 0))
        ffn(1, None, s5_parameters)
        norm(3, free=("kv", 1, 0))
        ffn(2)
        norm(4)
        odd_mixer()
        norm(5)
        cross(1)
        norm(6)
        ffn(3)
        norm(7, last=True)

    @block.vector
    def _(v):
        split = [0]
        V = nc.vector

        def split_to(u):
            while split[0] <= u:
                w = split[0]
                if w < n_units:
                    v.wait_ge(hi_done, w + 1)
                    s = w % NSLOT
                    V.tensor_tensor(w_lo[:, s, :], raw[:, s, :], w_hi[:, s, :].bitcast(F32), ALU.subtract
                                    ).then_inc(lo_done, 1)
                split[0] += 1

        def ffn(f, interlude=None, late=None):
            u, n = first[("ffn", f)], 2 * NB * f

            def lo(c, i):
                s = (u + 2 + c) % NSLOT
                v.wait_ge(hi_done, i * 3 + (u + 3 + c))
                V.tensor_tensor(w_lo[:, s, :], raw[:, s, :], w_hi[:, s, :].bitcast(F32), ALU.subtract
                                ).then_inc(lo_done, 1)

            def hidden(t, ready, turned):
                v.wait_ge(silu_done, ready + t)
                if turned is not None:
                    v.wait_ge(h_turned, turned + t)
                V.tensor_tensor(hid[:, t, :], act_h[:, t, :], banks[GU[t]][:, FB:2 * FB], ALU.mult
                                ).then_inc(h_done, 1)

            def hidden_lo(t, ready, hi, dst):
                v.wait_ge(h_hi, ready + t)
                V.tensor_tensor(dst[:, 0:2, t * P:(t + 1) * P],
                                banks[TR[t]][:, 0:2 * P].rearrange("p (k c) -> p k c", k=2),
                                hi[:, 0:2, t * P:(t + 1) * P].bitcast(F32), ALU.subtract).then_inc(h_lo, 1)

            split_to(u + 2)
            for t in range(TT):
                hidden(t, n + 1, n - 1 if f else None)
            if interlude:
                interlude()
            with v.Fori(0, NB - 2) as i:
                for t in range(TT):
                    hidden_lo(t, i * 2 + (n + 1), hT_hi, hT_lo)
                lo(1, i)
                lo(2, i)
                for t in range(TT):
                    hidden(t, i * 2 + (n + 3), i * 2 + (n + 1))
                lo(3, i)
            b = NB - 1
            for t in range(TT):
                hidden_lo(t, n + 2 * b - 1, hT_hi, hT_lo)
            split[0] = u + 3 * b
            split_to(u + 3 * b)
            if late:
                late()
            split_to(u + 3 * b + 1)
            for t in range(TT):
                hidden(t, n + 2 * b + 1, n + 2 * b - 1)
            hidden_lo(0, n + 2 * b + 1, xT_hi, xT_lo)
            split_to(u + 3 * b + 2)
            hidden_lo(1, n + 2 * b + 1, xT_hi, xT_lo)

        def split_operand(name, t, half, hi=None, lo=None):
            hi = xT_hi if hi is None else hi
            lo = xT_lo if lo is None else lo
            v.wait_ge(*act_hi.at(name, t, half))
            at = (slice(None), slice(4 * half, 4 * half + 4), slice(t * P, (t + 1) * P))
            V.tensor_tensor(lo[at], banks[XT[t][half]][:, :].rearrange("p (k c) -> p k c", k=4), hi[at].bitcast(F32),
                            ALU.subtract).then_inc(*dve_lo.up(name, t, half))

        def feature_out(name, dst):
            for t in range(TT):
                v.wait_ge(*pe_turn.at(name, t))
                V.tensor_copy(dst(t), banks[TR[t]][:, :].rearrange("p (k c) -> p k c", k=4)
                              ).then_inc(*dve_out.up(name, t))

        def kv_turned(l, c):
            if c < 2:
                feature_out(("kv", l, c), lambda t: k_mem[:, 4 * c:4 * c + 4, t * P:(t + 1) * P])

        def norm(i, scale, key, last=False):
            e = norm_units[i]

            def total(t, c):
                s = slice(c * 512, (c + 1) * 512)
                V.scalar_tensor_tensor(out=x[:, t, s], in0=banks[ACC[t] + c][:, :], scalar=scale,
                                       in1=ax[:, t, s], op0=ALU.mult, op1=ALU.add
                                       ).then_inc(*dve_ln.up("sum", i, t, c))

            def stats(t, c):
                v.wait_ge(*dve_ln.at("sum", i, t, c))
                V.bn_stats(bn[:, t, 6 * c:6 * c + 6], x[:, t, c * 512:(c + 1) * 512]).then_inc(*dve_ln.up())

            def centre(t):
                v.wait_ge(*dve_ln.now())
                V.bn_aggr(mv[:, t, 0:2], bn[:, t, :]).then_inc(*dve_ln.up("var", i, t))
                v.wait_ge(*dve_ln.now())
                V.scalar_tensor_tensor(out=x[:, t, :], in0=x[:, t, :], scalar=mv[:, t, 0:1], in1=gb[:, 0, :],
                                       op0=ALU.subtract, op1=ALU.mult).then_inc(*dve_ln.up())

            def finish(t):
                v.wait_ge(*act_ln.at("sd", i, t))
                V.reciprocal(mv[:, t, 3:4], mv[:, t, 2:3]).then_inc(*dve_ln.up())
                v.wait_ge(*dve_ln.now())
                V.scalar_tensor_tensor(out=x[:, t, :], in0=x[:, t, :], scalar=mv[:, t, 3:4], in1=gb[:, 1, :],
                                       op0=ALU.mult, op1=ALU.add).then_inc(*dve_ln.up("x", i, t))

            def operand(t):
                for half in range(2):
                    split_operand(("x", i), t, half)

            v.wait_ge(loaded["gb"], 32 * (i + 1))
            by_columns = key[0] != "acc"
            if by_columns:
                split_to(e)
                v.wait_ge(unit_done, e - 1)
                for t in range(TT):
                    v.wait_ge(*act_ln.at("ax", i - 1, t))
                    total(t, 0)
                for t in range(TT):
                    stats(t, 0)
            split_to(e + 1)
            for t in range(TT):
                if t == 0:
                    v.wait_ge(*pe_half.at(*key))
                else:
                    v.wait_ge(unit_done, e + 1)
                if not by_columns:
                    v.wait_ge(*act_ln.at("ax", i - 1, t))
                    total(t, 0)
                total(t, 1)
                if not by_columns:
                    stats(t, 0)
                stats(t, 1)
                centre(t)
                if t == 0:
                    split_to(e + 2)
                    finish(0)
            if not last and not kv_of_norm.get(i):
                operand(0)
            finish(1)
            if last:
                return
            kv = kv_of_norm.get(i)
            if kv:
                operand(0)
                split_to(e + 4)
            else:
                split_to(e + 3)
            operand(1)
            if kv:
                kv_turned(*kv)

        def op(ins, *name):
            return ins.then_inc(*dve_core.up(*name))

        def done():
            v.wait_ge(*dve_core.now())

        def rotate(name, t, data, halfw, cos, sin, ta, tb):
            lo, hi = slice(0, halfw), slice(halfw, 2 * halfw)
            V.tensor_tensor(ta, data, cos, ALU.mult).then_inc(*dve_core.up())
            V.tensor_tensor(tb[..., lo], data[..., hi], sin[..., lo], ALU.mult).then_inc(*dve_core.up())
            V.tensor_tensor(tb[..., hi], data[..., lo], sin[..., hi], ALU.mult).then_inc(*dve_core.up())
            v.wait_ge(*dve_core.now())
            V.tensor_tensor(data, ta, tb, ALU.add).then_inc(*dve_core.up(name, t))

        def even_mixer():
            split_to(first[("ev_in", 3)] + 3)
            V.memset(xrT[:, :, 0:3], 0.0).then_inc(*dve_core.up())
            feature_out("xr", lambda t: xrT[:, :, 3 + t * P:3 + (t + 1) * P])
            v.wait_ge(*dve_out.now())
            v.wait_ge(*dve_core.now())
            for k in range(4):
                for tile in range(4):
                    src = xrT[:, tile, k:k + SEQ]
                    if k == 0:
                        V.tensor_scalar(conv[:, tile, :], src, pv[:, tile, 0:1], pv[:, tile, 4:5], ALU.mult, ALU.add
                                        ).then_inc(*dve_core.up())
                    else:
                        v.wait_ge(dve_core.sem, dve_core.n - 3)
                        V.scalar_tensor_tensor(out=conv[:, tile, :], in0=src, scalar=pv[:, tile, k:k + 1],
                                               in1=conv[:, tile, :], op0=ALU.mult, op1=ALU.add
                                               ).then_inc(*dve_core.up("conv"))
            split_to(first[("ev_in", 0)] + 3)
            feature_out("gate", lambda t: gateT[:, :, t * P:(t + 1) * P])
            ta, tb = rot_tmp[:, 0, :], rot_tmp[:, 1, :]

            def rotate_da(name, buf):
                for t in range(TT):
                    v.wait_ge(*act_out.at(name, t))
                    d3 = tk[:, buf, t, :].rearrange("p (g d) -> p g d", d=DA_D)[:, :, 0:DA_ROPE]
                    cs, sn = (k_(n).rearrange("p (t g d) -> p t g d", t=TT, d=DA_ROPE)[:, t]
                              for n in ("da_cos", "da_sin"))
                    done()
                    rotate(name, t, d3, DA_ROPE // 2, cs, sn, ta.rearrange("p (g d) -> p g d", d=DA_ROPE),
                           tb.rearrange("p (g d) -> p g d", d=DA_ROPE))

            rotate_da("q", 0)
            split_to(first[("ev_in", 1)] + 3)
            v.wait_ge(*act_core.at("decay"))
            g0, g1 = lru_gate
            V.tensor_tensor(g0, lru_a[:, :, :], lru_a[:, :, :], ALU.mult).then_inc(*dve_core.up())
            v.wait_ge(*act_core.at("gates", 1, 1))
            V.tensor_tensor(g1, g1, conv[:, :, :], ALU.mult).then_inc(*dve_core.up())
            done()
            V.scalar_tensor_tensor(out=g0, in0=g0, scalar=1.0, in1=lru_b[:, :, :], op0=ALU.add, op1=ALU.mult
                                   ).then_inc(*dve_core.up("one_minus_a2"))
            rotate_da("k", 1)
            feature_out("q", lambda t: qT_da[:, :, t * P:(t + 1) * P])
            split_to(first[("ev_in", 2)] + 3)
            v.wait_ge(*act_core.at("root"))
            V.tensor_tensor(lru_b[:, :, :], g0, g1, ALU.mult).then_inc(*dve_core.up())
            done()
            for tile in range(4):
                V.tensor_tensor_scan(conv[:, tile, :], lru_a[:, tile, :], lru_b[:, tile, :], 0.0, ALU.mult, ALU.add
                                     ).then_inc(*dve_core.up())
            feature_out("k", lambda t: kT_da[:, :, t * P:(t + 1) * P])
            done()
            v.wait_ge(*dve_out.now())
            V.tensor_tensor(gateT[:, :, :], gateT[:, :, :], conv[:, :, :], ALU.mult
                            ).then_inc(*dve_core.up("b_out"))
            split_to(first[(("kv", 0), 1)] + 3)
            v.wait_ge(*act_hi.at("b_out"))
            V.tensor_tensor(xT_lo[:, 4:8, :], gateT[:, :, :], xT_hi[:, 4:8, :].bitcast(F32), ALU.subtract
                            ).then_inc(*dve_lo.up("b_out"))

            def masked(h):
                for m in range(2):
                    s = scores_sb(h, m)
                    k = 16 + 4 * (h % 2) + 2 * m
                    v.wait_ge(*pe_core.at("scores", h, m))
                    V.tensor_tensor(s, banks[2 * (h % 2) + m][:, 0:384], k_("mask"), ALU.add
                                    ).then_inc(*dve_core.up("masked", h, m))
                    done()
                    V.reduce_max(sm[:, 86:87], s[:, 0:P], AX_X).then_inc(*dve_core.up())
                    V.reduce_max(sm[:, 87:88], s[:, P:3 * P], AX_X).then_inc(*dve_core.up())
                    done()
                    V.tensor_scalar(sm[:, k:k + 2], sm[:, 86:88], -(DA_D ** -0.5), None, ALU.mult
                                    ).then_inc(*dve_core.up("max", h, m))
                    done()

            def combine(h):
                k = 24 + 4 * (h % 2)
                v.wait_ge(*act_core.at("exp", h, 1))
                if h >= 2:
                    v.wait_ge(*pe_turn.at("weights", h - 2))
                V.reciprocal(sm[:, k:k + 4], sm[:, k:k + 4]).then_inc(*dve_core.up())
                done()
                V.tensor_scalar(sm[:, k + 2:k + 4], sm[:, k + 2:k + 4], sm[:, 93:94], None, ALU.mult
                                ).then_inc(*dve_core.up())
                done()
                for t in range(TT):
                    c = slice(0, P) if t == 0 else slice(P, 3 * P)
                    s0, s1 = scores_sb(h, 0)[:, c], scores_sb(h, 1)[:, c]
                    V.tensor_scalar(s1, s1, sm[:, k + 2 + t:k + 3 + t], None, ALU.mult).then_inc(*dve_core.up())
                    done()
                    V.scalar_tensor_tensor(out=xrT_w(h)[:, c], in0=s0, scalar=sm[:, k + t:k + t + 1], in1=s1,
                                           op0=ALU.mult, op1=ALU.add).then_inc(*dve_core.up("weights", h))

            masked(0)
            masked(1)
            split_to(first[(("kv", 0), 2)] + 3)
            for h in range(DA_H):
                combine(h)
                done()
                if h + 2 < DA_H:
                    masked(h + 2)
            kv_turned(0, 1)
            v.wait_ge(*pe_core.at("o", DA_H - 1))
            o2 = lru_a[:, :, :].rearrange("p a b -> p (a b)").rearrange("p (t d) -> p t d", t=TT)
            sq = conv[:, :, :].rearrange("p a b -> p (a b)").rearrange("p (t d) -> p t d", t=TT)
            for t in range(TT):
                V.tensor_copy(o2[:, t, :], banks[4 + t][:, :]).then_inc(*dve_core.up("o_copy", t))
                done()
                V.tensor_tensor(sq[:, t, :], o2[:, t, :], o2[:, t, :], ALU.mult).then_inc(*dve_core.up())
                done()
                V.reduce_sum(sm[:, 36 + 4 * t:40 + 4 * t], sq[:, t, :].rearrange("p (h d) -> p h d", h=DA_H), AX_X
                             ).then_inc(*dve_core.up("rms", t))
            for t in range(TT):
                c = slice(44 + 4 * t, 48 + 4 * t)
                v.wait_ge(*act_core.at("rms", t))
                V.reciprocal(sm[:, c], sm[:, c]).then_inc(*dve_core.up())
                done()
                V.tensor_scalar(sm[:, c], sm[:, c], 1.0 - LAMBDA_INIT, None, ALU.mult).then_inc(*dve_core.up())
                done()
                for h in range(DA_H):
                    V.scalar_tensor_tensor(out=kT_da_flat(t)[:, h * P:(h + 1) * P], in0=o2[:, t, h * P:(h + 1) * P],
                                           scalar=sm[:, 44 + 4 * t + h:45 + 4 * t + h], in1=da_g[:, :],
                                           op0=ALU.mult, op1=ALU.mult).then_inc(*dve_core.up("a_out", t))
            for t in range(TT):
                split_operand("a_out", t, 0)

        def cross(l):
            split_to(first[(("xq", l), 1)] + 3)
            for c in range(2):
                feature_out(("xq", l, c), lambda t: q_x[:, 4 * c:4 * c + 4, t * P:(t + 1) * P])

            def maxima(h):
                v.wait_ge(*pe_core.at("xs", l, h))
                V.tensor_reduce(sm[:, 86:88], banks[h % 4][:, :].rearrange("p (t k) -> p t k", t=TT), AX_X, ALU.max
                                ).then_inc(*dve_core.up())
                done()
                k = 52 + 2 * (h % 2)
                V.tensor_scalar(sm[:, k:k + 2], sm[:, 86:88], -(XA_D ** -0.5), None, ALU.mult
                                ).then_inc(*dve_core.up("xmax", l, h))
                done()

            def normalise(h):
                k = 56 + 2 * (h % 2)
                v.wait_ge(*act_core.at("xp", l, h))
                V.reciprocal(sm[:, k:k + 2], sm[:, k:k + 2]).then_inc(*dve_core.up())
                done()
                for t in range(TT):
                    V.tensor_scalar(p_x[:, h % 2, t, :], p_x[:, h % 2, t, :], sm[:, k + t:k + t + 1], None, ALU.mult
                                    ).then_inc(*dve_core.up("xw", l, h))

            def out_lo(h):
                v.wait_ge(*act_hi.at("xo", l, h))
                V.tensor_tensor(xT_lo[:, 2 * h:2 * h + 2, :],
                                banks[GU[h % 2]][:, :].rearrange("p (k c) -> p k c", k=2),
                                xT_hi[:, 2 * h:2 * h + 2, :].bitcast(F32), ALU.subtract
                                ).then_inc(*dve_lo.up("xo", l, h))

            maxima(0)
            maxima(1)
            normalise(0)
            for h in range(XA_H):
                if h + 2 < XA_H:
                    maxima(h + 2)
                if h + 1 < XA_H:
                    normalise(h + 1)
                out_lo(h)
            split_to(first[(("xo", l), 0)] + 1)

        def s5_parameters():
            s = s5_par
            V.tensor_scalar(s(0), s(0), -1e-4, None, ALU.min).then_inc(*dve_core.up("s5_args"))
            v.wait_ge(*act_core.at("s5_step"))
            done()
            V.tensor_tensor(s(4), s(0), s(3), ALU.mult).then_inc(*dve_core.up())
            V.tensor_tensor(s(6), s(1), s(3), ALU.mult).then_inc(*dve_core.up())
            done()
            V.tensor_scalar(s(8), s(6), 1.0 / (2 * math.pi), 12582912.0, ALU.mult, ALU.add).then_inc(*dve_core.up())
            done()
            V.tensor_scalar(s(8), s(8), 12582912.0, None, ALU.subtract).then_inc(*dve_core.up())
            done()
            for part in (6.28125, 0.0019350051879882812, 3.0199159819500178e-07):
                V.scalar_tensor_tensor(out=s(6), in0=s(8), scalar=-part, in1=s(6), op0=ALU.mult, op1=ALU.add
                                       ).then_inc(*dve_core.up())
                done()
            V.tensor_scalar(s(6), s(6), 3.1415925, -3.1415925, ALU.min, ALU.max).then_inc(*dve_core.up("s5_angle"))
            v.wait_ge(*act_core.at("s5_sin"))
            V.tensor_tensor(s(7), s(7), s(7), ALU.mult).then_inc(*dve_core.up())
            done()
            cos, sin, mag = s(8), s(5), s(4)
            V.tensor_scalar(cos, s(7), -2.0, 1.0, ALU.mult, ALU.add).then_inc(*dve_core.up())
            done()
            nr, ni, lr, li = s(6), s(3), s(0), s(1)
            V.tensor_tensor(nr, mag, cos, ALU.mult).then_inc(*dve_core.up())
            V.tensor_tensor(ni, mag, sin, ALU.mult).then_inc(*dve_core.up())
            done()
            V.tensor_scalar(nr, nr, 1.0, None, ALU.subtract).then_inc(*dve_core.up())
            V.tensor_tensor(s(7), lr, lr, ALU.mult).then_inc(*dve_core.up())
            V.tensor_tensor(s(9), li, li, ALU.mult).then_inc(*dve_core.up())
            done()
            V.tensor_tensor(s(7), s(7), s(9), ALU.add).then_inc(*dve_core.up())
            done()
            V.reciprocal(s(7), s(7)).then_inc(*dve_core.up())
            V.tensor_tensor(s(9), nr, lr, ALU.mult).then_inc(*dve_core.up())
            V.tensor_tensor(s(10), ni, li, ALU.mult).then_inc(*dve_core.up())
            done()
            V.tensor_tensor(s(9), s(9), s(10), ALU.add).then_inc(*dve_core.up())
            done()
            V.tensor_tensor(s(9), s(9), s(7), ALU.mult).then_inc(*dve_core.up())
            V.tensor_tensor(s(10), ni, lr, ALU.mult).then_inc(*dve_core.up())
            V.tensor_tensor(s(11), nr, li, ALU.mult).then_inc(*dve_core.up())
            done()
            V.tensor_tensor(s(10), s(10), s(11), ALU.subtract).then_inc(*dve_core.up())
            done()
            V.tensor_tensor(s(10), s(10), s(7), ALU.mult).then_inc(*dve_core.up())
            done()

        def s5_prepare():
            s = s5_par
            v.wait_ge(loaded["s5"], 64)
            b = [qkT[:, ri, 0, :].rearrange("p (j c) -> p j c", c=16) for ri in range(2)]
            fr, fi = (s(n).unsqueeze(2).to_broadcast([P, 16, 16]) for n in (9, 10))
            flat, c_flat = s5_blocks
            bd = [flat[:, ri * 512:(ri + 1) * 512].rearrange("p (j c) -> p j c", c=32) for ri in range(2)]
            t1, t2 = (s5_cT[:, 0, 2 * a:2 * a + 2, :].rearrange("p a b -> p (a b)").rearrange(
                "p (j c) -> p j c", c=16) for a in range(2))
            V.memset(flat, 0.0).then_inc(*dve_core.up())
            for ri in range(2):
                V.tensor_tensor(t1, b[ri], fr, ALU.mult).then_inc(*dve_core.up())
                V.tensor_tensor(t2, b[1 - ri], fi, ALU.mult).then_inc(*dve_core.up())
                done()
                for g in range(2):
                    r = slice(64 * g, 64 * g + 64)
                    V.tensor_tensor(bd[ri][r, :, 16 * g:16 * g + 16], t1[r], t2[r],
                                    ALU.subtract if ri == 0 else ALU.add).then_inc(*dve_core.up("s5_b", ri))
                done()
            for ri in range(2):
                c = qkT[:, ri, 1, :].rearrange("p (q n) -> p q n", n=64)
                cd = c_flat[:, ri * 512:(ri + 1) * 512].rearrange("p (q n) -> p q n", n=P)
                for g in range(2):
                    V.tensor_scalar(cd[:, :, 64 * g:64 * g + 64], c, k_("parity")[:, g:g + 1],
                                    1.0 if ri == 0 else -1.0, ALU.mult, ALU.mult
                                    ).then_inc(*dve_core.up("s5_c", ri))
            for n, (kind, dst) in enumerate((("s5_b", s5_bT), ("s5_c", s5_cT))):
                for ri in range(2):
                    v.wait_ge(*pe_turn.at(kind, ri))
                    V.tensor_copy(dst[:, ri].rearrange("p a b -> p (a b)"), banks[XT[n][ri]][:, :]
                                  ).then_inc(*dve_core.up(kind + "T", ri))
            V.tensor_copy(e_cos[:, :, 0], s(8)).then_inc(*dve_core.up())
            V.tensor_copy(e_sin[:, :, 0], s(5)).then_inc(*dve_core.up("theta"))

        def odd_mixer():
            split_to(first[("od_in", 0)] + 3)
            rt = [w[:, :, :].rearrange("p a b -> p (a b)") for w in (act_h, hid)]

            def rotate_qk(t):
                v.wait_ge(*act_out.at("qk", t))
                done()
                data, ta, tb = (w.rearrange("p (a h d) -> p a h d", a=2, d=RET_D)
                                for w in (tk[:, 1, t, :], rt[0], rt[1]))
                cs, sn = (k_(n).rearrange("p (t h d) -> p t h d", t=TT, d=RET_D)[:, t] for n in ("ret_cos", "ret_sin"))
                lo, hi = slice(0, RET_D // 2), slice(RET_D // 2, RET_D)
                for a in range(2):
                    V.tensor_tensor(ta[:, a], data[:, a], cs, ALU.mult).then_inc(*dve_core.up())
                    V.tensor_tensor(tb[:, a, :, lo], data[:, a, :, hi], sn[:, :, lo], ALU.mult
                                    ).then_inc(*dve_core.up())
                    V.tensor_tensor(tb[:, a, :, hi], data[:, a, :, lo], sn[:, :, hi], ALU.mult
                                    ).then_inc(*dve_core.up())
                done()
                V.tensor_tensor(tk[:, 1, t, :], rt[0], rt[1], ALU.add).then_inc(*dve_core.up("qk", t))

            kv = first[(("kv", 1), 3)]
            split_to(kv)
            rotate_qk(0)
            v.wait_ge(*pool_core.at("powers"))
            feature_out("u", lambda t: uT[:, :, t * P:(t + 1) * P])
            rotate_qk(1)
            split_to(kv + 3)
            feature_out("qk", lambda t: qkT[:, :, :, t * P:(t + 1) * P].rearrange("p a b c -> p (a b) c"))
            v.wait_ge(unit_done, kv + 2)
            V.tensor_scalar(osb[:, 0, :], s5_cT[:, 0].rearrange("p a b -> p (a b)"), -1.0, None, ALU.mult
                            ).then_inc(*dve_core.up("s5_neg_c"))
            xp = [tk[:, 0, b, :].rearrange("p (r k) -> p r k", r=2) for b in range(2)]
            xc, xs = (tk[:, 1, b, :].rearrange("p (r k) -> p r k", r=2) for b in range(2))

            def products(j):
                src = banks[S5_IN[j % 4]][:, :].rearrange("p (r c k) -> p r c k", r=2, k=S5_CH)
                v.wait_ge(*pe_core.at("s5_x", j))
                for e, out in ((e_cos, xc), (e_sin, xs)):
                    V.tensor_tensor(out.rearrange("p r (c k) -> p r c k", k=S5_CH), src,
                                    e[:, j, :].unsqueeze(1).unsqueeze(1).to_broadcast([P, 2, 2, S5_CH]), ALU.mult
                                    ).then_inc(*dve_core.up("s5_in", j))

            def rotate_in(j):
                v.wait_ge(*dve_core.at("s5_in", j))
                V.tensor_tensor(xp[j % 2][:, 0], xc[:, 0], xs[:, 1], ALU.add).then_inc(*dve_core.up())
                V.tensor_tensor(xp[j % 2][:, 1], xc[:, 1], xs[:, 0], ALU.subtract).then_inc(*dve_core.up("s5_xp", j))

            split_at = {5: 2, 8: 3, 11: 4, 14: 5}
            products(0)
            rotate_in(0)
            for j in range(S5_TILES):
                if j in split_at:
                    split_to(first[("od_in", 2)] + split_at[j])
                g = s5_g[:, j % 2]
                decay = s5_par(4)[:, j:j + 1].to_broadcast([P, S5_CH])
                if j >= 2:
                    v.wait_ge(*pool_core.at("s5_h", j - 2))
                v.wait_ge(*dve_core.at("s5_xp", j))
                for r in range(2):
                    V.tensor_tensor_scan(g[:, r, 0:S5_CH], decay, xp[j % 2][:, r, 0:S5_CH], 0.0, ALU.mult, ALU.add
                                         ).then_inc(*dve_core.up("s5_first", j))
                if j + 1 < S5_TILES:
                    products(j + 1)
                last = slice(S5_CH - 1, S5_CH)
                ec, es = e_cos[:, j, last], e_sin[:, j, last]
                v.wait_ge(*dve_core.at("s5_first", j))
                V.tensor_tensor(sm[:, 86:87], g[:, 1, last], es, ALU.mult).then_inc(*dve_core.up())
                V.tensor_tensor(sm[:, 87:88], g[:, 1, last], ec, ALU.mult).then_inc(*dve_core.up("s5_part", j))
                if j + 1 < S5_TILES:
                    rotate_in(j + 1)
                v.wait_ge(*dve_core.at("s5_part", j))
                V.scalar_tensor_tensor(out=sm[:, 88:89], in0=g[:, 0, last], scalar=ec, in1=sm[:, 86:87],
                                       op0=ALU.mult, op1=ALU.subtract).then_inc(*dve_core.up())
                V.scalar_tensor_tensor(out=sm[:, 89:90], in0=g[:, 0, last], scalar=es, in1=sm[:, 87:88],
                                       op0=ALU.mult, op1=ALU.add).then_inc(*dve_core.up())
                done()
                for r in range(2):
                    V.tensor_tensor_scan(g[:, r, S5_CH:SEQ], decay, xp[j % 2][:, r, S5_CH:SEQ], sm[:, 88 + r:89 + r],
                                         ALU.mult, ALU.add).then_inc(*dve_core.up("s5_g", j))
            v.wait_ge(*pe_core.at("s5_y", S5_TILES - 1))
            for q in range(4):
                V.scalar_tensor_tensor(out=s5_y[q // 2][:, q % 2, :], in0=uT[:, q, :], scalar=pv[:, q, 8:9],
                                       in1=banks[4 + q // 2][:, (q % 2) * SEQ:(q % 2 + 1) * SEQ],
                                       op0=ALU.mult, op1=ALU.add).then_inc(*dve_core.up("s5_out", q))
            v.wait_ge(*act_hi.at("z"))
            for a in range(2):
                V.tensor_tensor(xT_lo[:, 2 * a:2 * a + 2, :], s5_y[a], xT_hi[:, 2 * a:2 * a + 2, :].bitcast(F32),
                                ALU.subtract).then_inc(*dve_lo.up("z"))
            for h in range(RET_H):
                v.wait_ge(*pe_core.at("ret_s", h))
                if h >= 2:
                    v.wait_ge(*pe_core.at("ret_o", h - 2))
                dec = k_("decay").rearrange("p (h k) -> p h k", h=RET_H)[:, h]
                V.tensor_tensor(ret_w(h)[:, 0:SEQ], banks[h][:, 0:SEQ], dec, ALU.mult).then_inc(*dve_core.up())
                V.tensor_tensor(ret_w(h)[:, SEQ:SEQ + P], banks[h][:, SEQ:SEQ + P], dec[:, 0:P], ALU.mult
                                ).then_inc(*dve_core.up("ret_w", h))
            v.wait_ge(*act_core.at("glu", 3))
            for a in range(2):
                V.tensor_tensor(s5_y[a], s5_y[a], s5_t[:, a], ALU.mult).then_inc(*dve_core.up("c_out"))
            v.wait_ge(*act_hi.at("c_out"))
            for a in range(2):
                V.tensor_tensor(xT_lo[:, 2 * a:2 * a + 2, :], s5_y[a], xT_hi[:, 2 * a:2 * a + 2, :].bitcast(F32),
                                ALU.subtract).then_inc(*dve_lo.up("c_out"))
            split_to(first[("od_out", 0)] + 1)
            stat = s5_h[:, 0, 0, 0:64].rearrange("p (a b) -> p a b", b=8)
            agg = s5_h[:, 0, 0, 64:80].rearrange("p (a b) -> p a b", b=2)
            v.wait_ge(*pe_core.at("ret_o", RET_H - 1))
            for t in range(TT):
                for h in range(RET_H):
                    V.bn_stats(stat[:, 4 * t + h, 0:6], banks[4 + t][:, h * P:(h + 1) * P]).then_inc(*dve_core.up())
            done()
            for n in range(8):
                V.bn_aggr(agg[:, n, :], stat[:, n, 0:6]).then_inc(*dve_core.up("ret_var"))
            v.wait_ge(*act_core.at("ret_sd"))
            V.reciprocal(sm[:, 78:86], sm[:, 78:86]).then_inc(*dve_core.up())
            done()
            for t in range(TT):
                for h in range(RET_H):
                    n = 4 * t + h
                    V.tensor_scalar(osb[:, t, h * P:(h + 1) * P], banks[4 + t][:, h * P:(h + 1) * P], agg[:, n, 0:1],
                                    sm[:, 78 + n:79 + n], ALU.subtract, ALU.mult).then_inc(*dve_core.up("ret_n", t))
                V.tensor_tensor(ret_gate[:, t, :].rearrange("p (h d) -> p h d", h=RET_H),
                                ret_gate[:, t, :].rearrange("p (h d) -> p h d", h=RET_H),
                                ret_g[:, :].unsqueeze(1).to_broadcast([P, RET_H, P]), ALU.mult
                                ).then_inc(*dve_core.up())
                done()
                V.tensor_tensor(osb[:, t, :], osb[:, t, :], ret_gate[:, t, :], ALU.mult
                                ).then_inc(*dve_core.up("d_out", t))
            for t in range(TT):
                split_operand("d_out", t, 1)

        V.memset(zero[:, :], 0.0).then_inc(*zeroed.up())
        v.wait_ge(*zeroed.now())
        V.tensor_copy(zero_r[:, :], zero[:, :]).then_inc(*zeroed.up("zero"))
        V.memset(sm[:, 92:93], LN_EPS).then_inc(*dve_core.up())
        def parameter_rows():
            v.wait_ge(loaded["nat"], 16 * 9)
            for g in range(2):
                V.tensor_copy(nat[0:16, 768 + 64 * g:832 + 64 * g], sm[0:16, 90 + g:91 + g].to_broadcast([16, 64])
                              ).then_inc(*dve_core.up("log_step"))

        def memory_tokens():
            parameter_rows()
            v.wait_ge(*pe_turn.at("params"))
            V.tensor_copy(pv[:, :, :], banks[2][:, 0:64].rearrange("p (a b) -> p a b", b=16)[:, :, 0:10]
                          ).then_inc(*dve_core.up())
            for n, at in ((0, 64), (1, 80), (3, 96)):
                V.tensor_copy(s5_par(n), banks[2][:, at:at + 16]).then_inc(*dve_core.up("params"))
            for t in range(TT):
                for half in range(2):
                    split_operand("mem", t, half, memT_hi, memT_lo)

        def lru_parameters():
            lam = pv[:, :, 7]
            nl, na, e4, z4, z2, pl = (sm[:, c:c + 4] for c in (60, 12, 8, 64, 68, 72))
            done()
            V.tensor_scalar(nl, lam, -1.0, None, ALU.mult).then_inc(*dve_core.up())
            done()
            V.tensor_tensor(na, nl, lam, ALU.min).then_inc(*dve_core.up("neg_abs"))
            v.wait_ge(loaded["rows"], 48)
            dl = tk[:, 0, 0, 0:256].rearrange("p (a b d) -> p a b d", a=2, b=2)
            pr = tk[:, 0, 0, 256:384].rearrange("p (a d) -> p a d", a=2)
            V.tensor_tensor(pr, dl[:, :, 0, :], dl[:, :, 1, :], ALU.mult).then_inc(*dve_core.up())
            done()
            V.reduce_sum(sm[:, 34:36], pr, AX_X).then_inc(*dve_core.up("lambda_sum"))
            v.wait_ge(*act_core.at("exp_lambda"))
            V.tensor_scalar(z4, e4, 2.0, None, ALU.add).then_inc(*dve_core.up())
            done()
            V.reciprocal(z4, z4).then_inc(*dve_core.up())
            done()
            V.tensor_tensor(z4, z4, e4, ALU.mult).then_inc(*dve_core.up())
            done()
            V.tensor_tensor(z2, z4, z4, ALU.mult).then_inc(*dve_core.up())
            V.memset(pl, 1.0 / 17).then_inc(*dve_core.up())
            for n in range(15, 0, -2):
                done()
                V.tensor_tensor(pl, pl, z2, ALU.mult).then_inc(*dve_core.up())
                done()
                V.tensor_scalar(pl, pl, 1.0 / n, None, ALU.add).then_inc(*dve_core.up())
            done()
            V.tensor_tensor(pl, pl, z4, ALU.mult).then_inc(*dve_core.up())
            V.tensor_scalar(nl, nl, 0.0, None, ALU.max).then_inc(*dve_core.up())
            done()
            V.scalar_tensor_tensor(out=nl, in0=pl, scalar=2.0, in1=nl, op0=ALU.mult, op1=ALU.add
                                   ).then_inc(*dve_core.up())
            done()
            V.tensor_scalar(sm[:, 0:4], nl, LRU_C, None, ALU.mult).then_inc(*dve_core.up())
            V.tensor_scalar(sm[:, 4:8], nl, -LRU_C, None, ALU.mult).then_inc(*dve_core.up("softplus"))
            v.wait_ge(*act_core.at("da_exp"))
            V.tensor_scalar(sm[:, 93:94], sm[:, 33:34], LAMBDA_INIT, sm[:, 32:33], ALU.subtract, ALU.subtract
                            ).then_inc(*dve_core.up())

        for t in range(TT):
            for half in range(2):
                split_operand("x_in", t, half)
        ffn(0, memory_tokens, lru_parameters)
        norm(0, 0.5, ("acc", 0))
        v.wait_ge(loaded["tables"], 16)
        even_mixer()
        norm(1, 1.0, ("ev_out", 1))
        cross(0)
        norm(2, 1.0, (("xo", 0), 1))
        ffn(1, None, s5_parameters)
        norm(3, 0.5, ("acc", 1))
        ffn(2, s5_prepare)
        norm(4, 0.5, ("acc", 2))
        odd_mixer()
        norm(5, 1.0, ("od_out", 1))
        cross(1)
        norm(6, 1.0, (("xo", 1), 1))
        ffn(3)
        norm(7, 0.5, ("acc", 3), last=True)


INPUTS = ("x", "mem", "ln_g", "ln_b", "ffn_w_gate", "ffn_w_up", "ffn_w_down", "xa_w_q", "xa_w_kv", "xa_w_o",
          "ev_w_in", "ev_w_out", "da_lambda", "da_norm_g", "lru_conv_w", "lru_conv_b", "lru_gate_w", "lru_gate_b",
          "lru_lambda", "od_w_in", "od_w_out", "s5_lam_re", "s5_lam_im", "s5_log_step", "s5_b_re", "s5_b_im",
          "s5_c_re", "s5_c_im", "s5_d", "s5_glu_w", "s5_glu_b", "ret_norm_g")


def kernel(**inputs):
    import concourse.bacc as bacc
    from concourse.bass_utils import run_bass_kernel_spmd

    arrays = {f"in_{n}": np.ascontiguousarray(inputs[n]) for n in INPUTS}
    arrays["in_constants"] = constant_table()[1]

    def program(marks, final):
        nc = bacc.Bacc("TRN2", target_bir_lowering=False, num_devices=1)
        A = {n[3:]: nc.dram_tensor(n, a.shape, mybir.dt.from_np(a.dtype), kind="ExternalInput").ap()
             for n, a in arrays.items()}
        A["out"] = nc.dram_tensor("out", (1, SEQ, D), F32, kind="ExternalOutput").ap()
        build(nc, A, marks, final)
        return nc

    marks = {}
    program(marks, False)
    nc = program(marks, True)
    got = run_bass_kernel_spmd(nc, [arrays], core_ids=[0])
    return got.results[0]["out"]
```

```python
import math
from contextlib import ExitStack

import numpy as np
import concourse.bass as bass
from concourse import mybir

F32 = mybir.dt.float32
F32R = mybir.dt.float32r
ALU = mybir.AluOpType
ACT = mybir.ActivationFunctionType
AX_X = mybir.AxisListType.X

P = 128
SEQ = 256
TT = SEQ // P
D = 1024
KT = D // P
DEPTH = 2
D_FF = 2816
FB = 256
NB = D_FF // FB
HALF = D // 2
UW = 2048
NSLOT = 3
FFN_UNITS = 3 * NB
ALPHA = (2 * DEPTH) ** 0.25
LN_EPS = 1e-5
LRU_C = 8.0
DA_H, DA_D, DA_ROPE, DA_THETA = 4, 64, 16, 500000.0
RET_H, RET_D, RET_THETA = 4, 64, 10000.0
XA_H, XA_D = 4, 256
S5_TILES = 16
S5_CH = 128
LAMBDA_INIT = 0.8 - 0.6 * math.exp(-0.3 * 0)
NORMS = 4 * DEPTH


class Steps:

    def __init__(self, name, sem, marks, final):
        self.name, self.sem, self.marks, self.final, self.n = name, sem, marks, final, 0

    def up(self, *step):
        self.n += 1
        if step:
            self.marks[(self.name, *step)] = self.n
        return self.sem, 1

    def now(self):
        return self.sem, self.n

    def at(self, *step):
        if self.final:
            return self.sem, self.marks[(self.name, *step)]
        return self.sem, 1


def constant_table():
    p = np.arange(P)
    parts = {"ident": np.eye(P)}
    tri = np.where(p[None, :] <= p[:, None], 0.0, -1e30)
    parts["mask"] = np.concatenate([tri, np.zeros((P, P)), tri], 1)

    def rope(rot, theta, heads):
        half = rot // 2
        inv = np.float32(theta) ** (-np.arange(half, dtype=np.float32) * np.float32(2.0 / rot))
        ang = np.arange(SEQ, dtype=np.float32)[:, None] * inv[None, :].astype(np.float32)
        c, s = np.cos(ang), np.sin(ang)
        c = np.tile(np.concatenate([c, c], 1), (1, heads)).reshape(TT, P, -1).transpose(1, 0, 2)
        s = np.tile(np.concatenate([-s, s], 1), (1, heads)).reshape(TT, P, -1).transpose(1, 0, 2)
        return c.reshape(P, -1), s.reshape(P, -1)

    parts["da_cos"], parts["da_sin"] = rope(DA_ROPE, DA_THETA, 2 * DA_H)
    parts["ret_cos"], parts["ret_sin"] = rope(RET_D, RET_THETA, RET_H)
    gamma = 1.0 - np.exp2(-5.0 - np.arange(RET_H))
    lag = np.arange(SEQ)[None, :] - p[:, None]
    decay = np.where(lag >= 0, np.exp(np.log(gamma)[:, None, None] * np.maximum(lag, 0)), 0.0)
    parts["decay"] = (decay * RET_D ** -0.5).transpose(1, 0, 2).reshape(P, -1)
    parity = (p // 16) % 2
    parts["parity"] = np.stack([parity == 0, parity == 1], 1)
    at, where, cols = 0, {}, []
    for name, a in parts.items():
        where[name] = (at, a.shape[1])
        at += a.shape[1]
        cols.append(np.asarray(a, np.float32))
    return where, np.ascontiguousarray(np.concatenate(cols, 1))


def unit_table():
    first, u = {}, 0

    def phase(key, n):
        nonlocal u
        first[key] = u
        u += n

    def blocks(kind, cols):
        for c in cols:
            phase((kind, c), 2)

    phase(("ffn", 0), FFN_UNITS)
    blocks(("kv", 0), [0])
    blocks("ev_in", [4, 3, 0, 1, 2])
    blocks(("kv", 0), [1, 2])
    blocks("ev_out", [0, 1])
    blocks(("kv", 0), [3])
    blocks(("xq", 0), [0, 1])
    blocks(("xo", 0), [0, 1])
    blocks(("kv", 1), [0])
    phase(("ffn", 1), FFN_UNITS)
    blocks(("kv", 1), [1])
    phase(("ffn", 2), FFN_UNITS)
    blocks(("kv", 1), [2])
    blocks("od_in", [0, 1])
    blocks(("kv", 1), [3])
    blocks("od_in", [2, 3])
    phase("glu", 1)
    blocks("od_out", [0, 1])
    blocks(("xq", 1), [0, 1])
    blocks(("xo", 1), [0, 1])
    phase(("ffn", 3), FFN_UNITS)
    return first, u


def build(nc, A, marks, final):
    ctx = ExitStack()
    with ctx:
        write_program(nc, ctx, A, marks, final)


def write_program(nc, ctx, A, marks, final):
    def sb(name, shape, dt=F32, to=ctx):
        return to.enter_context(nc.sbuf_tensor(name, shape, dt))

    def sem(name):
        return ctx.enter_context(nc.semaphore(name))

    def steps(name):
        return Steps(name, sem(name), marks, final)

    first, n_units = unit_table()
    where, _ = constant_table()
    n_const = sum(n for _, n in where.values())

    raw = sb("raw", [P, NSLOT, UW])
    w_hi = sb("w_hi", [P, NSLOT, UW], F32R)
    w_lo = sb("w_lo", [P, NSLOT, UW], F32R)
    x = sb("x", [P, TT, D])
    ax = sb("ax", [P, TT, D])
    xT_hi = sb("xT_hi", [P, KT, SEQ], F32R)
    xT_lo = sb("xT_lo", [P, KT, SEQ], F32R)
    zero_r = sb("zero_r", [P, P], F32R)
    k_mem = sb("k_mem", [P, KT, SEQ])
    v_mem = sb("v_mem", [P, TT, D])
    gb = sb("gb", [P, 2, D])
    const = sb("const", [P, n_const])
    act_h = sb("act_h", [P, TT, FB])
    hid = sb("hid", [P, TT, FB])
    hT_hi = sb("hT_hi", [P, 2, SEQ], F32R)
    hT_lo = sb("hT_lo", [P, 2, SEQ], F32R)
    tk = sb("tk", [P, 2, TT, HALF])
    pv = sb("pv", [P, 4, 10])
    da_g = sb("da_g", [P, 2 * DA_D])
    ret_g = sb("ret_g", [P, P])
    sm = sb("sm", [P, 96])
    bn = sb("bn", [P, TT, 12])
    mv = sb("mv", [P, TT, 4])
    nat = tk[0:16, 1, :, :].rearrange("p a b -> p (a b)")[:, 0:896]

    da_sm = sb("da_sm", [P, DA_H, 12])
    s5_small = sb("s5_small", [P, 12, S5_TILES])
    rot_tmp = v_mem[:, 0, 0:2 * P].rearrange("p (a b) -> p a b", a=2)

    def s5_par(n):
        return s5_small[:, n, :]

    memory = ExitStack()
    memT_hi = sb("memT_hi", [P, KT, SEQ], F32R, memory)
    memT_lo = sb("memT_lo", [P, KT, SEQ], F32R, memory)
    with ExitStack() as own:
        xrT = sb("xrT", [P, 4, SEQ + 3], F32, own)
        conv = sb("conv", [P, 4, SEQ], F32, own)
        lru_a = sb("lru_a", [P, 4, SEQ], F32, own)
        lru_b = sb("lru_b", [P, 4, SEQ], F32, own)
        gateT = sb("gateT", [P, 4, SEQ], F32, own)
        kT_da = sb("kT_da", [P, DA_H, SEQ], F32, own)
    qT_da = k_mem[:, 4:8, :]
    v_da = v_mem[:, :, HALF:D]
    with ExitStack() as own:
        q_x = sb("q_x", [P, KT, SEQ], F32, own)
        p_x = sb("p_x", [P, 2, TT, SEQ], F32, own)
        pT_x = sb("pT_x", [P, 2, TT, SEQ], F32, own)
    with ExitStack() as own:
        e_cos = sb("e_cos", [P, S5_TILES, S5_CH], F32, own)
        e_sin = sb("e_sin", [P, S5_TILES, S5_CH], F32, own)
        s5_bT = sb("s5_bT", [P, 2, 4, P], F32, own)
        s5_cT = sb("s5_cT", [P, 2, 4, P], F32, own)
        uT = sb("uT", [P, 4, SEQ], F32, own)
        qkT = sb("qkT", [P, 2, 2, SEQ], F32, own)
    memory.close()
    with ExitStack() as own:
        s5_g = sb("s5_g", [P, 2, 2, SEQ], F32, own)
        s5_t = sb("s5_t", [P, 2, 2, SEQ], F32, own)
        s5_h = sb("s5_h", [P, 2, 2, SEQ], F32, own)
        osb = sb("osb", [P, TT, HALF], F32, own)

    gw = act_h[:, :, :].rearrange("p a b -> p (a b)"), hid[:, :, :].rearrange("p a b -> p (a b)")
    gw = [g.rearrange("p (t c) -> p t c", t=4) for g in gw]

    def k_(name):
        a, n = where[name]
        return const[:, a:a + n]

    ident = k_("ident")
    banks = [ctx.enter_context(nc.psum_tensor(f"bank{i}", [P, 512], F32)) for i in range(8)]
    ACC, GU, TR = (0, 2), (4, 5), (6, 7)
    XQ_RIGHT = (2, 3)
    GLU = (2, 3)
    RET_S = (2, 3, 0, 1)
    S5_IN = (2, 3, 6, 7)
    XT = ((6, 7), (0, 1))

    raw_in = [sem(f"raw_in{s}") for s in range(NSLOT)]
    hi_done, lo_done, unit_done = sem("hi_done"), sem("lo_done"), sem("unit_done")
    gu_full, silu_done, h_done = sem("gu_full"), sem("silu_done"), sem("h_done")
    h_turned, h_hi, h_lo = sem("h_turned"), sem("h_hi"), sem("h_lo")
    loaded = {n: sem(f"in_{n}") for n in ("const", "x", "mem", "nat", "rows", "gates", "gb", "x1", "tables", "s5")}
    zeroed = steps("zeroed")
    gate_zero = steps("gate_zero")
    pe_half = steps("pe_half")
    pe_turn = steps("pe_turn")
    pe_core = steps("pe_core")
    act_ln = steps("act_ln")
    act_out = steps("act_out")
    act_hi = steps("act_hi")
    act_core = steps("act_core")
    dve_ln = steps("dve_ln")
    dve_out = steps("dve_out")
    dve_lo = steps("dve_lo")
    dve_core = steps("dve_core")
    pool_core = steps("pool_core")
    out_done = sem("out_done")

    EARLY = {"ev_out": 1, "od_out": 1, ("xo", 0): 0, ("xo", 1): 0}

    def w3(ring, u, k):
        return ring[:, u % NSLOT, :].rearrange("p (k c) -> p k c", k=k)

    kv_of_norm = {0: (0, 0), 1: (0, 3), 2: (1, 0), 3: (1, 1), 4: (1, 2)}
    norm_units = {
        0: first[("ffn", 0)] + FFN_UNITS - 1, 1: first[("ev_out", 1)] + 1,
        2: first[(("xo", 0), 1)] + 1, 3: first[("ffn", 1)] + FFN_UNITS - 1,
        4: first[("ffn", 2)] + FFN_UNITS - 1, 5: first[("od_out", 1)] + 1,
        6: first[(("xo", 1), 1)] + 1, 7: first[("ffn", 3)] + FFN_UNITS - 1}

    after_ffn = (0, 3, 4, 7)

    def xrT_w(h):
        return xrT[:, :, :].rearrange("p a b -> p (a b)")[:, (h % 2) * 384:(h % 2) * 384 + 384]

    def wT(h):
        return lru_b[:, :, :].rearrange("p a b -> p (a b)")[:, (h % 2) * 384:(h % 2) * 384 + 384]

    def kT_da_flat(t):
        return kT_da[:, 2 * t:2 * t + 2, :].rearrange("p a b -> p (a b)")

    def scores_sb(h, m):
        if h < 2:
            return x[:, h, m * 384:(m + 1) * 384]
        if h == 2:
            return (act_h, hid)[m][:, :, :].rearrange("p a b -> p (a b)")[:, 0:384]
        return tk[:, 0, m, 0:384]

    def ret_w(h):
        return tk[:, h // 2, h % 2, 0:384]

    s5_neg_c = osb[:, 0, :].rearrange("p (q c) -> p q c", q=4)
    s5_blocks = (uT[:, :, :].rearrange("p a b -> p (a b)"),
                 e_sin[:, :, :].rearrange("p a b -> p (a b)")[:, 0:1024])
    lru_gate = [x[:, g, :].rearrange("p (t k) -> p t k", t=4) for g in range(2)]
    ret_v = x[:, 0, :].rearrange("p (t d) -> p t d", t=TT)
    ret_gate = x[:, 1, :].rearrange("p (t d) -> p t d", t=TT)
    s5_y = [act_h[:, :, :], hid[:, :, :]]

    def loops(within):
        a = 0
        for b, work in within or ():
            yield a, b, work
            a = b
        yield a, NB - 2, None

    def split_bank(name, t, half):
        return TR[t] if name in ("a_out", "d_out") else XT[t][half]

    def end_of(key, t):
        name, u = key
        return pe_half.at(*name) if t == 0 else (unit_done, u + 2)

    block = ctx.enter_context(nc.Block())

    @block.sync
    def _(sp):
        sp.dma_start(ident, A["constants"][:, 0:P]).then_inc(loaded["const"], 16)
        sp.dma_start(x[:, 0, :], A["x"][0, 0:P, :]).then_inc(loaded["x"], 16)

        def room(u):
            if u >= NSLOT:
                sp.wait_ge(lo_done, u - NSLOT + 1)

        def columns(w, u):
            for half in range(2):
                room(u + half)
                for j in range(2):
                    r0 = half * HALF + j * 256
                    sp.dma_start(w3(raw, u + half, 4)[:, 2 * j:2 * j + 2, :],
                                 w[r0:r0 + 256, :].rearrange("(k p) c -> p k c", p=P)
                                 ).then_inc(raw_in[(u + half) % NSLOT], 16)

        def gate_up(wg, wu, u, b, wait):
            for half in range(2):
                if wait is not None:
                    sp.wait_ge(lo_done, wait + half)
                for j, w in enumerate((wg, wu)):
                    sp.dma_start(w3(raw, u + half, 4)[:, :, j * FB:(j + 1) * FB], w[b, half]
                                 ).then_inc(raw_in[(u + half) % NSLOT], 16)

        def down(wd, u, b, wait):
            sp.wait_ge(lo_done, wait)
            for j in range(2):
                sp.dma_start(w3(raw, u, 2)[:, j, :], wd[b, j]).then_inc(raw_in[u % NSLOT], 16)

        def ffn(f):
            l, j = f // 2, f % 2
            wg, wu = (A[n][l, j].rearrange("(h k p) (b c) -> b h p k c", p=P, k=4, c=FB)
                      for n in ("ffn_w_gate", "ffn_w_up"))
            wd = A["ffn_w_down"][l, j].rearrange("(b k p) c -> b k p c", p=P, k=2)
            u = first[("ffn", f)]
            gate_up(wg, wu, u, 0, u - NSLOT + 1 if u else None)
            with sp.Fori(0, NB - 1) as i:
                for half in range(2):
                    if u or half:
                        sp.wait_ge(lo_done, i * 3 + (u + 2 + half - NSLOT + 1))
                    else:
                        sp.wait_ge(lo_done, i * 3 + 1)
                    for q, w in enumerate((wg, wu)):
                        sp.dma_start(w3(raw, u + 2 + half, 4)[:, :, q * FB:(q + 1) * FB], w[i + 1, half]
                                     ).then_inc(raw_in[(u + 2 + half) % NSLOT], 16)
                down(wd, u + 4, i, i * 3 + (u + 4 - NSLOT + 1))
            down(wd, u + FFN_UNITS - 1, NB - 1, u + FFN_UNITS - NSLOT)

        def out_columns(name, l, kind):
            for n in range(4):
                half, c = EARLY[kind] ^ (n // 2), n % 2
                u = first[(kind, 0)] + n
                room(u)
                for j in range(2):
                    r0 = half * HALF + j * 256
                    sp.dma_start(w3(raw, u, 4)[:, 2 * j:2 * j + 2, :],
                                 cols_of(name, l, c)[r0:r0 + 256, :].rearrange("(k p) c -> p k c", p=P)
                                 ).then_inc(raw_in[u % NSLOT], 16)

        def cols_of(name, l, c):
            return A[name][l][:, c * 512:(c + 1) * 512]

        def kv(l, c):
            columns(cols_of("xa_w_kv", l, c), first[(("kv", l), c)])

        def cross(l):
            for c in range(2):
                columns(cols_of("xa_w_q", l, c), first[(("xq", l), c)])
            out_columns("xa_w_o", l, ("xo", l))

        ffn(0)
        kv(0, 0)
        for c in (4, 3, 0, 1, 2):
            columns(cols_of("ev_w_in", 0, c), first[("ev_in", c)])
        kv(0, 1)
        kv(0, 2)
        out_columns("ev_w_out", 0, "ev_out")
        kv(0, 3)
        cross(0)
        kv(1, 0)
        ffn(1)
        kv(1, 1)
        ffn(2)
        kv(1, 2)
        for c in range(2):
            columns(cols_of("od_w_in", 0, c), first[("od_in", c)])
        kv(1, 3)
        for c in range(2, 4):
            columns(cols_of("od_w_in", 0, c), first[("od_in", c)])
        u = first["glu"]
        room(u)
        for j in range(2):
            sp.dma_start(w3(raw, u, 4)[:, 2 * j:2 * j + 2, :],
                         A["s5_glu_w"][0][j * 256:(j + 1) * 256, :].rearrange("(k p) c -> p k c", p=P)
                         ).then_inc(raw_in[u % NSLOT], 16)
        out_columns("od_w_out", 0, "od_out")
        cross(1)
        ffn(3)
        for t in range(TT):
            sp.wait_ge(*dve_ln.at("x", NORMS - 1, t))
            sp.dma_start(A["out"][0, t * P:(t + 1) * P, :], x[:, t, :]).then_inc(out_done, 16)
        sp.wait_ge(out_done, 16 * TT)

    @block.gpsimd
    def _(pool):
        with nc.allow_non_contiguous_dma(reason="rows of parameters"):
            rows = [A["lru_conv_w"][0], A["lru_conv_b"], A["lru_gate_b"][0], A["lru_lambda"], A["s5_d"],
                    A["s5_glu_b"]]
            r = 0
            for a in rows:
                n = a.shape[0]
                pool.dma_start(nat[r:r + n, 0:512], a).then_inc(loaded["nat"], 16)
                r += n
            pool.dma_start(nat[0:16, 512:640], A["s5_lam_re"][0].rearrange("(j g) n -> j (g n)", g=2)
                           ).then_inc(loaded["nat"], 16)
            pool.dma_start(nat[0:16, 640:768], A["s5_lam_im"][0].rearrange("(j g) n -> j (g n)", g=2)
                           ).then_inc(loaded["nat"], 16)
            pool.dma_start(sm[0:16, 90:92], A["s5_log_step"][0].rearrange("(j g) -> j g", g=2)
                           ).then_inc(loaded["nat"], 16)
            pool.dma_start(da_g[:, :], A["da_norm_g"].partition_broadcast(P).rearrange("p a d -> p (a d)")
                           ).then_inc(loaded["rows"], 16)
            pool.dma_start(ret_g[:, :], A["ret_norm_g"].partition_broadcast(P).rearrange("p a d -> p (a d)")
                           ).then_inc(loaded["rows"], 16)
            pool.dma_start(tk[:, 0, 0, 0:256], A["da_lambda"].partition_broadcast(P)
                           .rearrange("p a b d -> p (a b d)")).then_inc(loaded["rows"], 16)

        def norm_rows(i):
            l, j = i // 4, i % 4
            pool.dma_start(gb[:, 0, :], A["ln_g"][l, j].partition_broadcast(P)).then_inc(loaded["gb"], 16)
            pool.dma_start(gb[:, 1, :], A["ln_b"][l, j].partition_broadcast(P)).then_inc(loaded["gb"], 16)

        pool.dma_start(ax[:, :, :], A["mem"][0].rearrange("(t p) d -> p t d", p=P)).then_inc(loaded["mem"], 16)
        norm_rows(0)
        pool.dma_start(const[:, P:n_const], A["constants"][:, P:n_const]).then_inc(loaded["tables"], 16)
        for i in range(NORMS - 1):
            if i not in after_ffn and i not in kv_of_norm:
                w = norm_units[i] + 2
                pool.wait_ge(hi_done, w + 1)
                pool.wait_ge(lo_done, w)
                pool.tensor_tensor(w_lo[:, w % NSLOT, :], raw[:, w % NSLOT, :], w_hi[:, w % NSLOT, :].bitcast(F32),
                                   ALU.subtract).then_inc(lo_done, 1)
            for t in range(TT):
                pool.wait_ge(*dve_ln.at("x", i, t))
            norm_rows(i + 1)
            if i == 0:
                for g in range(2):
                    pool.memset(gw[g], 0.0).then_inc(*gate_zero.up())
                pool.wait_ge(*gate_zero.now())
                with nc.allow_non_contiguous_dma(reason="64-float rows"):
                    for g in range(2):
                        for b in range(2):
                            src = A["lru_gate_w"][0, g].rearrange("(t b) c d -> b c t d", b=2)[b]
                            pool.dma_start(gw[g][64 * b:64 * b + 64, :, 64 * b:64 * b + 64], src
                                           ).then_inc(loaded["gates"], 16)
            if i == 2:
                with nc.allow_non_contiguous_dma(reason="16-float rows"):
                    for ri, n in enumerate(("s5_b_re", "s5_b_im")):
                        pool.dma_start(qkT[:, ri, 0, :].rearrange("p (j c) -> p j c", c=16),
                                       A[n][0].rearrange("(j g) n c -> (g n) j c", g=2)).then_inc(loaded["s5"], 16)
                    for ri, n in enumerate(("s5_c_re", "s5_c_im")):
                        pool.dma_start(qkT[:, ri, 1, :].rearrange("p (q n) -> p q n", n=64),
                                       A[n][0].rearrange("(q g) c n -> (g c) q n", g=8)).then_inc(loaded["s5"], 16)
            if i == 3:
                pool.wait_ge(*dve_core.at("theta"))
                pool.wait_ge(*pe_turn.at("s5_c", 1))
                n = 1
                while n < S5_CH:
                    sc = uT[:, :, :].rearrange("p a b -> p (a b)")[:, 0:16 * n].rearrange("p (j k) -> p j k", k=n)
                    ss = qkT[:, :, :, :].rearrange("p a b c -> p (a b c)")[:, 0:16 * n].rearrange(
                        "p (j k) -> p j k", k=n)
                    cl = e_cos[:, :, n - 1:n].to_broadcast([P, 16, n])
                    sl = e_sin[:, :, n - 1:n].to_broadcast([P, 16, n])
                    c0, s0 = e_cos[:, :, 0:n], e_sin[:, :, 0:n]
                    c1, s1 = e_cos[:, :, n:2 * n], e_sin[:, :, n:2 * n]
                    for a, b, c, d, out, op in ((c0, cl, s0, sl, c1, ALU.subtract), (s0, cl, c0, sl, s1, ALU.add)):
                        pool.tensor_tensor(sc, a, b, ALU.mult).then_inc(*pool_core.up())
                        pool.tensor_tensor(ss, c, d, ALU.mult).then_inc(*pool_core.up())
                        pool.wait_ge(*pool_core.now())
                        pool.tensor_tensor(out, sc, ss, op).then_inc(*pool_core.up("powers"))
                        pool.wait_ge(*pool_core.now())
                    n *= 2
            if i == 4:
                for j in range(S5_TILES):
                    pool.wait_ge(*dve_core.at("s5_g", j))
                    if j >= 2:
                        pool.wait_ge(*pe_core.at("s5_y", j - 2))
                    g = s5_g[:, j % 2]
                    for e, out in ((e_cos, s5_h), (e_sin, s5_t)):
                        pool.tensor_tensor(out[:, j % 2].rearrange("p r (c k) -> p r c k", k=S5_CH),
                                           g.rearrange("p r (c k) -> p r c k", k=S5_CH),
                                           e[:, j, :].unsqueeze(1).unsqueeze(1).to_broadcast([P, 2, 2, S5_CH]),
                                           ALU.mult).then_inc(*pool_core.up("s5_h", j))

    @block.tensor
    def _(pe):
        emptied = {}

        def take(b):
            for who, step in emptied.pop(b, ()):
                pe.wait_ge(*who.at(*step))

        def three(out, lh, ll, rh, rl, start, stop):
            pe.matmul(out, lh, rh, start=start, stop=False)
            pe.matmul(out, lh, rl, start=False, stop=False)
            return pe.matmul(out, ll, rh, start=False, stop=stop)

        def column_part(u, t, half, sh, sl, dst, key, need=None, steps_k=range(4)):
            if t == 0:
                pe.wait_ge(lo_done, u + 1)
            if need:
                for who, step in need(t, half):
                    pe.wait_ge(*who.at(*step))
            wh, wl = w3(w_hi, u, 4), w3(w_lo, u, 4)
            for k in steps_k:
                kk = 4 * half + k
                mm = three(banks[dst[t]][:, :], sh[:, kk, t * P:(t + 1) * P], sl[:, kk, t * P:(t + 1) * P],
                           wh[:, k, :], wl[:, k, :], kk == 0, kk == KT - 1)
            if 3 not in steps_k:
                return
            if t == 1:
                mm.then_inc(unit_done, 1)
            elif half == 1:
                mm.then_inc(*pe_half.up(*key))

        def column_block(key, u, sh, sl, dst, readers=None, need=None, between=None):
            for t in range(TT):
                take(dst[t])
                for half in range(2):
                    column_part(u + half, t, half, sh, sl, dst, key, need)
                    if between and (t, half) in between:
                        between[t, half]()
            if readers:
                for t in range(TT):
                    emptied[dst[t]] = [(who, (*step, t)) for who, step in readers]

        def gate_up_part(u, t, half):
            wh, wl = w3(w_hi, u + half, 4), w3(w_lo, u + half, 4)
            for k in range(4):
                kk = 4 * half + k
                mm = three(banks[GU[t]][:, :], xT_hi[:, kk, t * P:(t + 1) * P], xT_lo[:, kk, t * P:(t + 1) * P],
                           wh[:, k, :], wl[:, k, :], kk == 0, kk == KT - 1)
            if t == 1:
                mm.then_inc(unit_done, 1)
            elif half == 1:
                mm.then_inc(gu_full, 1)

        def gate_up_first(u, free, need, between):
            for t in range(TT):
                if free is not None:
                    pe.wait_ge(h_done, free + t)
                for half in range(2):
                    if t == 0:
                        pe.wait_ge(lo_done, u + half + 1)
                    for who, step in need(t, half):
                        pe.wait_ge(*who.at(*step))
                    gate_up_part(u, t, half)
                if t == 0 and between:
                    between()

        def gate_up_block(u, split, free):
            for half in range(2):
                pe.wait_ge(lo_done, split + half)
                for t in range(TT):
                    if half == 0:
                        pe.wait_ge(h_done, free + t)
                    gate_up_part(u, t, half)

        def down_part(u, t, hi, lo, key=None):
            wh, wl = w3(w_hi, u, 2), w3(w_lo, u, 2)
            for c in range(2):
                for k in range(2):
                    mm = three(banks[ACC[t] + c][:, :], hi[:, k, t * P:(t + 1) * P], lo[:, k, t * P:(t + 1) * P],
                               wh[:, k, c * 512:(c + 1) * 512], wl[:, k, c * 512:(c + 1) * 512], False,
                               bool(key) and k == 1)
                if key and (t, c) != (1, 1):
                    mm.then_inc(*pe_half.up(*key, t, c))
            return mm

        def turn_hidden(t, ready, free):
            pe.wait_ge(h_done, ready + t)
            if free is not None:
                pe.wait_ge(h_lo, free + t)
            for k in range(2):
                mm = pe.transpose(banks[TR[t]][:, k * P:(k + 1) * P], hid[:, t, k * P:(k + 1) * P], ident)
            mm.then_inc(h_turned, 1)

        def ffn(f, need, between=None, interlude=None):
            u, n = first[("ffn", f)], 2 * NB * f
            for b in GU:
                take(b)
            gate_up_first(u, n - 1 if f else None, need, between)
            if interlude:
                interlude()
            for t in range(TT):
                take(TR[t])
                turn_hidden(t, n + 1, n - 1 if f else None)
            for c in range(2):
                for t in range(TT):
                    take(ACC[t] + c)
                    pe.matmul(banks[ACC[t] + c][:, :], zero_r[:, :], xT_hi[:, 0:2, :], start=True, stop=False)
            with pe.Fori(0, NB - 2) as i:
                gate_up_block(u + 2, i * 3 + (u + 3), i * 2 + (n + 1))
                pe.wait_ge(lo_done, i * 3 + (u + 5))
                pe.wait_ge(h_lo, i * 2 + (n + 2))
                for t in range(TT):
                    mm = down_part(u + 4, t, hT_hi, hT_lo)
                mm.then_inc(unit_done, 1)
                for t in range(TT):
                    turn_hidden(t, i * 2 + (n + 3), i * 2 + (n + 1))
            b = NB - 1
            d0, d1 = u + 3 * NB - 2, u + 3 * NB - 1
            gate_up_block(u + 3 * b - 1, u + 3 * b, n + 2 * b - 1)
            turn_hidden(0, n + 2 * b + 1, n + 2 * b - 1)
            pe.wait_ge(lo_done, d0 + 1)
            pe.wait_ge(h_lo, n + 2 * b)
            down_part(d0, 0, hT_hi, hT_lo)
            turn_hidden(1, n + 2 * b + 1, n + 2 * b - 1)
            pe.wait_ge(lo_done, d1 + 1)
            pe.wait_ge(h_lo, n + 2 * b + 1)
            down_part(d1, 0, xT_hi, xT_lo, ("acc", f))
            down_part(d0, 1, hT_hi, hT_lo).then_inc(unit_done, 1)
            pe.wait_ge(h_lo, n + 2 * b + 2)
            down_part(d1, 1, xT_hi, xT_lo, ("acc", f)).then_inc(unit_done, 1)

        def turn(name, src, ready, bank, reader, n=4):
            for who, step in ready:
                pe.wait_ge(*who.at(*step))
            take(bank)
            for j in range(n):
                mm = pe.transpose(banks[bank][:, j * P:(j + 1) * P], src[:, j * P:(j + 1) * P], ident)
            mm.then_inc(*pe_turn.up(*name))
            emptied[bank] = reader

        def turn_split(name, t, half, src, ready):
            turn((name, t, half), src, ready, split_bank(name, t, half), [(dve_lo, (name, t, half))])

        def turn_out(name, src, who=act_out):
            for t in range(TT):
                turn((name, t), src[:, t, :], [(who, (name, t))], TR[t], [(dve_out, (name, t))])

        def kv_block(l, c, dst=GU, between=None):
            name = ("kv", l, c)
            column_block(name, first[(("kv", l), c)], memT_hi, memT_lo, dst, [(act_out, (name,))],
                         lambda t, half: [(dve_lo, ("mem", t, half))], between)

        def turn_x(i, t):
            for half in range(2):
                turn_split(("x", i), t, half, x[:, t, half * HALF:(half + 1) * HALF], [(dve_ln, ("x", i, t))])

        def norm(i):
            for t in range(TT):
                for c in range(2):
                    emptied[ACC[t] + c] = [(dve_ln, ("sum", i, t, c))]
            kv = kv_of_norm.get(i)
            if not kv:
                turn_x(i, 0)
                return lambda: turn_x(i, 1)
            kv_block(*kv, between={(0, 1): lambda: turn_x(i, 0)})

            def between():
                turn_x(i, 1)
                if kv[1] < 2:
                    turn_out(("kv", *kv), tk[:, kv[1] % 2])

            return between

        def x_ready(i):
            return lambda t, half: [(dve_lo, (("x", i), t, half))]

        def out_part(kind, n, t, c):
            u = first[(kind, 0)] + 2 * n + c
            half = EARLY[kind] ^ n
            wh, wl = w3(w_hi, u, 4), w3(w_lo, u, 4)
            for k in range(4):
                kk = 4 * half + k
                mm = three(banks[ACC[t] + c][:, :], xT_hi[:, kk, t * P:(t + 1) * P], xT_lo[:, kk, t * P:(t + 1) * P],
                           wh[:, k, :], wl[:, k, :], n == 0 and k == 0, n == 1 and k == 3)
            return mm

        def out_early(kind, c, need, tiles=range(TT)):
            pe.wait_ge(lo_done, first[(kind, 0)] + c + 1)
            for t in tiles:
                for who, step in need(t):
                    pe.wait_ge(*who.at(*step))
                take(ACC[t] + c)
                mm = out_part(kind, 0, t, c)
            if t == 1:
                mm.then_inc(unit_done, 1)

        def out_late(kind, need):
            for t in range(TT):
                for who, step in need(t):
                    pe.wait_ge(*who.at(*step))
                for c in range(2):
                    if t == 0:
                        pe.wait_ge(lo_done, first[(kind, 0)] + 2 + c + 1)
                    mm = out_part(kind, 1, t, c)
                    if t == 0:
                        mm.then_inc(*pe_half.up(kind, c))
                    else:
                        mm.then_inc(unit_done, 1)

        def even_mixer(need, between):
            nm = {4: "xr", 3: "gate", 0: "q", 1: "k", 2: "v"}

            def project(c, dst, **first_one):
                column_block(("ev", c), first[("ev_in", c)], xT_hi, xT_lo, dst, [(act_out, (nm[c],))], **first_one)

            project(4, (4, 5), need=need, between={(0, 1): between} if between else None)
            project(3, (0, 1))
            turn_out("xr", tk[:, 0])
            project(0, (2, 3))
            pe.wait_ge(loaded["gates"], 64)
            pe.wait_ge(*dve_core.at("conv"))
            for g in range(2):
                for t2 in range(2):
                    take(TR[t2])
                    for j in range(2):
                        tile = 2 * t2 + j
                        mm = pe.matmul(banks[TR[t2]][:, j * SEQ:(j + 1) * SEQ], gw[g][:, tile, :],
                                       conv[:, tile, :], start=True, stop=True)
                    mm.then_inc(*pe_core.up("gates", g, t2))
                    emptied[TR[t2]] = [(act_core, ("gates", g, t2))]
            turn_out("gate", tk[:, 1])
            project(1, (4, 5))
            turn_out("q", tk[:, 0], dve_core)
            project(2, (0, 1))
            turn_out("k", tk[:, 1], dve_core)
            kv_block(0, 1)

            def scores(h):
                for m in range(2):
                    b = 2 * (h % 2) + m
                    take(b)
                    r = slice(64 * m, 64 * m + 64)
                    pe.matmul(banks[b][:, 0:P], qT_da[r, h, 0:P], kT_da[r, h, 0:P], start=True, stop=True)
                    pe.matmul(banks[b][:, P:3 * P], qT_da[r, h, P:SEQ], kT_da[r, h, :], start=True, stop=True
                              ).then_inc(*pe_core.up("scores", h, m))
                    emptied[b] = [(dve_core, ("masked", h, m))]

            def weights(h):
                b = TR[h % 2]
                pe.wait_ge(*dve_core.at("weights", h))
                take(b)
                for j in range(3):
                    mm = pe.transpose(banks[b][:, j * P:(j + 1) * P], xrT_w(h)[:, j * P:(j + 1) * P], ident)
                mm.then_inc(*pe_turn.up("weights", h))
                emptied[b] = [(act_core, ("wT", h))]

            def values(h):
                pe.wait_ge(*act_core.at("wT", h))
                w = wT(h)
                c = slice(h * P, (h + 1) * P)
                if h == 0:
                    take(4)
                    take(5)
                pe.matmul(banks[4][:, c], w[:, 0:P], v_da[:, 0, c], start=True, stop=True)
                pe.matmul(banks[5][:, c], w[:, P:2 * P], v_da[:, 0, c], start=True, stop=False)
                pe.matmul(banks[5][:, c], w[:, 2 * P:3 * P], v_da[:, 1, c], start=False, stop=True
                          ).then_inc(*pe_core.up("o", h))

            for n in ("q", "k"):
                for t in range(TT):
                    pe.wait_ge(*dve_out.at(n, t))
            for t in range(TT):
                pe.wait_ge(*act_out.at("v", t))
            scores(0)
            scores(1)

            def other_heads():
                scores(2)
                scores(3)
                weights(0)
                weights(1)

            kv_block(0, 2, between={(0, 1): other_heads})
            turn_out(("kv", 0, 1), tk[:, 1])
            for h in range(DA_H):
                values(h)
                if h + 2 < DA_H:
                    weights(h + 2)
            for t in range(TT):
                emptied[4 + t] = [(dve_core, ("a_out", t))]
            out_early("ev_out", 0, lambda t: [(dve_lo, ("b_out",))])
            for t in range(TT):
                turn_split("a_out", t, 0, kT_da_flat(t), [(dve_core, ("a_out", t))])
            out_early("ev_out", 1, lambda t: [(dve_lo, ("b_out",))])
            out_late("ev_out", lambda t: [(dve_lo, ("a_out", t, 0))])

        def cross(l, need, between):
            def scores(h):
                b = h
                take(b)
                for t in range(TT):
                    for j in range(2):
                        mm = pe.matmul(banks[b][:, t * SEQ:(t + 1) * SEQ], q_x[:, 2 * h + j, t * P:(t + 1) * P],
                                       k_mem[:, 2 * h + j, :], start=(j == 0), stop=(j == 1))
                mm.then_inc(*pe_core.up("xs", l, h))
                emptied[b] = [(act_core, ("xp", l, h))]

            def weights(h):
                b = TR[h % 2]
                pe.wait_ge(*dve_core.at("xw", l, h))
                take(b)
                for mt in range(2):
                    for t in range(TT):
                        mm = pe.transpose(banks[b][:, mt * SEQ + t * P:mt * SEQ + (t + 1) * P],
                                          p_x[:, h % 2, t, mt * P:(mt + 1) * P], ident)
                mm.then_inc(*pe_turn.up("xw", l, h))
                emptied[b] = [(act_core, ("xpT", l, h))]

            def values(h):
                pe.wait_ge(*act_core.at("xpT", l, h))
                b = GU[h % 2]
                take(b)
                for j in range(2):
                    for mt in range(2):
                        c0 = h * XA_D + j * P
                        mm = pe.matmul(banks[b][:, j * SEQ:(j + 1) * SEQ], v_mem[:, mt, c0:c0 + P],
                                       pT_x[:, h % 2, mt, :], start=(mt == 0), stop=(mt == 1))
                mm.then_inc(*pe_core.up("xo", l, h))
                emptied[b] = [(dve_lo, ("xo", l, h))]

            def first_heads():
                for t in range(TT):
                    pe.wait_ge(*dve_out.at(("xq", l, 0), t))
                scores(0)
                scores(1)

            column_block(("xq", l, 0), first[(("xq", l), 0)], xT_hi, xT_lo, GU, [(act_out, (("xq", l, 0),))], need,
                         {(0, 1): between} if between else None)
            column_block(("xq", l, 1), first[(("xq", l), 1)], xT_hi, xT_lo, XQ_RIGHT,
                         [(act_out, (("xq", l, 1),))],
                         between={(0, 0): lambda: turn_out(("xq", l, 0), tk[:, 0]), (1, 0): first_heads})
            turn_out(("xq", l, 1), tk[:, 1])
            for t in range(TT):
                pe.wait_ge(*act_out.at(("kv", l, 3), t))
            for t in range(TT):
                pe.wait_ge(*dve_out.at(("xq", l, 1), t))
                pe.wait_ge(*act_out.at(("kv", l, 2), t))
            for h in range(XA_H):
                if h < 2:
                    scores(h + 2)
                weights(h)
                if h == 2:
                    out_early(("xo", l), 0, lambda t: [(dve_lo, ("xo", l, 1))])
                elif h == 3:
                    out_early(("xo", l), 1, lambda t: [], (0,))
                values(h)
            out_early(("xo", l), 1, lambda t: [], (1,))
            out_late(("xo", l), lambda t: [(dve_lo, ("xo", l, 3))])

        def s5_prepare():
            for kind, n in (("s5_b", 0), ("s5_c", 1)):
                for ri in range(2):
                    src = s5_blocks[n][:, ri * 512:(ri + 1) * 512]
                    turn((kind, ri), src, [(dve_core, (kind, ri))], XT[n][ri], [(dve_core, (kind + "T", ri))])

        def odd_mixer(need, between):
            nm = {0: "u", 1: "qk", 2: "rv", 3: "rg"}

            def project(c, dst, **first_one):
                column_block(("od", c), first[("od_in", c)], xT_hi, xT_lo, dst, [(act_out, (nm[c],))], **first_one)

            def inputs(j):
                b = S5_IN[j % 4]
                take(b)
                r = slice(32 * (j % 4), 32 * (j % 4) + 32)
                for ri in range(2):
                    mm = pe.matmul(banks[b][:, ri * SEQ:(ri + 1) * SEQ], s5_bT[r, ri, j // 4, :],
                                   uT[r, j // 4, :], start=True, stop=True)
                mm.then_inc(*pe_core.up("s5_x", j))
                emptied[b] = [(dve_core, ("s5_in", j))]

            def outputs(j):
                pe.wait_ge(*pool_core.at("s5_h", j))
                if j == 0:
                    pe.wait_ge(*dve_core.at("s5_neg_c"))
                    take(4)
                    take(5)
                q, r = j // 4, 32 * (j % 4)
                b = j % 2
                terms = ((s5_cT[:, 0], s5_h[:, b, 0]), (s5_neg_c, s5_t[:, b, 1]),
                         (s5_cT[:, 1], s5_t[:, b, 0]), (s5_cT[:, 1], s5_h[:, b, 1]))
                for n, (c, h) in enumerate(terms):
                    mm = pe.matmul(banks[4 + q // 2][r:r + 32, (q % 2) * SEQ:(q % 2 + 1) * SEQ],
                                   c[:, q, r:r + 32], h, start=(n == 0), stop=(n == len(terms) - 1))
                mm.then_inc(*pe_core.up("s5_y", j))

            project(0, (4, 5), need=need, between={(0, 1): between} if between else None)
            project(1, (0, 1))
            turn_out("u", tk[:, 0])
            kv_block(1, 3, (4, 5))
            turn_out("qk", tk[:, 1], dve_core)
            for t in range(TT):
                pe.wait_ge(*dve_out.at("u", t))
            for j in range(4):
                inputs(j)
            def ret_scores(h):
                b = RET_S[h]
                take(b)
                r = slice(64 * (h % 2), 64 * (h % 2) + 64)
                q, k = qkT[r, 0, h // 2, :], qkT[r, 1, h // 2, :]
                pe.matmul(banks[b][:, 0:SEQ], k[:, 0:P], q, start=True, stop=True)
                pe.matmul(banks[b][:, SEQ:SEQ + P], k[:, P:SEQ], q[:, P:SEQ], start=True, stop=True
                          ).then_inc(*pe_core.up("ret_s", h))
                emptied[b] = [(dve_core, ("ret_w", h))]

            parts = [(c, t, half, k) for c in (2, 3) for t in range(TT) for half in range(2) for k in (0, 2)]
            for j, (c, t, half, k) in enumerate(parts):
                if half == 0 and k == 0:
                    take(t)
                column_part(first[("od_in", c)] + half, t, half, xT_hi, xT_lo, (0, 1), ("od", c),
                            steps_k=(k, k + 1))
                emptied[t] = [(act_out, (nm[c], t))]
                if j >= 1 and j + 3 < S5_TILES:
                    inputs(j + 3)
                if j:
                    outputs(j - 1)
            for t in range(TT):
                pe.wait_ge(*dve_out.at("qk", t))
            for h in range(RET_H - 1):
                ret_scores(h)
            outputs(S5_TILES - 1)
            ret_scores(RET_H - 1)
            pe.wait_ge(*dve_core.at("s5_out", 3))
            for h in range(RET_H):
                pe.wait_ge(*dve_core.at("ret_w", h))
                w, v = ret_w(h), ret_v
                c = slice(h * P, (h + 1) * P)
                pe.matmul(banks[4][:, c], w[:, 0:P], v[:, 0, c], start=True, stop=True)
                pe.matmul(banks[5][:, c], w[:, P:SEQ], v[:, 0, c], start=True, stop=False)
                pe.matmul(banks[5][:, c], w[:, SEQ:SEQ + P], v[:, 1, c], start=False, stop=True
                          ).then_inc(*pe_core.up("ret_o", h))

            u = first["glu"]
            pe.wait_ge(lo_done, u + 1)
            pe.wait_ge(*dve_lo.at("z"))
            wh, wl = w3(w_hi, u, 4), w3(w_lo, u, 4)
            for o in range(4):
                if o % 2 == 0:
                    take(GLU[o // 2])
                for k in range(4):
                    c = slice(o * P, (o + 1) * P)
                    mm = three(banks[GLU[o // 2]][:, (o % 2) * SEQ:(o % 2 + 1) * SEQ], wh[:, k, c], wl[:, k, c],
                               xT_hi[:, k, :], xT_lo[:, k, :], k == 0, k == 3)
            mm.then_inc(unit_done, 1)
            for q in range(2):
                emptied[GLU[q]] = [(act_core, ("glu", 3))]

            for t in range(TT):
                emptied[4 + t] = [(dve_core, ("ret_n", t))]
            for t in range(TT):
                turn_split("d_out", t, 1, osb[:, t, :], [(dve_core, ("d_out", t))])
            for c in range(2):
                out_early("od_out", c, lambda t: [(dve_lo, ("d_out", t, 1))])
            out_late("od_out", lambda t: [(dve_lo, ("c_out",))])

        def memory_tokens():
            pe.wait_ge(loaded["nat"], 16 * 9)
            pe.wait_ge(*dve_core.at("log_step"))
            for j in range(4):
                pe.transpose(banks[2][:, 16 * j:16 * j + 10], nat[0:10, j * P:(j + 1) * P], ident[0:10, 0:10])
            for j in range(3):
                mm = pe.transpose(banks[2][:, 64 + 16 * j:80 + 16 * j], nat[0:16, 512 + j * P:512 + (j + 1) * P],
                                  ident[0:16, 0:16])
            mm.then_inc(*pe_turn.up("params"))
            emptied[2] = [(dve_core, ("params",))]
            pe.wait_ge(loaded["mem"], 16)
            for t in range(TT):
                for half in range(2):
                    turn_split("mem", t, half, ax[:, t, half * HALF:(half + 1) * HALF], [])

        def turn_x_in(t):
            pe.wait_ge(loaded["x" if t == 0 else "x1"], 16)
            for half in range(2):
                turn_split("x_in", t, half, x[:, t, half * HALF:(half + 1) * HALF], [])

        pe.wait_ge(loaded["const"], 16)
        pe.wait_ge(*zeroed.at("zero"))
        turn_x_in(0)
        ffn(0, lambda t, half: [(dve_lo, ("x_in", t, half))], lambda: turn_x_in(1), memory_tokens)
        between = norm(0)
        even_mixer(x_ready(0), between)
        between = norm(1)
        cross(0, x_ready(1), between)
        between = norm(2)
        ffn(1, x_ready(2), between)
        between = norm(3)
        ffn(2, x_ready(3), between, s5_prepare)
        between = norm(4)
        odd_mixer(x_ready(4), between)
        between = norm(5)
        cross(1, x_ready(5), between)
        between = norm(6)
        ffn(3, x_ready(6), between)

    @block.scalar
    def _(act):
        split = [0]

        def split_to(u):
            while split[0] <= u:
                v = split[0]
                if v < n_units:
                    act.wait_ge(raw_in[v % NSLOT], 32 * (v // NSLOT + 1))
                    if v >= NSLOT:
                        act.wait_ge(unit_done, v - NSLOT + 1)
                    act.activation(w_hi[:, v % NSLOT, :], raw[:, v % NSLOT, :], ACT.Copy).then_inc(hi_done, 1)
                split[0] += 1

        def ffn(f, interlude=None, within=None):
            u, n = first[("ffn", f)], 2 * NB * f

            def hi(c, i):
                v = u + 2 + c
                act.wait_ge(raw_in[v % NSLOT], i * 32 + 32 * (v // NSLOT + 1))
                act.wait_ge(unit_done, i * 3 + (v - NSLOT + 1))
                act.activation(w_hi[:, v % NSLOT, :], raw[:, v % NSLOT, :], ACT.Copy).then_inc(hi_done, 1)

            def silu(t, full0, full1, free):
                if t == 0:
                    act.wait_ge(gu_full, full0)
                else:
                    act.wait_ge(unit_done, full1)
                if free is not None:
                    act.wait_ge(h_done, free + t)
                act.activation(act_h[:, t, :], banks[GU[t]][:, 0:FB], ACT.Silu).then_inc(silu_done, 1)

            def hidden_hi(t, ready, dst):
                act.wait_ge(h_turned, ready + t)
                act.activation(dst[:, 0:2, t * P:(t + 1) * P],
                               banks[TR[t]][:, 0:2 * P].rearrange("p (k c) -> p k c", k=2), ACT.Copy
                               ).then_inc(h_hi, 1)

            split_to(u + 2)
            for t in range(TT):
                silu(t, NB * f + 1, u + 2, n - 1 if f else None)
            if interlude:
                interlude()
            for a, b, work in loops(within):
                with act.Fori(a, b) as i:
                    for t in range(TT):
                        hidden_hi(t, i * 2 + (n + 1), hT_hi)
                    hi(1, i)
                    hi(2, i)
                    for t in range(TT):
                        silu(t, i + (NB * f + 2), i * 3 + (u + 4), i * 2 + (n + 1))
                    hi(3, i)
                if work:
                    work()
            b = NB - 1
            for t in range(TT):
                hidden_hi(t, n + 2 * b - 1, hT_hi)
            split[0] = u + 3 * b
            split_to(u + 3 * b + 2)
            silu(0, NB * f + NB, None, n + 2 * b - 1)
            silu(1, None, u + 3 * b + 1, n + 2 * b - 1)
            hidden_hi(0, n + 2 * b + 1, xT_hi)
            hidden_hi(1, n + 2 * b + 1, xT_hi)

        def split_operand(name, t, half, dst=None):
            act.wait_ge(*pe_turn.at(name, t, half))
            dst = xT_hi if dst is None else dst
            act.activation(dst[:, 4 * half:4 * half + 4, t * P:(t + 1) * P],
                           banks[split_bank(name, t, half)][:, :].rearrange("p (k c) -> p k c", k=4), ACT.Copy
                           ).then_inc(*act_hi.up(name, t, half))

        def copy_out(name, key, u, dst, bank, fn=ACT.Copy, free=None):
            split_to(u + 3)
            if free is not None:
                for t in range(TT):
                    act.wait_ge(*pe_turn.at(free, t))
            for t in range(TT):
                act.wait_ge(*end_of((key, u), t))
                act.activation(dst[:, t, :], banks[bank[t]][:, :], fn).then_inc(*act_out.up(name, t))

        def kv_out(l, c, bank=GU, free=None):
            name = ("kv", l, c)
            u = first[(("kv", l), c)]
            if c < 2:
                copy_out(name, name, u, tk[:, c % 2], bank, free=free)
            else:
                copy_out(name, name, u, v_mem[:, :, (c - 2) * HALF:(c - 1) * HALF], bank)

        def norm(i, last=False, free=None):
            e = norm_units[i]

            def deviation(t):
                act.wait_ge(*dve_ln.at("var", i, t))
                act.activation(mv[:, t, 2:3], mv[:, t, 1:2], ACT.Sqrt, bias=eps_col).then_inc(*act_ln.up("sd", i, t))

            def operand(t):
                for half in range(2):
                    split_operand(("x", i), t, half)

            def scaled(t):
                act.wait_ge(*dve_ln.at("x", i, t))
                act.activation(ax[:, t, :], x[:, t, :], ACT.Copy, scale=ALPHA).then_inc(*act_ln.up("ax", i, t))

            kv = kv_of_norm.get(i)
            split_to(e + 1)
            if i in after_ffn:
                split_to(e + 2)
                deviation(0)
            else:
                deviation(0)
                split_to(e + 2)
                if not kv:
                    operand(0)
            if kv:
                split_to(e + 3)
            deviation(1)
            if last:
                return
            if kv:
                operand(0)
                kv_out(*kv, free=free)
                operand(1)
                scaled(0)
                scaled(1)
                split_to(e + 3)
            else:
                scaled(0)
                split_to(e + 3)
                operand(1)
                scaled(1)

        def even_mixer():
            copy_out("xr", ("ev", 4), first[("ev_in", 4)], tk[:, 0], (4, 5), free=("kv", 0, 0))
            copy_out("gate", ("ev", 3), first[("ev_in", 3)], tk[:, 1], (0, 1), ACT.Gelu_apprx_tanh)
            copy_out("q", ("ev", 0), first[("ev_in", 0)], tk[:, 0], (2, 3), free="xr")
            for g in range(2):
                for t2 in range(2):
                    act.wait_ge(*pe_core.at("gates", g, t2))
                    for j in range(2):
                        tile = 2 * t2 + j
                        ins = act.activation(lru_gate[g][:, tile, :], banks[TR[t2]][:, j * SEQ:(j + 1) * SEQ],
                                             ACT.Sigmoid, bias=pv[:, tile, 5 + g:6 + g]
                                             ).then_inc(*act_core.up("gates", g, t2))
            act.wait_ge(*act_core.now())
            act.wait_ge(*dve_core.at("softplus"))
            for tile in range(4):
                act.activation(lru_a[:, tile, :], lru_gate[0][:, tile, :], ACT.Exp, scale=sm[:, 4 + tile:5 + tile]
                               ).then_inc(*act_core.up())
                act.activation(lru_b[:, tile, :], lru_gate[0][:, tile, :], ACT.Tanh, scale=sm[:, tile:tile + 1]
                               ).then_inc(*act_core.up("decay"))
            copy_out("k", ("ev", 1), first[("ev_in", 1)], tk[:, 1], (4, 5), free="gate")
            act.wait_ge(*dve_core.at("one_minus_a2"))
            act.activation(lru_gate[0], lru_gate[0], ACT.Sqrt).then_inc(*act_core.up("root"))
            copy_out("v", ("ev", 2), first[("ev_in", 2)], v_da, (0, 1))
            kv_out(0, 1, free="k")
            act.wait_ge(*dve_core.at("b_out"))
            act.activation(xT_hi[:, 4:8, :], gateT[:, :, :], ACT.Copy).then_inc(*act_hi.up("b_out"))

            def exps(h):
                act.wait_ge(*dve_core.at("max", h))
                for m in range(2):
                    for t in range(TT):
                        c = slice(0, P) if t == 0 else slice(P, 3 * P)
                        s = scores_sb(h, m)[:, c]
                        k = 4 + 2 * m + t
                        act.activation(s, s, ACT.Exp, bias=da_sm[:, h, k:k + 1], scale=DA_D ** -0.5,
                                       accum_out=da_sm[:, h, k + 4:k + 5]).then_inc(*act_core.up("exp", h, m))

            def turned(h):
                act.wait_ge(*pe_turn.at("weights", h))
                act.activation(wT(h), banks[TR[h % 2]][:, 0:384], ACT.Copy).then_inc(*act_core.up("wT", h))

            split_to(first[("ev_out", 0)])
            exps(0)
            exps(1)
            turned(0)
            turned(1)
            kv_out(0, 2)
            exps(2)
            exps(3)
            turned(2)
            turned(3)
            squares = conv
            act.wait_ge(*pe_core.at("o", DA_H - 1))
            for h in range(DA_H):
                for t in range(TT):
                    act.activation(squares[:, h, t * P:(t + 1) * P], banks[4 + t][:, h * P:(h + 1) * P], ACT.Square,
                                   accum_out=sm[:, 36 + 4 * t + h:37 + 4 * t + h]).then_inc(*act_core.up())
            act.wait_ge(*act_core.now())
            act.activation(sm[:, 44:52], sm[:, 36:44], ACT.Sqrt, scale=1.0 / (2 * DA_D), bias=eps_col
                           ).then_inc(*act_core.up("rms"))
            split_to(first[("ev_out", 0)] + 2)
            for t in range(TT):
                split_operand("a_out", t, 0)

        def cross(l):
            for c in range(2):
                name = ("xq", l, c)
                copy_out(name, name, first[(("xq", l), c)], tk[:, c], GU if c == 0 else XQ_RIGHT)

            def exps(h):
                act.wait_ge(*dve_core.at("xmax", l, h))
                for t in range(TT):
                    k = 52 + 2 * (h % 2) + t
                    act.activation(p_x[:, h % 2, t, :], banks[h % 4][:, t * SEQ:(t + 1) * SEQ], ACT.Exp,
                                   bias=sm[:, k:k + 1], scale=XA_D ** -0.5, accum_out=sm[:, k + 4:k + 5]
                                   ).then_inc(*act_core.up("xp", l, h))

            def out_hi(h):
                act.wait_ge(*pe_core.at("xo", l, h))
                act.activation(xT_hi[:, 2 * h:2 * h + 2, :],
                               banks[GU[h % 2]][:, :].rearrange("p (k c) -> p k c", k=2), ACT.Copy
                               ).then_inc(*act_hi.up("xo", l, h))

            exps(0)
            exps(1)
            for h in range(XA_H):
                act.wait_ge(*pe_turn.at("xw", l, h))
                act.activation(pT_x[:, h % 2, :, :], banks[TR[h % 2]][:, :].rearrange("p (k c) -> p k c", k=2),
                               ACT.Copy).then_inc(*act_core.up("xpT", l, h))
                if h + 2 < XA_H:
                    exps(h + 2)
                else:
                    split_to(first[(("xo", l), 0)] + h)
                out_hi(h)

        def odd_mixer():
            copy_out("u", ("od", 0), first[("od_in", 0)], tk[:, 0], (4, 5))
            copy_out("qk", ("od", 1), first[("od_in", 1)], tk[:, 1], (0, 1))
            kv_out(1, 3, (4, 5))
            for c, name, dst, fn in ((2, "rv", ret_v, ACT.Copy), (3, "rg", ret_gate, ACT.Silu)):
                u = first[("od_in", c)]
                for t in range(TT):
                    split_to(u + 2 + t)
                    act.wait_ge(*end_of((("od", c), u), t))
                    act.activation(dst[:, t, :], banks[t][:, :], fn).then_inc(*act_out.up(name, t))
            split_to(first[("od_out", 0)] + 1)
            act.wait_ge(*dve_core.at("s5_out", 3))
            for a in range(2):
                act.activation(s5_y[a], s5_y[a], ACT.Gelu_apprx_tanh).then_inc(*act_core.up("gelu"))
            act.wait_ge(*act_core.now())
            for a in range(2):
                act.activation(xT_hi[:, 2 * a:2 * a + 2, :], s5_y[a], ACT.Copy).then_inc(*act_hi.up("z"))
            act.wait_ge(*dve_core.at("ret_var"))
            act.activation(sm[:, 78:86], s5_h[:, 0, 0, 64:80].rearrange("p (a b) -> p a b", b=2)[:, :, 1], ACT.Sqrt,
                           bias=eps_col).then_inc(*act_core.up("ret_sd"))
            act.wait_ge(unit_done, first["glu"] + 1)
            for o in range(4):
                act.activation(s5_t[:, o // 2, o % 2, :], banks[GLU[o // 2]][:, (o % 2) * SEQ:(o % 2 + 1) * SEQ],
                               ACT.Sigmoid, bias=pv[:, o, 9:10]).then_inc(*act_core.up("glu", o))
            for t in range(TT):
                split_operand("d_out", t, 1)
            split_to(first[("od_out", 0)] + 2)
            act.wait_ge(*dve_core.at("c_out"))
            for a in range(2):
                act.activation(xT_hi[:, 2 * a:2 * a + 2, :], s5_y[a], ACT.Copy).then_inc(*act_hi.up("c_out"))

        eps_col = sm[:, 92:93]

        def memory_tokens():
            for t in range(TT):
                for half in range(2):
                    split_operand("mem", t, half, memT_hi)
            for t in range(TT):
                act.activation(ax[:, t, :], x[:, t, :], ACT.Copy, scale=ALPHA).then_inc(*act_ln.up("ax", -1, t))

        def lru_parameters():
            act.wait_ge(*dve_core.at("neg_abs"))
            act.activation(sm[:, 8:12], sm[:, 12:16], ACT.Exp).then_inc(*act_core.up("exp_lambda"))
            act.wait_ge(*dve_core.at("lambda_sum"))
            act.activation(sm[:, 32:34], sm[:, 34:36], ACT.Exp).then_inc(*act_core.up("da_exp"))

        def s5_parameters():
            s = s5_par
            act.wait_ge(*dve_core.at("s5_args"))
            act.activation(s(3), s(3), ACT.Exp).then_inc(*act_core.up("s5_step"))

        def s5_sines():
            s = s5_par
            act.wait_ge(*dve_core.at("s5_angle"))
            act.activation(s(4), s(4), ACT.Exp).then_inc(*act_core.up())
            act.activation(s(5), s(6), ACT.Sin).then_inc(*act_core.up())
            act.activation(s(7), s(6), ACT.Sin, scale=0.5).then_inc(*act_core.up("s5_sin"))

        act.dma_start(x[:, 1, :], A["x"][0, P:SEQ, :]).then_inc(loaded["x1"], 16)
        for t in range(TT):
            for half in range(2):
                split_operand("x_in", t, half)
            split_to(1)
        ffn(0, memory_tokens, [(2, lru_parameters)])
        norm(0)
        even_mixer()
        norm(1)
        cross(0)
        norm(2, free=("xq", 0, 0))
        ffn(1, None, [(1, s5_parameters), (4, s5_sines)])
        norm(3, free=("kv", 1, 0))
        ffn(2)
        norm(4)
        odd_mixer()
        norm(5)
        cross(1)
        norm(6)
        ffn(3)
        norm(7, last=True)

    @block.vector
    def _(v):
        split = [0]
        V = nc.vector

        def split_to(u):
            while split[0] <= u:
                w = split[0]
                if w < n_units:
                    v.wait_ge(hi_done, w + 1)
                    s = w % NSLOT
                    V.tensor_tensor(w_lo[:, s, :], raw[:, s, :], w_hi[:, s, :].bitcast(F32), ALU.subtract
                                    ).then_inc(lo_done, 1)
                split[0] += 1

        def ffn(f, interlude=None, within=None):
            u, n = first[("ffn", f)], 2 * NB * f

            def lo(c, i):
                s = (u + 2 + c) % NSLOT
                v.wait_ge(hi_done, i * 3 + (u + 3 + c))
                V.tensor_tensor(w_lo[:, s, :], raw[:, s, :], w_hi[:, s, :].bitcast(F32), ALU.subtract
                                ).then_inc(lo_done, 1)

            def hidden(t, ready, turned):
                v.wait_ge(silu_done, ready + t)
                if turned is not None:
                    v.wait_ge(h_turned, turned + t)
                V.tensor_tensor(hid[:, t, :], act_h[:, t, :], banks[GU[t]][:, FB:2 * FB], ALU.mult
                                ).then_inc(h_done, 1)

            def hidden_lo(t, ready, hi, dst):
                v.wait_ge(h_hi, ready + t)
                V.tensor_tensor(dst[:, 0:2, t * P:(t + 1) * P],
                                banks[TR[t]][:, 0:2 * P].rearrange("p (k c) -> p k c", k=2),
                                hi[:, 0:2, t * P:(t + 1) * P].bitcast(F32), ALU.subtract).then_inc(h_lo, 1)

            split_to(u + 2)
            for t in range(TT):
                hidden(t, n + 1, n - 1 if f else None)
            if interlude:
                interlude()
            for a, b, work in loops(within):
                with v.Fori(a, b) as i:
                    for t in range(TT):
                        hidden_lo(t, i * 2 + (n + 1), hT_hi, hT_lo)
                    lo(1, i)
                    lo(2, i)
                    for t in range(TT):
                        hidden(t, i * 2 + (n + 3), i * 2 + (n + 1))
                    lo(3, i)
                if work:
                    work()
            b = NB - 1
            for t in range(TT):
                hidden_lo(t, n + 2 * b - 1, hT_hi, hT_lo)
            split[0] = u + 3 * b
            split_to(u + 3 * b + 2)
            for t in range(TT):
                hidden(t, n + 2 * b + 1, n + 2 * b - 1)
            hidden_lo(0, n + 2 * b + 1, xT_hi, xT_lo)
            hidden_lo(1, n + 2 * b + 1, xT_hi, xT_lo)

        def split_operand(name, t, half, hi=None, lo=None):
            hi = xT_hi if hi is None else hi
            lo = xT_lo if lo is None else lo
            v.wait_ge(*act_hi.at(name, t, half))
            at = (slice(None), slice(4 * half, 4 * half + 4), slice(t * P, (t + 1) * P))
            src = banks[split_bank(name, t, half)][:, :].rearrange("p (k c) -> p k c", k=4)
            V.tensor_tensor(lo[at], src, hi[at].bitcast(F32), ALU.subtract).then_inc(*dve_lo.up(name, t, half))

        def feature_out(name, dst):
            for t in range(TT):
                v.wait_ge(*pe_turn.at(name, t))
                V.tensor_copy(dst(t), banks[TR[t]][:, :].rearrange("p (k c) -> p k c", k=4)
                              ).then_inc(*dve_out.up(name, t))

        def kv_turned(l, c):
            if c < 2:
                feature_out(("kv", l, c), lambda t: k_mem[:, 4 * c:4 * c + 4, t * P:(t + 1) * P])

        def norm(i, scale, key, last=False):
            e = norm_units[i]

            def total(t, c):
                s = slice(c * 512, (c + 1) * 512)
                V.scalar_tensor_tensor(out=x[:, t, s], in0=banks[ACC[t] + c][:, :], scalar=scale,
                                       in1=ax[:, t, s], op0=ALU.mult, op1=ALU.add
                                       ).then_inc(*dve_ln.up("sum", i, t, c))

            def stats(t, c):
                v.wait_ge(*dve_ln.at("sum", i, t, c))
                V.bn_stats(bn[:, t, 6 * c:6 * c + 6], x[:, t, c * 512:(c + 1) * 512]).then_inc(*dve_ln.up())

            def moments(t):
                v.wait_ge(*dve_ln.now())
                V.bn_aggr(mv[:, t, 0:2], bn[:, t, :]).then_inc(*dve_ln.up("var", i, t))

            def centre(t):
                v.wait_ge(*dve_ln.at("var", i, t))
                V.scalar_tensor_tensor(out=x[:, t, :], in0=x[:, t, :], scalar=mv[:, t, 0:1], in1=gb[:, 0, :],
                                       op0=ALU.subtract, op1=ALU.mult).then_inc(*dve_ln.up("centred", i, t))

            def finish(t):
                v.wait_ge(*act_ln.at("sd", i, t))
                v.wait_ge(*dve_ln.at("centred", i, t))
                V.reciprocal(mv[:, t, 3:4], mv[:, t, 2:3]).then_inc(*dve_ln.up())
                v.wait_ge(*dve_ln.now())
                V.scalar_tensor_tensor(out=x[:, t, :], in0=x[:, t, :], scalar=mv[:, t, 3:4], in1=gb[:, 1, :],
                                       op0=ALU.mult, op1=ALU.add).then_inc(*dve_ln.up("x", i, t))

            def operand(t):
                for half in range(2):
                    split_operand(("x", i), t, half)

            v.wait_ge(loaded["gb"], 32 * (i + 1))
            kv = kv_of_norm.get(i)
            split_to(e + 1)
            if i in after_ffn:
                for t in range(TT):
                    v.wait_ge(*act_ln.at("ax", i - 1, t))
                    for c in range(2):
                        v.wait_ge(*((unit_done, e + 1) if (t, c) == (1, 1) else pe_half.at(*key, t, c)))
                        total(t, c)
                        stats(t, c)
                    moments(t)
                    split_to(e + 2 + t)
                    if t == 1 and not last:
                        operand(0)
                    centre(t)
                    if t == 1:
                        split_to(e + 4)
                    finish(t)
                if last:
                    return
            else:
                for t in range(TT):
                    v.wait_ge(*act_ln.at("ax", i - 1, t))
                    for c in range(2):
                        v.wait_ge(*(pe_half.at(key, c) if t == 0 else (unit_done, e + c)))
                        total(t, c)
                        if t == 1 and c == 1 and not kv:
                            operand(0)
                            split[0] = e + 3
                        stats(t, c)
                    moments(t)
                    if kv:
                        split_to(e + 2 + t)
                        if t == 1:
                            operand(0)
                    centre(t)
                    if kv and t == 1:
                        split_to(e + 4)
                    finish(t)
            if kv:
                operand(1)
                kv_turned(*kv)
            else:
                v.wait_ge(lo_done, e + 3)
                split_to(e + 3)
                operand(1)

        def done():
            v.wait_ge(*dve_core.now())

        def rotate(name, t, data, halfw, cos, sin, ta, tb):
            lo, hi = slice(0, halfw), slice(halfw, 2 * halfw)
            V.tensor_tensor(ta, data, cos, ALU.mult).then_inc(*dve_core.up())
            V.tensor_tensor(tb[..., lo], data[..., hi], sin[..., lo], ALU.mult).then_inc(*dve_core.up())
            V.tensor_tensor(tb[..., hi], data[..., lo], sin[..., hi], ALU.mult).then_inc(*dve_core.up())
            v.wait_ge(*dve_core.now())
            V.tensor_tensor(data, ta, tb, ALU.add).then_inc(*dve_core.up(name, t))

        def even_mixer():
            split_to(first[("ev_in", 3)] + 3)
            V.memset(xrT[:, :, 0:3], 0.0).then_inc(*dve_core.up())
            feature_out("xr", lambda t: xrT[:, :, 3 + t * P:3 + (t + 1) * P])
            v.wait_ge(*dve_out.now())
            v.wait_ge(*dve_core.now())
            for k in range(4):
                for tile in range(4):
                    src = xrT[:, tile, k:k + SEQ]
                    if k == 0:
                        V.tensor_scalar(conv[:, tile, :], src, pv[:, tile, 0:1], pv[:, tile, 4:5], ALU.mult, ALU.add
                                        ).then_inc(*dve_core.up())
                    else:
                        v.wait_ge(dve_core.sem, dve_core.n - 3)
                        V.scalar_tensor_tensor(out=conv[:, tile, :], in0=src, scalar=pv[:, tile, k:k + 1],
                                               in1=conv[:, tile, :], op0=ALU.mult, op1=ALU.add
                                               ).then_inc(*dve_core.up("conv"))
            split_to(first[("ev_in", 0)] + 3)
            feature_out("gate", lambda t: gateT[:, :, t * P:(t + 1) * P])
            ta, tb = rot_tmp[:, 0, :], rot_tmp[:, 1, :]

            def rotate_da(name, buf):
                for t in range(TT):
                    v.wait_ge(*act_out.at(name, t))
                    d3 = tk[:, buf, t, :].rearrange("p (g d) -> p g d", d=DA_D)[:, :, 0:DA_ROPE]
                    cs, sn = (k_(n).rearrange("p (t g d) -> p t g d", t=TT, d=DA_ROPE)[:, t]
                              for n in ("da_cos", "da_sin"))
                    done()
                    rotate(name, t, d3, DA_ROPE // 2, cs, sn, ta.rearrange("p (g d) -> p g d", d=DA_ROPE),
                           tb.rearrange("p (g d) -> p g d", d=DA_ROPE))

            rotate_da("q", 0)
            split_to(first[("ev_in", 1)] + 3)
            v.wait_ge(*act_core.at("decay"))
            g0, g1 = lru_gate
            V.tensor_tensor(g0, lru_a[:, :, :], lru_a[:, :, :], ALU.mult).then_inc(*dve_core.up())
            v.wait_ge(*act_core.at("gates", 1, 1))
            V.tensor_tensor(g1, g1, conv[:, :, :], ALU.mult).then_inc(*dve_core.up())
            done()
            V.scalar_tensor_tensor(out=g0, in0=g0, scalar=1.0, in1=lru_b[:, :, :], op0=ALU.add, op1=ALU.mult
                                   ).then_inc(*dve_core.up("one_minus_a2"))
            rotate_da("k", 1)
            feature_out("q", lambda t: qT_da[:, :, t * P:(t + 1) * P])
            split_to(first[("ev_in", 2)] + 3)
            v.wait_ge(*act_core.at("root"))
            V.tensor_tensor(lru_b[:, :, :], g0, g1, ALU.mult).then_inc(*dve_core.up())
            done()
            for tile in range(4):
                V.tensor_tensor_scan(conv[:, tile, :], lru_a[:, tile, :], lru_b[:, tile, :], 0.0, ALU.mult, ALU.add
                                     ).then_inc(*dve_core.up())
            feature_out("k", lambda t: kT_da[:, :, t * P:(t + 1) * P])
            done()
            v.wait_ge(*dve_out.now())
            V.tensor_tensor(gateT[:, :, :], gateT[:, :, :], conv[:, :, :], ALU.mult
                            ).then_inc(*dve_core.up("b_out"))
            split_to(first[(("kv", 0), 1)] + 3)
            v.wait_ge(*act_hi.at("b_out"))
            V.tensor_tensor(xT_lo[:, 4:8, :], gateT[:, :, :], xT_hi[:, 4:8, :].bitcast(F32), ALU.subtract
                            ).then_inc(*dve_lo.up("b_out"))

            def masked(h):
                for m in range(2):
                    v.wait_ge(*pe_core.at("scores", h, m))
                    V.tensor_tensor(scores_sb(h, m), banks[2 * (h % 2) + m][:, 0:384], k_("mask"), ALU.add
                                    ).then_inc(*dve_core.up("masked", h, m))
                for m in range(2):
                    v.wait_ge(*dve_core.at("masked", h, m))
                    for t, c in ((0, slice(0, P)), (1, slice(P, 3 * P))):
                        V.reduce_max(da_sm[:, h, 2 * m + t:2 * m + t + 1], scores_sb(h, m)[:, c], AX_X
                                     ).then_inc(*dve_core.up())
                done()
                V.tensor_scalar(da_sm[:, h, 4:8], da_sm[:, h, 0:4], -(DA_D ** -0.5), None, ALU.mult
                                ).then_inc(*dve_core.up("max", h))

            def combine(h):
                r = da_sm[:, h, 8:12]
                v.wait_ge(*act_core.at("exp", h, 1))
                if h >= 2:
                    v.wait_ge(*pe_turn.at("weights", h - 2))
                V.reciprocal(r, r).then_inc(*dve_core.up())
                done()
                V.tensor_scalar(r[:, 2:4], r[:, 2:4], sm[:, 93:94], None, ALU.mult).then_inc(*dve_core.up())
                done()
                for t, c in ((0, slice(0, P)), (1, slice(P, 3 * P))):
                    s1 = scores_sb(h, 1)[:, c]
                    V.tensor_scalar(s1, s1, r[:, 2 + t:3 + t], None, ALU.mult).then_inc(*dve_core.up("map1", h, t))
                for t, c in ((0, slice(0, P)), (1, slice(P, 3 * P))):
                    v.wait_ge(*dve_core.at("map1", h, t))
                    V.scalar_tensor_tensor(out=xrT_w(h)[:, c], in0=scores_sb(h, 0)[:, c], scalar=r[:, t:t + 1],
                                           in1=scores_sb(h, 1)[:, c], op0=ALU.mult, op1=ALU.add
                                           ).then_inc(*dve_core.up("weights", h))

            masked(0)
            masked(1)
            combine(0)
            combine(1)
            split_to(first[("ev_out", 0)])
            masked(2)
            masked(3)
            kv_turned(0, 1)
            combine(2)
            combine(3)
            split_to(first[("ev_out", 0)] + 1)
            r = sm[:, 44:52]
            v.wait_ge(*act_core.at("rms"))
            V.reciprocal(r, r).then_inc(*dve_core.up())
            done()
            V.tensor_scalar(r, r, 1.0 - LAMBDA_INIT, None, ALU.mult).then_inc(*dve_core.up())
            done()
            for t in range(TT):
                for h in range(DA_H):
                    V.scalar_tensor_tensor(out=kT_da_flat(t)[:, h * P:(h + 1) * P],
                                           in0=banks[4 + t][:, h * P:(h + 1) * P],
                                           scalar=r[:, 4 * t + h:4 * t + h + 1], in1=da_g[:, :],
                                           op0=ALU.mult, op1=ALU.mult).then_inc(*dve_core.up("a_out", t))
            split_to(first[("ev_out", 0)] + 2)
            for t in range(TT):
                split_operand("a_out", t, 0)

        def cross(l):
            def queries(c):
                feature_out(("xq", l, c), lambda t: q_x[:, 4 * c:4 * c + 4, t * P:(t + 1) * P])

            def maxima(h):
                v.wait_ge(*pe_core.at("xs", l, h))
                V.tensor_reduce(sm[:, 86:88], banks[h % 4][:, :].rearrange("p (t k) -> p t k", t=TT), AX_X, ALU.max
                                ).then_inc(*dve_core.up())
                done()
                k = 52 + 2 * (h % 2)
                V.tensor_scalar(sm[:, k:k + 2], sm[:, 86:88], -(XA_D ** -0.5), None, ALU.mult
                                ).then_inc(*dve_core.up("xmax", l, h))
                done()

            def normalise(h):
                k = 56 + 2 * (h % 2)
                v.wait_ge(*act_core.at("xp", l, h))
                V.reciprocal(sm[:, k:k + 2], sm[:, k:k + 2]).then_inc(*dve_core.up())
                done()
                for t in range(TT):
                    V.tensor_scalar(p_x[:, h % 2, t, :], p_x[:, h % 2, t, :], sm[:, k + t:k + t + 1], None, ALU.mult
                                    ).then_inc(*dve_core.up("xw", l, h))

            def out_lo(h):
                v.wait_ge(*act_hi.at("xo", l, h))
                V.tensor_tensor(xT_lo[:, 2 * h:2 * h + 2, :],
                                banks[GU[h % 2]][:, :].rearrange("p (k c) -> p k c", k=2),
                                xT_hi[:, 2 * h:2 * h + 2, :].bitcast(F32), ALU.subtract
                                ).then_inc(*dve_lo.up("xo", l, h))

            split_to(first[(("xq", l), 1)] + 1)
            queries(0)
            split_to(first[(("xo", l), 0)])
            maxima(0)
            maxima(1)
            queries(1)
            normalise(0)
            split_to(first[(("xo", l), 0)] + 1)
            for h in range(XA_H):
                if h + 2 < XA_H:
                    maxima(h + 2)
                if h + 1 < XA_H:
                    normalise(h + 1)
                if h >= 2:
                    split_to(first[(("xo", l), 0)] + h)
                out_lo(h)

        def s5_parameters():
            s = s5_par
            V.tensor_scalar(s(0), s(0), -1e-4, None, ALU.min).then_inc(*dve_core.up("s5_args"))

        def s5_angles():
            s = s5_par
            v.wait_ge(*act_core.at("s5_step"))
            done()
            V.tensor_tensor(s(4), s(0), s(3), ALU.mult).then_inc(*dve_core.up())
            V.tensor_tensor(s(6), s(1), s(3), ALU.mult).then_inc(*dve_core.up())
            done()
            V.tensor_scalar(s(8), s(6), 1.0 / (2 * math.pi), 12582912.0, ALU.mult, ALU.add).then_inc(*dve_core.up())
            done()
            V.tensor_scalar(s(8), s(8), 12582912.0, None, ALU.subtract).then_inc(*dve_core.up())
            done()
            for part in (6.28125, 0.0019350051879882812, 3.0199159819500178e-07):
                V.scalar_tensor_tensor(out=s(6), in0=s(8), scalar=-part, in1=s(6), op0=ALU.mult, op1=ALU.add
                                       ).then_inc(*dve_core.up())
                done()
            V.tensor_scalar(s(6), s(6), 3.1415925, -3.1415925, ALU.min, ALU.max).then_inc(*dve_core.up("s5_angle"))

        def s5_factors():
            s = s5_par
            v.wait_ge(*act_core.at("s5_sin"))
            done()
            V.tensor_tensor(s(7), s(7), s(7), ALU.mult).then_inc(*dve_core.up())
            done()
            cos, sin, mag = s(8), s(5), s(4)
            V.tensor_scalar(cos, s(7), -2.0, 1.0, ALU.mult, ALU.add).then_inc(*dve_core.up())
            done()
            nr, ni, lr, li = s(6), s(3), s(0), s(1)
            V.tensor_tensor(nr, mag, cos, ALU.mult).then_inc(*dve_core.up())
            V.tensor_tensor(ni, mag, sin, ALU.mult).then_inc(*dve_core.up())
            done()
            V.tensor_scalar(nr, nr, 1.0, None, ALU.subtract).then_inc(*dve_core.up())
            V.tensor_tensor(s(7), lr, lr, ALU.mult).then_inc(*dve_core.up())
            V.tensor_tensor(s(9), li, li, ALU.mult).then_inc(*dve_core.up())
            done()
            V.tensor_tensor(s(7), s(7), s(9), ALU.add).then_inc(*dve_core.up())
            done()
            V.reciprocal(s(7), s(7)).then_inc(*dve_core.up())
            V.tensor_tensor(s(9), nr, lr, ALU.mult).then_inc(*dve_core.up())
            V.tensor_tensor(s(10), ni, li, ALU.mult).then_inc(*dve_core.up())
            done()
            V.tensor_tensor(s(9), s(9), s(10), ALU.add).then_inc(*dve_core.up())
            done()
            V.tensor_tensor(s(9), s(9), s(7), ALU.mult).then_inc(*dve_core.up())
            V.tensor_tensor(s(10), ni, lr, ALU.mult).then_inc(*dve_core.up())
            V.tensor_tensor(s(11), nr, li, ALU.mult).then_inc(*dve_core.up())
            done()
            V.tensor_tensor(s(10), s(10), s(11), ALU.subtract).then_inc(*dve_core.up())
            done()
            V.tensor_tensor(s(10), s(10), s(7), ALU.mult).then_inc(*dve_core.up())
            done()

        def s5_operands():
            s = s5_par
            v.wait_ge(loaded["s5"], 64)
            b = [qkT[:, ri, 0, :].rearrange("p (j c) -> p j c", c=16) for ri in range(2)]
            fr, fi = (s(n).unsqueeze(2).to_broadcast([P, 16, 16]) for n in (9, 10))
            flat = s5_blocks[0]
            bd = [flat[:, ri * 512:(ri + 1) * 512].rearrange("p (j c) -> p j c", c=32) for ri in range(2)]
            t1, t2 = (s5_cT[:, 0, 2 * a:2 * a + 2, :].rearrange("p a b -> p (a b)").rearrange(
                "p (j c) -> p j c", c=16) for a in range(2))
            V.memset(flat, 0.0).then_inc(*dve_core.up())
            for ri in range(2):
                V.tensor_tensor(t1, b[ri], fr, ALU.mult).then_inc(*dve_core.up())
                V.tensor_tensor(t2, b[1 - ri], fi, ALU.mult).then_inc(*dve_core.up())
                done()
                for g in range(2):
                    r = slice(64 * g, 64 * g + 64)
                    V.tensor_tensor(bd[ri][r, :, 16 * g:16 * g + 16], t1[r], t2[r],
                                    ALU.subtract if ri == 0 else ALU.add).then_inc(*dve_core.up("s5_b", ri))
                done()

        def s5_output_operands():
            c_flat = s5_blocks[1]
            for ri in range(2):
                c = qkT[:, ri, 1, :].rearrange("p (q n) -> p q n", n=64)
                cd = c_flat[:, ri * 512:(ri + 1) * 512].rearrange("p (q n) -> p q n", n=P)
                for g in range(2):
                    V.tensor_scalar(cd[:, :, 64 * g:64 * g + 64], c, k_("parity")[:, g:g + 1],
                                    1.0 if ri == 0 else -1.0, ALU.mult, ALU.mult
                                    ).then_inc(*dve_core.up("s5_c", ri))

        def s5_prepare():
            s = s5_par
            for n, (kind, dst) in enumerate((("s5_b", s5_bT), ("s5_c", s5_cT))):
                for ri in range(2):
                    v.wait_ge(*pe_turn.at(kind, ri))
                    V.tensor_copy(dst[:, ri].rearrange("p a b -> p (a b)"), banks[XT[n][ri]][:, :]
                                  ).then_inc(*dve_core.up(kind + "T", ri))
            V.tensor_copy(e_cos[:, :, 0], s(8)).then_inc(*dve_core.up())
            V.tensor_copy(e_sin[:, :, 0], s(5)).then_inc(*dve_core.up("theta"))

        def odd_mixer():
            split_to(first[("od_in", 0)] + 3)
            rt = [w[:, :, :].rearrange("p a b -> p (a b)") for w in (act_h, hid)]

            def rotate_qk(t):
                v.wait_ge(*act_out.at("qk", t))
                done()
                data, ta, tb = (w.rearrange("p (a h d) -> p a h d", a=2, d=RET_D)
                                for w in (tk[:, 1, t, :], rt[0], rt[1]))
                cs, sn = (k_(n).rearrange("p (t h d) -> p t h d", t=TT, d=RET_D)[:, t] for n in ("ret_cos", "ret_sin"))
                lo, hi = slice(0, RET_D // 2), slice(RET_D // 2, RET_D)
                for a in range(2):
                    V.tensor_tensor(ta[:, a], data[:, a], cs, ALU.mult).then_inc(*dve_core.up())
                    V.tensor_tensor(tb[:, a, :, lo], data[:, a, :, hi], sn[:, :, lo], ALU.mult
                                    ).then_inc(*dve_core.up())
                    V.tensor_tensor(tb[:, a, :, hi], data[:, a, :, lo], sn[:, :, hi], ALU.mult
                                    ).then_inc(*dve_core.up())
                done()
                V.tensor_tensor(tk[:, 1, t, :], rt[0], rt[1], ALU.add).then_inc(*dve_core.up("qk", t))

            kv = first[(("kv", 1), 3)]
            split_to(kv + 1)
            rotate_qk(0)
            v.wait_ge(*pool_core.at("powers"))
            feature_out("u", lambda t: uT[:, :, t * P:(t + 1) * P])
            rotate_qk(1)
            split_to(kv + 3)
            feature_out("qk", lambda t: qkT[:, :, :, t * P:(t + 1) * P].rearrange("p a b c -> p (a b) c"))
            v.wait_ge(unit_done, kv + 2)
            V.tensor_scalar(osb[:, 0, :], s5_cT[:, 0].rearrange("p a b -> p (a b)"), -1.0, None, ALU.mult
                            ).then_inc(*dve_core.up("s5_neg_c"))
            xp = [tk[:, 0, b, :].rearrange("p (r k) -> p r k", r=2) for b in range(2)]
            xc, xs = (tk[:, 1, b, :].rearrange("p (r k) -> p r k", r=2) for b in range(2))

            def products(j):
                src = banks[S5_IN[j % 4]][:, :].rearrange("p (r c k) -> p r c k", r=2, k=S5_CH)
                v.wait_ge(*pe_core.at("s5_x", j))
                for e, out in ((e_cos, xc), (e_sin, xs)):
                    V.tensor_tensor(out.rearrange("p r (c k) -> p r c k", k=S5_CH), src,
                                    e[:, j, :].unsqueeze(1).unsqueeze(1).to_broadcast([P, 2, 2, S5_CH]), ALU.mult
                                    ).then_inc(*dve_core.up("s5_in", j))

            def rotate_in(j):
                v.wait_ge(*dve_core.at("s5_in", j))
                V.tensor_tensor(xp[j % 2][:, 0], xc[:, 0], xs[:, 1], ALU.add).then_inc(*dve_core.up())
                V.tensor_tensor(xp[j % 2][:, 1], xc[:, 1], xs[:, 0], ALU.subtract).then_inc(*dve_core.up("s5_xp", j))

            split_at = {5: 2, 8: 3}
            products(0)
            rotate_in(0)
            for j in range(S5_TILES):
                if j in split_at:
                    split_to(first[("od_in", 2)] + split_at[j])
                g = s5_g[:, j % 2]
                decay = s5_par(4)[:, j:j + 1].to_broadcast([P, S5_CH])
                if j >= 2:
                    v.wait_ge(*pool_core.at("s5_h", j - 2))
                v.wait_ge(*dve_core.at("s5_xp", j))
                for r in range(2):
                    V.tensor_tensor_scan(g[:, r, 0:S5_CH], decay, xp[j % 2][:, r, 0:S5_CH], 0.0, ALU.mult, ALU.add
                                         ).then_inc(*dve_core.up("s5_first", j))
                if j + 1 < S5_TILES:
                    products(j + 1)
                last = slice(S5_CH - 1, S5_CH)
                ec, es = e_cos[:, j, last], e_sin[:, j, last]
                v.wait_ge(*dve_core.at("s5_first", j))
                V.tensor_tensor(sm[:, 86:87], g[:, 1, last], es, ALU.mult).then_inc(*dve_core.up())
                V.tensor_tensor(sm[:, 87:88], g[:, 1, last], ec, ALU.mult).then_inc(*dve_core.up("s5_part", j))
                if j + 1 < S5_TILES:
                    rotate_in(j + 1)
                v.wait_ge(*dve_core.at("s5_part", j))
                V.scalar_tensor_tensor(out=sm[:, 88:89], in0=g[:, 0, last], scalar=ec, in1=sm[:, 86:87],
                                       op0=ALU.mult, op1=ALU.subtract).then_inc(*dve_core.up())
                V.scalar_tensor_tensor(out=sm[:, 89:90], in0=g[:, 0, last], scalar=es, in1=sm[:, 87:88],
                                       op0=ALU.mult, op1=ALU.add).then_inc(*dve_core.up())
                done()
                for r in range(2):
                    V.tensor_tensor_scan(g[:, r, S5_CH:SEQ], decay, xp[j % 2][:, r, S5_CH:SEQ], sm[:, 88 + r:89 + r],
                                         ALU.mult, ALU.add).then_inc(*dve_core.up("s5_g", j))

            def ret_weights(h):
                v.wait_ge(*pe_core.at("ret_s", h))
                dec = k_("decay").rearrange("p (h k) -> p h k", h=RET_H)[:, h]
                b = banks[RET_S[h]]
                V.tensor_tensor(ret_w(h)[:, 0:SEQ], b[:, 0:SEQ], dec, ALU.mult).then_inc(*dve_core.up())
                V.tensor_tensor(ret_w(h)[:, SEQ:SEQ + P], b[:, SEQ:SEQ + P], dec[:, 0:P], ALU.mult
                                ).then_inc(*dve_core.up("ret_w", h))

            split_to(first[("od_out", 0)])
            done()
            for h in range(RET_H - 1):
                ret_weights(h)
            v.wait_ge(*pe_core.at("s5_y", S5_TILES - 1))
            for q in range(4):
                V.scalar_tensor_tensor(out=s5_y[q // 2][:, q % 2, :], in0=uT[:, q, :], scalar=pv[:, q, 8:9],
                                       in1=banks[4 + q // 2][:, (q % 2) * SEQ:(q % 2 + 1) * SEQ],
                                       op0=ALU.mult, op1=ALU.add).then_inc(*dve_core.up("s5_out", q))
            ret_weights(RET_H - 1)
            v.wait_ge(*act_out.at("rg", TT - 1))
            for t in range(TT):
                gate = ret_gate[:, t, :].rearrange("p (h d) -> p h d", h=RET_H)
                V.tensor_tensor(gate, gate, ret_g[:, :].unsqueeze(1).to_broadcast([P, RET_H, P]), ALU.mult
                                ).then_inc(*dve_core.up("ret_gate"))
            v.wait_ge(*act_hi.at("z"))
            for a in range(2):
                V.tensor_tensor(xT_lo[:, 2 * a:2 * a + 2, :], s5_y[a], xT_hi[:, 2 * a:2 * a + 2, :].bitcast(F32),
                                ALU.subtract).then_inc(*dve_lo.up("z"))
            stat = s5_h[:, 0, 0, 0:64].rearrange("p (a b) -> p a b", b=8)
            agg = s5_h[:, 0, 0, 64:80].rearrange("p (a b) -> p a b", b=2)
            v.wait_ge(*pe_core.at("ret_o", RET_H - 1))
            for t in range(TT):
                for h in range(RET_H):
                    V.bn_stats(stat[:, 4 * t + h, 0:6], banks[4 + t][:, h * P:(h + 1) * P]).then_inc(*dve_core.up())
            done()
            for n in range(8):
                V.bn_aggr(agg[:, n, :], stat[:, n, 0:6]).then_inc(*dve_core.up("ret_var"))
            v.wait_ge(*act_core.at("ret_sd"))
            V.reciprocal(sm[:, 78:86], sm[:, 78:86]).then_inc(*dve_core.up())
            done()
            for t in range(TT):
                for h in range(RET_H):
                    n = 4 * t + h
                    V.tensor_scalar(osb[:, t, h * P:(h + 1) * P], banks[4 + t][:, h * P:(h + 1) * P], agg[:, n, 0:1],
                                    sm[:, 78 + n:79 + n], ALU.subtract, ALU.mult).then_inc(*dve_core.up("ret_n", t))
                done()
                V.tensor_tensor(osb[:, t, :], osb[:, t, :], ret_gate[:, t, :], ALU.mult
                                ).then_inc(*dve_core.up("d_out", t))
            for t in range(TT):
                split_operand("d_out", t, 1)
            v.wait_ge(*act_core.at("glu", 3))
            for a in range(2):
                V.tensor_tensor(s5_y[a], s5_y[a], s5_t[:, a], ALU.mult).then_inc(*dve_core.up("c_out"))
            split_to(first[("od_out", 0)] + 1)
            v.wait_ge(*act_hi.at("c_out"))
            for a in range(2):
                V.tensor_tensor(xT_lo[:, 2 * a:2 * a + 2, :], s5_y[a], xT_hi[:, 2 * a:2 * a + 2, :].bitcast(F32),
                                ALU.subtract).then_inc(*dve_lo.up("c_out"))

        zero = rot_tmp[:, 0, :]
        V.memset(zero, 0.0).then_inc(*zeroed.up())
        v.wait_ge(*zeroed.now())
        V.tensor_copy(zero_r[:, :], zero).then_inc(*zeroed.up("zero"))
        V.memset(sm[:, 92:93], LN_EPS).then_inc(*dve_core.up())
        def parameter_rows():
            v.wait_ge(loaded["nat"], 16 * 9)
            for g in range(2):
                V.tensor_copy(nat[0:16, 768 + 64 * g:832 + 64 * g], sm[0:16, 90 + g:91 + g].to_broadcast([16, 64])
                              ).then_inc(*dve_core.up("log_step"))

        def memory_tokens():
            parameter_rows()
            v.wait_ge(*pe_turn.at("params"))
            V.tensor_copy(pv[:, :, :], banks[2][:, 0:64].rearrange("p (a b) -> p a b", b=16)[:, :, 0:10]
                          ).then_inc(*dve_core.up())
            for n, at in ((0, 64), (1, 80), (3, 96)):
                V.tensor_copy(s5_par(n), banks[2][:, at:at + 16]).then_inc(*dve_core.up("params"))
            for t in range(TT):
                for half in range(2):
                    split_operand("mem", t, half, memT_hi, memT_lo)

        def lru_parameters():
            lam = pv[:, :, 7]
            nl, na = sm[:, 60:64], sm[:, 12:16]
            done()
            V.tensor_scalar(nl, lam, -1.0, None, ALU.mult).then_inc(*dve_core.up())
            done()
            V.tensor_tensor(na, nl, lam, ALU.min).then_inc(*dve_core.up("neg_abs"))
            v.wait_ge(loaded["rows"], 48)
            dl = tk[:, 0, 0, 0:256].rearrange("p (a b d) -> p a b d", a=2, b=2)
            pr = tk[:, 0, 0, 256:384].rearrange("p (a d) -> p a d", a=2)
            V.tensor_tensor(pr, dl[:, :, 0, :], dl[:, :, 1, :], ALU.mult).then_inc(*dve_core.up())
            done()
            V.reduce_sum(sm[:, 34:36], pr, AX_X).then_inc(*dve_core.up("lambda_sum"))

        def lru_series():
            e4, z4, z2, pl = (sm[:, c:c + 4] for c in (8, 64, 68, 72))
            v.wait_ge(*act_core.at("exp_lambda"))
            V.tensor_scalar(z4, e4, 2.0, None, ALU.add).then_inc(*dve_core.up())
            done()
            V.reciprocal(z4, z4).then_inc(*dve_core.up())
            done()
            V.tensor_tensor(z4, z4, e4, ALU.mult).then_inc(*dve_core.up())
            done()
            V.tensor_tensor(z2, z4, z4, ALU.mult).then_inc(*dve_core.up())
            V.memset(pl, 1.0 / 17).then_inc(*dve_core.up())
            for n in (15, 13, 11, 9):
                done()
                V.tensor_tensor(pl, pl, z2, ALU.mult).then_inc(*dve_core.up())
                done()
                V.tensor_scalar(pl, pl, 1.0 / n, None, ALU.add).then_inc(*dve_core.up())

        def lru_softplus():
            nl, z4, z2, pl = (sm[:, c:c + 4] for c in (60, 64, 68, 72))
            for n in (7, 5, 3, 1):
                done()
                V.tensor_tensor(pl, pl, z2, ALU.mult).then_inc(*dve_core.up())
                done()
                V.tensor_scalar(pl, pl, 1.0 / n, None, ALU.add).then_inc(*dve_core.up())
            done()
            V.tensor_tensor(pl, pl, z4, ALU.mult).then_inc(*dve_core.up())
            V.tensor_scalar(nl, nl, 0.0, None, ALU.max).then_inc(*dve_core.up())
            done()
            V.scalar_tensor_tensor(out=nl, in0=pl, scalar=2.0, in1=nl, op0=ALU.mult, op1=ALU.add
                                   ).then_inc(*dve_core.up())
            done()
            V.tensor_scalar(sm[:, 0:4], nl, LRU_C, None, ALU.mult).then_inc(*dve_core.up())
            V.tensor_scalar(sm[:, 4:8], nl, -LRU_C, None, ALU.mult).then_inc(*dve_core.up("softplus"))
            v.wait_ge(*act_core.at("da_exp"))
            V.tensor_scalar(sm[:, 93:94], sm[:, 33:34], LAMBDA_INIT, sm[:, 32:33], ALU.subtract, ALU.subtract
                            ).then_inc(*dve_core.up())

        for t in range(TT):
            for half in range(2):
                split_operand("x_in", t, half)
            split_to(1)
        ffn(0, memory_tokens, [(2, lru_parameters), (4, lru_series), (6, lru_softplus)])
        norm(0, 0.5, ("acc", 0))
        v.wait_ge(loaded["tables"], 16)
        even_mixer()
        norm(1, 1.0, "ev_out")
        cross(0)
        norm(2, 1.0, ("xo", 0))
        ffn(1, None, [(1, s5_parameters), (3, s5_angles), (5, s5_factors), (6, s5_operands),
                      (8, s5_output_operands)])
        norm(3, 0.5, ("acc", 1))
        ffn(2, s5_prepare)
        norm(4, 0.5, ("acc", 2))
        odd_mixer()
        norm(5, 1.0, "od_out")
        cross(1)
        norm(6, 1.0, ("xo", 1))
        ffn(3)
        norm(7, 0.5, ("acc", 3), last=True)


INPUTS = ("x", "mem", "ln_g", "ln_b", "ffn_w_gate", "ffn_w_up", "ffn_w_down", "xa_w_q", "xa_w_kv", "xa_w_o",
          "ev_w_in", "ev_w_out", "da_lambda", "da_norm_g", "lru_conv_w", "lru_conv_b", "lru_gate_w", "lru_gate_b",
          "lru_lambda", "od_w_in", "od_w_out", "s5_lam_re", "s5_lam_im", "s5_log_step", "s5_b_re", "s5_b_im",
          "s5_c_re", "s5_c_im", "s5_d", "s5_glu_w", "s5_glu_b", "ret_norm_g")


def kernel(**inputs):
    import concourse.bacc as bacc
    from concourse.bass_utils import run_bass_kernel_spmd

    arrays = {f"in_{n}": np.ascontiguousarray(inputs[n]) for n in INPUTS}
    arrays["in_constants"] = constant_table()[1]

    def program(marks, final):
        nc = bacc.Bacc("TRN2", target_bir_lowering=False, num_devices=1)
        A = {n[3:]: nc.dram_tensor(n, a.shape, mybir.dt.from_np(a.dtype), kind="ExternalInput").ap()
             for n, a in arrays.items()}
        A["out"] = nc.dram_tensor("out", (1, SEQ, D), F32, kind="ExternalOutput").ap()
        build(nc, A, marks, final)
        return nc

    marks = {}
    program(marks, False)
    nc = program(marks, True)
    got = run_bass_kernel_spmd(nc, [arrays], core_ids=[0])
    return got.results[0]["out"]
```
